# Optimizing a Trainium2 kernel written in Bass

```python
import math
import jax
import jax.numpy as jnp
from jax import lax
import numpy as np

D_MODEL = 2048
BATCH = 1
SEQ = 128
DEPTH = 1
DEC_BATCH = 1
DEC_SEQ = 128
PAST_LEN = 128

GRID_W = 64
H_A = 8
DK_A = 128
DV_A = 128
CONV_K = 3
CHUNK = 64
H_B = 8
DQK_B = 64
DV_B = 2 * DQK_B
Q_BLOCK = 128
ROPE_BASE = 10000.0
N_GROUPS = 4
E_PER_GROUP = 8
N_EXPERTS = N_GROUPS * E_PER_GROUP
TOP_K = 2
D_FF_E = D_MODEL // 4
EPS = 1e-6
QKV_A = 2 * H_A * DK_A + H_A * DV_A
IN_SIZES = (QKV_A, H_A * DV_A, 2 * H_A, 2 * H_A, H_B * 2 * DQK_B, H_B * 2 * DQK_B, H_B * DV_B, 2 * D_MODEL)
N_IN = QKV_A + H_A * DV_A + 4 * H_A + 2 * H_B * 2 * DQK_B + H_B * DV_B + 2 * D_MODEL
F32 = jnp.float32

kernel_name = 'hybrid_deltanet_diffattn_hmoe_dit_step'

def _rmsnorm(x, g):
    xf = x.astype(F32)
    y = xf * lax.rsqrt(jnp.mean(xf * xf, axis=-1, keepdims=True) + EPS)
    return (y * g.astype(F32)).astype(x.dtype)

def _l2norm(x):
    xf = x.astype(F32)
    return (xf * lax.rsqrt(jnp.sum(xf * xf, axis=-1, keepdims=True) + EPS)).astype(x.dtype)

def _adaln(cvec, w_ada, b_ada):
    m = jax.nn.silu(cvec) @ w_ada + b_ada
    return jnp.split(m[:, None, :], 6, axis=-1)

def _modulate(h, shift, scale):
    return h * (1 + scale) + shift

def _split_cols(z):
    idx, acc = [], 0
    for s in IN_SIZES[:-1]:
        acc += s
        idx.append(acc)
    return jnp.split(z, idx, axis=-1)

def _dwconv(x, w):
    pad = CONV_K // 2
    return lax.conv_general_dilated(x, w[:, None, :], window_strides=(1,), padding=[(pad, pad)],
                                    dimension_numbers=('NWC', 'WIO', 'NWC'), feature_group_count=x.shape[-1])

def _axial_rope(x):
    t = x.shape[1]
    rows = t // GRID_W
    row = jnp.broadcast_to(jnp.arange(rows)[:, None], (rows, GRID_W)).reshape(t)
    col = jnp.broadcast_to(jnp.arange(GRID_W)[None, :], (rows, GRID_W)).reshape(t)
    half = DQK_B // 2
    nf = half // 2
    inv_freq = ROPE_BASE ** (-jnp.arange(nf, dtype=F32) / nf)

    def rot(xh, pos):
        ang = pos.astype(F32)[:, None] * inv_freq
        cos = jnp.cos(ang)[None, :, None, None, :]
        sin = jnp.sin(ang)[None, :, None, None, :]
        x1, x2 = xh[..., :nf], xh[..., nf:]
        return jnp.concatenate([x1 * cos - x2 * sin, x2 * cos + x1 * sin], axis=-1)

    xf = x.astype(F32)
    return jnp.concatenate([rot(xf[..., :half], row), rot(xf[..., half:], col)], axis=-1).astype(x.dtype)

def _diff_attention(q, k, v, lam):
    b, tq, h, _, d = q.shape
    kf, vf = k.astype(F32), v.astype(F32)
    qb = jnp.moveaxis(q.reshape(b, tq // Q_BLOCK, Q_BLOCK, h, 2, d), 1, 0)

    def block(qblk):
        s = jnp.einsum('bqhmd,bkhmd->bhmqk', qblk.astype(F32), kf) * (d ** -0.5)
        p = jax.nn.softmax(s, axis=-1)
        a = p[:, :, 0] - lam * p[:, :, 1]
        return jnp.einsum('bhqk,bkhe->bqhe', a, vf)

    o = lax.map(block, qb)
    return jnp.moveaxis(o, 0, 1).reshape(b, tq, h, v.shape[-1]).astype(v.dtype)

def _gated_delta_chunked(q, k, v, g, beta, s0):
    out_dtype = v.dtype
    q, k, v = q.astype(F32), k.astype(F32), v.astype(F32)
    lead = q.shape[:-2]
    t = q.shape[-2]
    n = t // CHUNK
    dv = v.shape[-1]
    ch = lambda a: a.reshape(lead + (n, CHUNK) + a.shape[len(lead) + 1:])
    qc = ch(q) * (DK_A ** -0.5)
    kc, vc = ch(k), ch(v)
    gc = jnp.cumsum(ch(g.astype(F32)), axis=-1)
    bc = ch(beta.astype(F32))
    causal = jnp.tril(jnp.ones((CHUNK, CHUNK), dtype=bool))
    decay = jnp.where(causal, jnp.exp(jnp.where(causal, gc[..., :, None] - gc[..., None, :], 0.0)), 0.0)
    kb = kc * bc[..., None]
    a_low = jnp.tril(jnp.einsum('...id,...jd->...ij', kb, kc) * decay, -1)
    eye = jnp.eye(CHUNK, dtype=F32)
    rhs = jnp.concatenate([vc * bc[..., None], kb * jnp.exp(gc)[..., None]], axis=-1)
    sol = lax.linalg.triangular_solve(a_low + eye, rhs, left_side=True, lower=True, unit_diagonal=True)
    u, w = sol[..., :dv], sol[..., dv:]
    a_qk = jnp.einsum('...id,...jd->...ij', qc, kc) * decay
    mv = lambda a, ax: jnp.moveaxis(a, ax, 0)
    xs = (mv(qc * jnp.exp(gc)[..., None], -3), mv(kc * jnp.exp(gc[..., -1:] - gc)[..., None], -3),
          mv(u, -3), mv(w, -3), mv(gc[..., -1], -1), mv(a_qk, -3))

    def step(s, inp):
        q_i, kd_i, u_i, w_i, glast_i, aqk_i = inp
        v_new = u_i - jnp.einsum('...cd,...de->...ce', w_i, s)
        o_i = jnp.einsum('...cd,...de->...ce', q_i, s) + jnp.einsum('...ij,...je->...ie', aqk_i, v_new)
        s = s * jnp.exp(glast_i)[..., None, None] + jnp.einsum('...cd,...ce->...de', kd_i, v_new)
        return s, o_i

    s_fin, o = lax.scan(step, s0.astype(F32), xs)
    o = jnp.moveaxis(o, 0, -3).reshape(lead + (t, dv))
    return o.astype(out_dtype), s_fin

def _mixer(h, lp, lam_init, ctx):
    b, t, _ = h.shape
    qkv_a, gate_a, beta_l, alpha_l, q_b, k_b, v_b, g_merge = _split_cols(h @ lp['w_in'])
    qkv_a = jax.nn.silu(_dwconv(qkv_a, lp['conv_a']))
    q_a, k_a, v_a = jnp.split(qkv_a, [H_A * DK_A, 2 * H_A * DK_A], axis=-1)
    q_a = _l2norm(q_a.reshape(b, t, H_A, DK_A)).transpose(0, 2, 1, 3)
    k_a = _l2norm(k_a.reshape(b, t, H_A, DK_A)).transpose(0, 2, 1, 3)
    v_a = v_a.reshape(b, t, H_A, DV_A).transpose(0, 2, 1, 3)
    per_dir = lambda a: a.astype(F32).reshape(b, t, 2, H_A).transpose(2, 0, 3, 1)
    beta = jax.nn.sigmoid(per_dir(beta_l))
    g = -jnp.exp(lp['a_log'].astype(F32))[:, None, :, None] * jax.nn.softplus(
        per_dir(alpha_l) + lp['dt_bias'].astype(F32)[:, None, :, None])
    both = lambda a: jnp.stack([a, jnp.flip(a, axis=2)])
    rev = lambda a: jnp.stack([a[0], jnp.flip(a[1], axis=-1)])
    if ctx is None:
        s0 = jnp.zeros((2, b, H_A, DK_A, DV_A), F32)
    else:
        s0 = jnp.swapaxes(ctx[0], 0, 1)
    o2, s_fin = _gated_delta_chunked(both(q_a), both(k_a), both(v_a), rev(g), rev(beta), s0)
    o_a = (o2[0] + jnp.flip(o2[1], axis=2)).transpose(0, 2, 1, 3)
    o_a = _rmsnorm(o_a, lp['onorm_a']) * jax.nn.silu(gate_a.reshape(b, t, H_A, DV_A))
    q_b = q_b.reshape(b, t, H_B, 2, DQK_B)
    k_b = k_b.reshape(b, t, H_B, 2, DQK_B)
    v_b = v_b.reshape(b, t, H_B, DV_B)
    if ctx is None:
        keys, vals = k_b, v_b
    else:
        q_b = _axial_rope(q_b)
        n_ctx = ctx[1].shape[2]
        k_ctx = ctx[1].reshape(b, H_B, n_ctx, 2, DQK_B).transpose(0, 2, 1, 3, 4).astype(k_b.dtype)
        keys = jnp.concatenate([k_ctx, _axial_rope(k_b)], axis=1)
        vals = jnp.concatenate([ctx[2].transpose(0, 2, 1, 3).astype(v_b.dtype), v_b], axis=1)
    lv = lp['lam'].astype(F32)
    lam = jnp.exp(jnp.sum(lv[0] * lv[1])) - jnp.exp(jnp.sum(lv[2] * lv[3])) + lam_init
    o_b = _rmsnorm(_diff_attention(q_b, keys, vals, lam), lp['subln_b']) * (1.0 - lam_init)
    g_a, g_b = jnp.split(jax.nn.sigmoid(g_merge), 2, axis=-1)
    mixed = g_a * (o_a.reshape(b, t, -1) @ lp['w_up_a']) + g_b * (o_b.reshape(b, t, -1) @ lp['w_up_b'])
    out = mixed @ lp['w_o']
    if ctx is None:
        return out, (jnp.swapaxes(s_fin, 0, 1),
                     k_b.reshape(b, t, H_B, 2 * DQK_B).transpose(0, 2, 1, 3),
                     v_b.transpose(0, 2, 1, 3))
    return out, None

def _hier_moe(x, w_rg, b_rg, w_re, b_re, w_g, w_u, w_d):
    b, t, d = x.shape
    h = x.reshape(b * t, d)
    p_grp = jax.nn.softmax((h @ w_rg).astype(F32) + b_rg.astype(F32), axis=-1)
    pg_top, g_idx = lax.top_k(p_grp, 1)
    le = ((h @ w_re).astype(F32) + b_re.astype(F32)).reshape(-1, N_GROUPS, E_PER_GROUP)
    le_sel = jnp.einsum('nge,ng->ne', le, jax.nn.one_hot(g_idx[:, 0], N_GROUPS, dtype=F32))
    p_exp = jax.nn.softmax(le_sel, axis=-1)
    pe_top, e_idx = lax.top_k(p_exp, TOP_K)
    w_tok = pg_top * pe_top / jnp.sum(pe_top, axis=-1, keepdims=True)
    combine = jnp.einsum('nk,nke->ne', w_tok,
                         jax.nn.one_hot(g_idx * E_PER_GROUP + e_idx, N_EXPERTS, dtype=F32)).astype(h.dtype)
    y = jnp.zeros_like(h)
    for gi in range(N_GROUPS):
        e0, e1 = gi * E_PER_GROUP, (gi + 1) * E_PER_GROUP
        act = jax.nn.silu(jnp.einsum('nd,edf->enf', h, w_g[e0:e1])) * jnp.einsum('nd,edf->enf', h, w_u[e0:e1])
        y = y + jnp.einsum('enf,efd->nd', act * combine[:, e0:e1].T[:, :, None], w_d[e0:e1])
    return y.reshape(b, t, d)

def setup_inputs(seed: int = 0) -> dict:
    key = jax.random.key(seed)
    ks = jax.random.split(key, 32)
    nrm = lambda k, shape, s: jax.random.normal(k, shape, F32) * s
    gain = lambda k, shape: 1.0 + 0.02 * jax.random.normal(k, shape, F32)
    dt = jnp.exp(jax.random.uniform(ks[14], (DEPTH, 2, H_A), F32, math.log(1e-3), math.log(1e-1)))
    return {
        'x_prompt': nrm(ks[0], (BATCH, SEQ, D_MODEL), 1.0),
        'x_sample': nrm(ks[1], (DEC_BATCH, DEC_SEQ, D_MODEL), 1.0),
        'c': nrm(ks[2], (DEC_BATCH, D_MODEL), 1.0),
        'state_delta': nrm(ks[3], (DEC_BATCH, DEPTH, 2, H_A, DK_A, DV_A), 0.1),
        'cache_k': nrm(ks[4], (DEC_BATCH, DEPTH, H_B, PAST_LEN, 2 * DQK_B), 1.0),
        'cache_v': nrm(ks[5], (DEC_BATCH, DEPTH, H_B, PAST_LEN, DV_B), 1.0),
        'c_ctx': nrm(ks[6], (D_MODEL,), 1.0),
        'w_ada': nrm(ks[7], (DEPTH, D_MODEL, 6 * D_MODEL), 0.5 * D_MODEL ** -0.5),
        'b_ada': nrm(ks[8], (DEPTH, 6 * D_MODEL), 0.02),
        'norm_mix': gain(ks[9], (DEPTH, D_MODEL)),
        'norm_ffn': gain(ks[10], (DEPTH, D_MODEL)),
        'w_in': nrm(ks[11], (DEPTH, D_MODEL, N_IN), D_MODEL ** -0.5),
        'conv_a': nrm(ks[12], (DEPTH, CONV_K, QKV_A), CONV_K ** -0.5),
        'a_log': jnp.log(jax.random.uniform(ks[13], (DEPTH, 2, H_A), F32, 1.0, 16.0)),
        'dt_bias': dt + jnp.log(-jnp.expm1(-dt)),
        'onorm_a': gain(ks[15], (DEPTH, DV_A)),
        'lam': nrm(ks[16], (DEPTH, 4, DQK_B), 0.1),
        'subln_b': gain(ks[17], (DEPTH, DV_B)),
        'w_up_a': nrm(ks[18], (DEPTH, H_A * DV_A, D_MODEL), (H_A * DV_A) ** -0.5),
        'w_up_b': nrm(ks[19], (DEPTH, H_B * DV_B, D_MODEL), (H_B * DV_B) ** -0.5),
        'w_o': nrm(ks[20], (DEPTH, D_MODEL, D_MODEL), D_MODEL ** -0.5),
        'w_rg': nrm(ks[21], (DEPTH, D_MODEL, N_GROUPS), D_MODEL ** -0.5),
        'b_rg': nrm(ks[22], (DEPTH, N_GROUPS), 0.01),
        'w_re': nrm(ks[23], (DEPTH, D_MODEL, N_EXPERTS), D_MODEL ** -0.5),
        'b_re': nrm(ks[24], (DEPTH, N_EXPERTS), 0.01),
        'w_e_gate': nrm(ks[25], (DEPTH, N_EXPERTS, D_MODEL, D_FF_E), D_MODEL ** -0.5),
        'w_e_up': nrm(ks[26], (DEPTH, N_EXPERTS, D_MODEL, D_FF_E), D_MODEL ** -0.5),
        'w_e_down': nrm(ks[27], (DEPTH, N_EXPERTS, D_FF_E, D_MODEL), D_FF_E ** -0.5),
        'norm_final': gain(ks[28], (D_MODEL,)),
    }

def reference(x_prompt, x_sample, c, state_delta, cache_k, cache_v, c_ctx,
              w_ada, b_ada, norm_mix, norm_ffn, w_in, conv_a, a_log, dt_bias, onorm_a,
              lam, subln_b, w_up_a, w_up_b, w_o, w_rg, b_rg, w_re, b_re,
              w_e_gate, w_e_up, w_e_down, norm_final):
    xp, xs = x_prompt, x_sample
    st_new, k_new, v_new = [], [], []
    for l in range(DEPTH):
        lam_init = 0.8 - 0.6 * math.exp(-0.3 * l)
        lp = {'w_in': w_in[l], 'conv_a': conv_a[l], 'a_log': a_log[l], 'dt_bias': dt_bias[l],
              'onorm_a': onorm_a[l], 'lam': lam[l], 'subln_b': subln_b[l],
              'w_up_a': w_up_a[l], 'w_up_b': w_up_b[l], 'w_o': w_o[l]}
        mp = (w_rg[l], b_rg[l], w_re[l], b_re[l], w_e_gate[l], w_e_up[l], w_e_down[l])
        sh1, sc1, gt1, sh2, sc2, gt2 = _adaln(c_ctx[None, :], w_ada[l], b_ada[l])
        mix, (s_ctx, k_ctx, v_ctx) = _mixer(_modulate(_rmsnorm(xp, norm_mix[l]), sh1, sc1), lp, lam_init, None)
        xp = xp + gt1 * mix
        xp = xp + gt2 * _hier_moe(_modulate(_rmsnorm(xp, norm_ffn[l]), sh2, sc2), *mp)
        st_new.append(s_ctx)
        k_new.append(k_ctx)
        v_new.append(v_ctx)
        sh1, sc1, gt1, sh2, sc2, gt2 = _adaln(c, w_ada[l], b_ada[l])
        mix, _ = _mixer(_modulate(_rmsnorm(xs, norm_mix[l]), sh1, sc1), lp, lam_init,
                        (state_delta[:, l], cache_k[:, l], cache_v[:, l]))
        xs = xs + gt1 * mix
        xs = xs + gt2 * _hier_moe(_modulate(_rmsnorm(xs, norm_ffn[l]), sh2, sc2), *mp)
    y_prompt = _rmsnorm(xp, norm_final)
    y_sample = _rmsnorm(xs, norm_final)
    new_state_delta = jnp.stack(st_new, axis=1)
    new_cache_k = jnp.stack(k_new, axis=1)
    new_cache_v = jnp.stack(v_new, axis=1)
    return (y_prompt, y_sample, new_state_delta, new_cache_k, new_cache_v)


_drawn_inputs = setup_inputs


def setup_inputs(seed=0):
    import zlib

    import numpy as np

    out = dict(_drawn_inputs(seed))
    spreads = {}
    factors = {'norm_ffn': 3.375,
     'onorm_a': 8.0,
     'lam': 4.293,
     'subln_b': 8.0,
     'b_rg': 8.0,
     'b_re': 7.02,
     'norm_final': 2.728}
    for name, (base, spread) in spreads.items():
        noise = np.random.default_rng([zlib.crc32(name.encode()), seed]).standard_normal(out[name].shape)
        drawn = base * np.exp(spread * noise) if base else spread * noise
        out[name] = jnp.asarray(drawn.astype(out[name].dtype))
    for name, factor in factors.items():
        out[name] = (out[name] * factor).astype(out[name].dtype)
    return out
```

```python
from contextlib import ExitStack

import numpy as np
import concourse.bass as bass
from concourse import mybir

F32 = mybir.dt.float32
I32 = mybir.dt.int32
ALU = mybir.AluOpType
ACT = mybir.ActivationFunctionType
AX = mybir.AxisListType.X

P = 128
NP = 2
D = 2048
KT = D // P
H = 8
HD = H * P
GW = 64
NG, EG = 4, 8
NE = NG * EG
FF = 512
EPS = 1e-6
LAM_INIT = 0.2
SLOTS = 8
SW = 2048
CAP = 64
PAIRS = NE // 2
MAX_SLABS = NP * P // CAP
LEVELS = 7
QKV_A = 3 * HD

R_ADA, R_IN = 0, 12
R_GM = R_IN + 7
R_UPA, R_UPB, R_O, R_MOE = R_IN + 11, R_IN + 12, R_IN + 13, R_IN + 15

C_ID, C_ONE, C_U, C_SU, C_IOTA, C_SEL, C_COS, C_SIN, C_TIE, C_THR, C_SEL2 = (
    0, 128, 256, 512, 640, 704, 960, 1024, 1088, 1096, 1099)
C_N = 1104
A_CONV, A_GATE, A_QB, A_OBT, A_OAT, A_TMP, A_N = 0, 6144, 8192, 14336, 16384, 18432, 24324


def constants():
    i = np.arange(P)
    c = np.zeros((P, C_N), np.float32)
    c[:, C_ID:C_ID + P] = np.eye(P)
    c[:, C_ONE:C_ONE + P] = 1.0
    c[:, C_U:C_U + P] = i[:, None] <= i[None]
    c[:, C_U + P:C_U + 2 * P] = i[:, None] >= i[None]
    c[:, C_SU:C_SU + P] = i[:, None] < i[None]
    c[:, C_IOTA:C_IOTA + CAP] = np.arange(CAP)
    for p in range(NP):
        c[p::32, C_SEL + p * P:C_SEL + (p + 1) * P] = 1.0
        c[p::32, C_SEL2 + p] = 1.0
    nf = 16
    inv = (10000.0 ** (-np.arange(nf, dtype=np.float32) / nf)).astype(np.float32)
    for half, pos in enumerate((i // GW, i % GW)):
        ang = pos.astype(np.float32)[:, None] * inv
        for x in range(2):
            at = half * 32 + x * 16
            c[:, C_COS + at:C_COS + at + nf] = np.cos(ang)
            c[:, C_SIN + at:C_SIN + at + nf] = np.sin(ang) * (-1 if x == 0 else 1)
    c[:, C_TIE:C_TIE + 8] = 8 - np.arange(8)
    c[:, C_THR:C_THR + 3] = CAP * np.arange(1, 4)
    lv = np.zeros((P, LEVELS, 2, P), np.float32)
    for n in range(LEVELS):
        s = 1 << n
        same = (i[:, None] // (2 * s)) == (i[None] // (2 * s))
        lo, hi = (i // s) % 2 == 0, (i // s) % 2 == 1
        lv[:, n, 0] = same & lo[:, None] & hi[None]
        lv[:, n, 1] = same & hi[:, None] & lo[None]
    return c, lv.reshape(P, -1)


def program(nc, x_prompt, x_sample, c, state_delta, cache_k, cache_v, c_ctx, w_ada, b_ada, norm_mix, norm_ffn,
            w_in, conv_a, a_log, dt_bias, onorm_a, lam, subln_b, w_up_a, w_up_b, w_o, w_rg, b_rg, w_re, b_re,
            w_e_gate, w_e_up, w_e_down, norm_final, consts, level_masks,
            y_prompt, y_sample, new_state, new_k, new_v):
    ctx = ExitStack()
    with ctx:
        sb = lambda name, *shape, dt=F32: ctx.enter_context(nc.sbuf_tensor(name, [P, *shape], dt))
        sem = lambda name: ctx.enter_context(nc.semaphore(name))

        ring = sb("ring", SLOTS, SW)
        hT = sb("hT", KT, NP * P)
        gate_rows = sb("gate_rows", 2, D)
        cst = sb("cst", C_N)
        arena = sb("arena", A_N)
        silu_cT = sb("silu_cT", KT, 32)
        cT = sb("cT", NP, KT)
        vecT = sb("vecT", P)
        cw = sb("cw", 3, 24)
        mod = sb("mod", 6, KT, NP)
        modA = sb("modA", 2, KT, NP)
        w_ba = sb("w_ba", KT, 32)
        w_rt = sb("w_rt", KT, NG + NE)
        alog = sb("alog", 16)
        dtb = sb("dtb", 16)
        lamv = sb("lamv", 4, 64)
        onorm = sb("onorm", P)
        subln = sb("subln", P)
        b_rt = sb("b_rt", NG + NE)
        eps = sb("eps", 1)
        ba = sb("ba", NP, 32)
        sc = sb("sc", 2, 48)
        beta = sb("beta", NP, 16)
        g = sb("g", NP, 16)
        gc = sb("gc", 48)
        egc = sb("egc", 32)
        egl = sb("egl", 16)
        lam_t = sb("lam_t", 8)
        ms = sb("ms", 16)
        rs = sb("rs", 16)
        mx = sb("mx", 16)
        den = sb("den", 16)
        ps = ctx.enter_context(nc.psum_tensor("ps", [P, 8, 512], F32))

        ident = cst[:, C_ID:C_ID + P]
        ones = cst[:, C_ONE:C_ONE + P]
        U = [cst[:, C_U + d * P:C_U + (d + 1) * P] for d in range(2)]
        strict = cst[:, C_SU:C_SU + P]
        sel_row = [cst[:, C_SEL + p * P:C_SEL + (p + 1) * P] for p in range(NP)]
        sel2 = cst[:, C_SEL2:C_SEL2 + 2]

        def ar(at, n):
            return arena[:, at:at + n]

        def heads(ap):
            return ap.rearrange("p (h d) -> p h d", d=P)

        def per_head(ap, n=P):
            return ap.unsqueeze(2).to_broadcast([P, ap.shape[1], n])

        def over_heads(ap, m=H):
            return ap.unsqueeze(1).to_broadcast([P, m, ap.shape[1]])

        def banks(a, n):
            return ps[:, a:a + n, :].rearrange("p b n -> p (b n)")

        vec_rows = ar(4096, P)
        conv_rows = ar(4096 + P, P)
        xin = ar(A_TMP, 4096).rearrange("p (a d) -> p a d", a=NP)
        ada_rows = ar(0, 4096).rearrange("p (a d) -> p a d", a=2)
        convT = ar(A_CONV, 6144).rearrange("p (m t) -> p m t", t=NP * P)
        gateS = ar(A_GATE, 2048).rearrange("p (a n) -> p a n", a=NP)
        qkvb = ar(A_QB, 6144).rearrange("p (s a n) -> p s a n", s=3, a=NP)
        obT = ar(A_OBT, 2048).rearrange("p (h t) -> p h t", t=NP * P)
        oaT = ar(A_OAT, 2048).rearrange("p (h t) -> p h t", t=NP * P)

        slot_full = [sem(f"slot_full{j}") for j in range(SLOTS)]
        slot_used = [sem(f"slot_used{j}") for j in range(SLOTS)]
        round_done = slot_used[SLOTS - 1]
        boot_in = sem("boot_in")
        small_in = sem("small_in")
        vec_turned = sem("vec_turned")
        vec_saved = sem("vec_saved")
        silu_ready = sem("silu_ready")
        ada_saved = sem("ada_saved")
        mod_turned = sem("mod_turned")
        mod_saved = sem("mod_saved")
        ssq_ready = sem("ssq_ready")
        ms_ready = sem("ms_ready")
        root_ready = sem("root_ready")
        xn_ready = sem("xn_ready")
        xn_turned = sem("xn_turned")
        hT_saved = sem("hT_saved")
        ba_done = sem("ba_done")
        ba_saved = sem("ba_saved")
        conv_mid = sem("conv_mid")
        in_saved = sem("in_saved")
        conv_done = sem("conv_done")
        dve_step = sem("dve_step")
        act_step = sem("act_step")
        kv_out = sem("kv_out")
        bag_exp = sem("bag_exp")
        bag_dve = sem("bag_dve")
        bag_ready = sem("bag_ready")
        at_in = sem("at_in")
        rope_done = sem("rope_done")
        at_turned = sem("at_turned")
        at_saved = sem("at_saved")
        at_scores = sem("at_scores")
        at_cent = sem("at_cent")
        at_exp = sem("at_exp")
        at_prob = sem("at_prob")
        at_pT = sem("at_pT")
        at_pT_saved = sem("at_pT_saved")
        at_o = sem("at_o")
        at_o_saved = sem("at_o_saved")
        at_on = sem("at_on")
        at_oT = sem("at_oT")
        at_oT_saved = sem("at_oT_saved")
        l2_sq = sem("l2_sq")
        l2_sum = sem("l2_sum")
        l2_root = sem("l2_root")
        l2_done = sem("l2_done")
        gc_done = sem("gc_done")
        gc_saved = sem("gc_saved")
        gc_exp = sem("gc_exp")
        lv_in = sem("lv_in")
        tok_turned = sem("tok_turned")
        tok_saved = sem("tok_saved")
        s0_in = sem("s0_in")
        dl_rhs = sem("dl_rhs")
        dl_gram = sem("dl_gram")
        dl_diff = sem("dl_diff")
        dl_dec = sem("dl_dec")
        dl_A = sem("dl_A")
        dl_M = sem("dl_M")
        dl_X = sem("dl_X")
        dl_Xs = sem("dl_Xs")
        dl_Y = sem("dl_Y")
        dl_T = sem("dl_T")
        dl_S0 = sem("dl_S0")
        dl_S0r = sem("dl_S0r")
        dl_R = sem("dl_R")
        dl_V = sem("dl_V")
        dl_Vs = sem("dl_Vs")
        dl_O = sem("dl_O")
        dl_Os = sem("dl_Os")
        dl_Vd = sem("dl_Vd")
        dl_S = sem("dl_S")
        dl_Ss = sem("dl_Ss")
        st_out = sem("st_out")
        dl_on = sem("dl_on")
        dl_oT = sem("dl_oT")
        dl_oTs = sem("dl_oTs")
        gm_saved = sem("gm_saved")
        up_done = sem("up_done")
        up_saved = sem("up_saved")
        mix_T = sem("mix_T")
        mix_Ts = sem("mix_Ts")
        gt_in = sem("gt_in")
        gt_done = sem("gt_done")
        gt_saved = sem("gt_saved")
        x_saved = sem("x_saved")
        x_in = sem("x_in")
        h2_T = sem("h2_T")
        h2_saved = sem("h2_saved")
        rt_done = sem("rt_done")
        rt_exp = sem("rt_exp")
        rt_dve = sem("rt_dve")
        rt_mask = sem("rt_mask")
        rt_pos = sem("rt_pos")
        rt_ready = sem("rt_ready")
        places = sem("places")
        mo_oh = sem("mo_oh")
        mo_P = sem("mo_P")
        mo_gath = sem("mo_gath")
        mo_gaths = sem("mo_gaths")
        mo_PT = sem("mo_PT")
        mo_PTs = sem("mo_PTs")
        mo_silu = sem("mo_silu")
        mo_act = sem("mo_act")
        mo_aT = sem("mo_aT")
        mo_aTs = sem("mo_aTs")
        mo_dns = sem("mo_dns")
        mo_y = sem("mo_y")
        mo_ys = sem("mo_ys")
        nf_in = sem("nf_in")
        y_ready = sem("y_ready")
        y_out = sem("y_out")

        cent = ar(A_OAT, 4096)
        qT = heads(ar(A_OAT + 4096, 1024))
        kT = heads(ar(A_OAT + 5120, 1024))
        pT = ar(A_OAT + 4096, 2048).rearrange("p (k h q) -> p k h q", k=2, h=H)
        cv = ar(A_OAT + 6144, 1024)
        ck = ar(A_OAT + 2048, 1024)
        kcT = heads(ar(A_QB, 1024))
        rope_a = ar(A_OAT, 1024)
        rope_b = ar(A_OAT + 1024, 1024)
        o_b = ar(A_OAT + 3072, 1024)
        o_sq = ar(A_OAT + 2048, 1024)
        l2_buf = ar(A_QB, 4096)
        E_, Aqk, At, X_, T_, Tt = (heads(ar(A_QB + n * 1024, 1024)) for n in range(6))
        M_, V_, O_, K_ = (heads(ar(A_TMP + n * 1024, 1024)) for n in range(4))
        lvl = ar(A_TMP + 4096, LEVELS * 256).rearrange("p (n d i) -> p n d i", n=LEVELS, d=2)
        gm = ar(0, 8192).rearrange("p (s a n) -> p s a n", s=4, a=NP)
        mixed = ar(8192, 4096).rearrange("p (a n) -> p a n", a=NP)
        gt_b = ar(A_TMP, 4096).rearrange("p (a n) -> p a n", a=NP)
        gm_tmp = ar(12288, 2048)
        xres = ar(0, 4096).rearrange("p (a n) -> p a n", a=NP)
        xn2 = ar(4096, 4096).rearrange("p (a n) -> p a n", a=NP)
        h2 = xn2
        yacc = ar(8192, 4096).rearrange("p (a n) -> p a n", a=NP)
        yacc_b = ar(8192, 4096).rearrange("p (b n) -> p b n", b=8)
        hg = ar(12288, 2048).rearrange("p (k s) -> p k s", k=KT)
        oe = ar(14336, 2048)
        a_silu = ar(16384, 512)
        a_act = ar(16896, 512)
        aT = ar(17408, 512).rearrange("p (k s) -> p k s", k=4)
        onehot = ar(17920, 256).rearrange("p (a s) -> p a s", a=NP)
        onehot_c = ar(18176, 256).rearrange("p (a s) -> p a s", a=NP)
        ohT = ar(18432, 256).rearrange("p (a t) -> p a t", a=NP)
        gt2_b = ar(18688, 4096).rearrange("p (a n) -> p a n", a=NP)
        rt = ar(22784, 1400)
        nf_b = ar(12288, 2048)
        rt_at = [0]

        def router(*shape):
            n = int(np.prod(shape))
            rt_at[0] += n
            t = rt[:, rt_at[0] - n:rt_at[0]]
            return t.rearrange("p (a b) -> p a b", a=shape[0]) if len(shape) > 1 else t

        r_log = router(NP, NG + NE)
        r_gmax, r_tm, r_pg, r_m1, r_m2, r_e2, r_w1, r_w2 = (router(NP) for _ in range(8))
        r_t4, r_goh, r_ge = (router(NP, NG) for _ in range(3))
        r_les, r_les2, r_t8, r_oh1, r_oh2, r_c8, r_s8 = (router(NP, EG) for _ in range(7))
        r_big = router(NP, NE)
        r_mask = router(NP, NE)
        r_comb = router(NP, NE + 2)
        r_pos = router(NP, NE + 2)
        r_cnt = router(1)
        r_gt = router(3)
        n_slab = sb("n_slab", 1, dt=I32)

        x_dram = [x_prompt[0], x_sample[0]]
        ada_dram = w_ada[0].rearrange("(p k) n -> p k n", k=KT)
        in_dram = w_in[0].rearrange("(k p) n -> p k n", p=P)
        wo_dram = w_o[0].rearrange("(k p) n -> p k n", p=P)
        IN_COLS = [0, 1024, 2048, 3072, 4128, 5152, 6176, 7200, 8224, 9248, 10272]

        block = ctx.enter_context(nc.Block())

        @block.sync
        def _(sp):
            def load(j, r, dst, src):
                if r > 0:
                    sp.wait_ge(slot_used[j], r)
                sp.dma_start(dst, src).then_inc(slot_full[j], 16)

            for s in range(6):
                for h in range(2):
                    for j in range(SLOTS):
                        load(j, 2 * s + h, ring[:, j, :], ada_dram[:, 8 * h + j, s * D:(s + 1) * D])
            for n, col in enumerate(IN_COLS):
                for j in range(SLOTS):
                    load(j, R_IN + n, ring[:, j, :].rearrange("p (k n) -> p k n", k=2),
                         in_dram[:, 2 * j:2 * j + 2, col:col + 1024])
            for r, w in ((R_UPA, w_up_a), (R_UPB, w_up_b)):
                for j in range(SLOTS):
                    load(j, r, ring[:, j, :], w[0, j * P:(j + 1) * P, :])
            for h in range(2):
                for j in range(SLOTS):
                    load(j, R_O + h, ring[:, j, :], wo_dram[:, 8 * h + j, :])
            sp.wait_ge(rt_ready, 1)
            n_slabs = sp.value_load(n_slab[0:1, 0:1], min_val=1, max_val=MAX_SLABS)
            seen = sp.alloc_register("sp_seen")
            sp.reg_mov(seen, R_MOE)
            with sp.Fori(0, n_slabs):
                with sp.Fori(0, PAIRS) as i:
                    for part in range(3):
                        r = sp.snap(seen)
                        for j in range(SLOTS):
                            sp.wait_ge(slot_used[j], r)
                            if part < 2:
                                w = (w_e_gate, w_e_up)[part]
                                kq, e = j // 2, j % 2
                                src = w[0, bass.ds(i * 2 + e, 1), 512 * kq:512 * kq + 512, :].rearrange(
                                    "a (k p) n -> (a p) k n", p=P)
                                dst = ring[:, j, :].rearrange("p (k n) -> p k n", k=4)
                            else:
                                fk, e = j // 2, j % 2
                                src = w_e_down[0, bass.ds(i * 2 + e, 1), P * fk:P * fk + P, :].rearrange(
                                    "a p n -> (a p) n")
                                dst = ring[:, j, :]
                            sp.dma_start(dst, src).then_inc(slot_full[j], 16)
                        sp.reg_add(seen, seen, 1)
            sp.wait_ge(y_ready, 1)
            sp.dma_start(y_prompt[0], yacc[:, 0, :]).then_inc(y_out, 16)
            sp.wait_ge(y_ready, 2)
            sp.dma_start(y_sample[0], yacc[:, 1, :]).then_inc(y_out, 16)
            sp.wait_ge(y_out, 32)

        @block.tensor
        def _(pe):
            def full(j, r):
                pe.wait_ge(slot_full[j], 16 * (r + 1))

            def turn_norm(n):
                src = (xin, xn2)[n]
                for b in range(8):
                    for kk in range(2):
                        for p in range(NP):
                            last = pe.transpose(ps[:, b, (2 * kk + p) * P:(2 * kk + p + 1) * P],
                                                src[:, p, (2 * b + kk) * P:(2 * b + kk + 1) * P], ident)
                    last.then_inc(xn_turned, 1)

            pe.wait_ge(boot_in, 16 * 9)
            pe.transpose(ps[:, 7, 0:P], vec_rows, ident)
            pe.transpose(ps[:, 7, P:P + 72], conv_rows[0:72, :], ident[0:72, 0:72]).then_inc(vec_turned, 1)

            def turn_mod(s, n):
                pe.wait_ge(ada_saved, s + 1)
                for k in range(KT):
                    last = pe.matmul(ps[:, 4 * (s % 2), 2 * k:2 * k + 2], ada_rows[:, s % 2, k * P:(k + 1) * P], sel2,
                                     start=True, stop=True)
                last.then_inc(mod_turned, 1)

            pe.wait_ge(silu_ready, 2)
            for s in range(6):
                if s >= 2:
                    pe.wait_ge(ada_saved, s - 1)
                if s >= 2:
                    pe.wait_ge(mod_saved, [0, 0, 1, 2, 2, 3][s])
                if s == 1:
                    pe.wait_ge(vec_saved, 3)
                for q in range(4):
                    for j in range(4):
                        full((4 * q + j) % SLOTS, 2 * s + q // 2)
                    for n in range(4):
                        for j in range(4):
                            k = 4 * q + j
                            mm = pe.matmul(ps[32 * j:32 * j + 32, 4 * (s % 2) + n, :], silu_cT[:, k, :],
                                           ring[:, k % SLOTS, n * 512:(n + 1) * 512], start=(q == 0), stop=(q == 3),
                                           tile_position=(0, 32 * j))
                            if n == 3:
                                mm.then_inc(slot_used[k % SLOTS], 1)
                if s in (1, 2, 4, 5):
                    turn_mod(s - 1, s)

            pe.wait_ge(mod_saved, 4)
            pe.wait_ge(ada_saved, 6)
            pe.wait_ge(xn_ready, 1)
            turn_norm(0)

            pe.wait_ge(hT_saved, 8)
            pe.wait_ge(small_in, 16 * 10)
            for p in range(NP):
                for k in range(KT):
                    mm = pe.matmul(ps[:, 7, 32 * p:32 * p + 32], hT[:, k, p * P:(p + 1) * P], w_ba[:, k, :],
                                   start=(k == 0), stop=(k == KT - 1))
            mm.then_inc(ba_done, 1)

            def in_group(n, r, turned):
                b0 = 4 * (n % 2)
                for j in range(SLOTS):
                    full(j, r)
                    w = ring[:, j, :].rearrange("p (k n) -> p k n", k=2)
                    for kk in range(2):
                        k = 2 * j + kk
                        if turned:
                            for m in range(8):
                                mm = pe.matmul(ps[:, b0 + m // 2, 256 * (m % 2):256 * (m % 2) + 256],
                                               w[:, kk, m * P:(m + 1) * P], hT[:, k, :],
                                               start=(k == 0 and m % 2 == 0), stop=(k == KT - 1),
                                               skip_group_check=True)
                        else:
                            for p in range(NP):
                                for h in range(2):
                                    mm = pe.matmul(ps[:, b0 + 2 * p + h, :], hT[:, k, p * P:(p + 1) * P],
                                                   w[:, kk, h * 512:(h + 1) * 512], start=(k == 0), stop=(k == KT - 1))
                    mm.then_inc(slot_used[j], 1)
                return mm

            for n in range(7):
                if n == 1:
                    pe.wait_ge(ba_saved, 1)
                if n >= 2:
                    pe.wait_ge(in_saved, n - 1)
                in_group(n, R_IN + n, n < 3)

            pe.wait_ge(in_saved, 7)
            for p in range(NP):
                if p == 1:
                    pe.wait_ge(rope_done, 2)
                    pe.wait_ge(at_in, 32)
                    pe.wait_ge(at_oT_saved, 1)
                for h in range(H):
                    pe.transpose(ps[:, h // 4, (h % 4) * P:(h % 4 + 1) * P], qkvb[:, 0, p, h * P:(h + 1) * P], ident)
                for h in range(H):
                    last = pe.transpose(ps[:, 2 + h // 4, (h % 4) * P:(h % 4 + 1) * P],
                                        qkvb[:, 1, p, h * P:(h + 1) * P], ident)
                if p == 1:
                    for h in range(H):
                        last = pe.transpose(ps[:, 4 + h // 4, (h % 4) * P:(h % 4 + 1) * P],
                                            ck[:, h * P:(h + 1) * P], ident)
                last.then_inc(at_turned, 1)
                pe.wait_ge(at_saved, p + 1)
                for h in range(H):
                    for m in range(2):
                        rows = slice(64 * m, 64 * m + 64)
                        if p == 0:
                            out = ps[:, 2 * m + h // 4, (h % 4) * P:(h % 4 + 1) * P]
                            last = pe.matmul(out, qT[rows, h, :], kT[rows, h, :], start=True, stop=True)
                        else:
                            for s, keys in enumerate((kcT, kT)):
                                at = 256 * (h % 2) + P * s
                                last = pe.matmul(ps[:, 4 * m + h // 2, at:at + P], qT[rows, h, :], keys[rows, h, :],
                                                 start=True, stop=True)
                last.then_inc(at_scores, 1)
                pe.wait_ge(at_prob, p + 1)
                nk = 1 + p
                pr = cent[:, 0:H * nk * P].rearrange("p (h k n) -> p h k n", h=H, n=P)
                for s in range(nk):
                    for h in range(H):
                        last = pe.transpose(ps[:, 2 * s + h // 4, (h % 4) * P:(h % 4 + 1) * P], pr[:, h, s, :], ident)
                last.then_inc(at_pT, 1)
                pe.wait_ge(at_pT_saved, p + 1)
                for h in range(H):
                    for s in range(nk):
                        v = cv if (p == 1 and s == 0) else qkvb[:, 2, p, :]
                        last = pe.matmul(ps[:, 4 + h // 4, (h % 4) * P:(h % 4 + 1) * P], pT[:, s, h, :],
                                         v[:, h * P:(h + 1) * P], start=(s == 0), stop=(s == nk - 1))
                last.then_inc(at_o, 1)
                pe.wait_ge(at_on, p + 1)
                for h in range(H):
                    last = pe.transpose(ps[:, 6 + h // 4, (h % 4) * P:(h % 4 + 1) * P], o_b[:, h * P:(h + 1) * P], ident)
                last.then_inc(at_oT, 1)

            pe.wait_ge(l2_sq, 1)
            pe.wait_ge(at_oT_saved, 2)
            for b in range(8):
                last = pe.matmul(ps[:, b, :], ones, l2_buf[:, b * 512:(b + 1) * 512], start=True, stop=True)
            last.then_inc(l2_sum, 1)
            pe.wait_ge(l2_root, 1)
            pe.wait_ge(bag_ready, 1)
            for p in range(NP):
                for d in range(2):
                    pe.matmul(ps[:, 0, 16 * p + 8 * d:16 * p + 8 * d + 8], U[d], g[:, p, 8 * d:8 * d + 8],
                              start=True, stop=True)
            pe.matmul(ps[:, 0, 32:48], ones, g[:, 0, :], start=True, stop=True).then_inc(gc_done, 1)
            pe.wait_ge(l2_done, 1)
            pe.wait_ge(gc_saved, 1)

            def each_head(bank, lhs, rhs):
                for h in range(H):
                    mm = pe.matmul(ps[:, bank + h // 4, (h % 4) * P:(h % 4 + 1) * P], lhs(h), rhs(h),
                                   start=True, stop=True)
                return mm

            for p in range(NP):
                tok = slice(p * P, (p + 1) * P)
                kTh = lambda h: convT[:, H + h, tok]
                qTh = lambda h: convT[:, h, tok]
                if p == 1:
                    pe.wait_ge(dl_oTs, 1)
                for h in range(H):
                    last = pe.transpose(ps[:, h // 4, (h % 4) * P:(h % 4 + 1) * P], convT[:, 2 * H + h, tok], ident)
                if p == 0:
                    for h in range(H):
                        last = pe.transpose(ps[:, 2 + h // 4, (h % 4) * P:(h % 4 + 1) * P], kTh(h), ident)
                last.then_inc(tok_turned, 1)
                pe.wait_ge(tok_saved, p + 1)
                for d in range(2):
                    n = 2 * p + d
                    pe.wait_ge(dl_rhs, n + 1)
                    if n in (1, 2):
                        pe.wait_ge(dl_Ss, n)
                    for b in range(2):
                        pe.matmul(ps[:, b, :], ones, At[:, 4 * b:4 * b + 4, :], start=True, stop=True)
                    for b in range(2):
                        pe.matmul(ps[:, 2 + b, :], ones, Aqk[:, 4 * b:4 * b + 4, :], start=True, stop=True)
                    each_head(4, kTh, kTh)
                    each_head(6, kTh, qTh).then_inc(dl_gram, 1)
                    pe.wait_ge(dl_A, n + 1)
                    if p == 1:
                        pe.wait_ge(s0_in, 16 * (d + 1))
                        each_head(6, kTh, lambda h: K_[:, h, :]).then_inc(dl_S0, 1)
                        pe.wait_ge(dl_S0r, 2 * d + 1)
                        each_head(6, qTh, lambda h: K_[:, h, :]).then_inc(dl_S0, 1)
                    for lv in range(LEVELS):
                        pe.wait_ge(dl_M, LEVELS * n + lv + 1)
                        each_head(0, lambda h: M_[:, h, :], lambda h: ident if lv == 0 else T_[:, h, :]).then_inc(dl_X, 1)
                        if lv:
                            pe.wait_ge(dl_Xs, (LEVELS - 1) * n + lv)
                            if lv < LEVELS - 1:
                                each_head(2, lambda h: Tt[:, h, :], lambda h: X_[:, h, :])
                            each_head(4, lambda h: X_[:, h, :], lambda h: Tt[:, h, :]).then_inc(dl_Y, 1)
                    pe.wait_ge(dl_T, n + 1)
                    pe.wait_ge(dl_R, n + 1)
                    each_head(6, lambda h: Tt[:, h, :], lambda h: E_[:, h, :]).then_inc(dl_V, 1)
                    pe.wait_ge(dl_Vs, n + 1)
                    each_head(0, lambda h: Aqk[:, h, :], lambda h: M_[:, h, :]).then_inc(dl_O, 1)
                    if p == 0:
                        pe.wait_ge(dl_Vd, d + 1)
                        each_head(2, lambda h: K_[:, h, :], lambda h: X_[:, h, :]).then_inc(dl_S, 1)
                pe.wait_ge(dl_on, p + 1)
                for h in range(H):
                    last = pe.transpose(ps[:, 6 + h // 4, (h % 4) * P:(h % 4 + 1) * P], O_[:, h, :], ident)
                last.then_inc(dl_oT, 1)

            pe.wait_ge(dl_oTs, 2)
            pe.wait_ge(dl_Ss, 2)
            for n in range(4):
                if n >= 2:
                    pe.wait_ge(gm_saved, n - 1)
                in_group(n, R_GM + n, False)

            for br, r in ((0, R_UPA), (1, R_UPB)):
                src = (oaT, obT)[br]
                for p in range(NP):
                    if br == 0:
                        pe.wait_ge(gm_saved, 3 + p)
                    else:
                        pe.wait_ge(up_saved, 1 + p)
                    for k in range(H):
                        if p == 0:
                            full(k, r)
                        for n in range(4):
                            mm = pe.matmul(ps[:, 4 * p + n, :], src[:, k, p * P:(p + 1) * P],
                                           ring[:, k, n * 512:(n + 1) * 512], start=(k == 0), stop=(k == H - 1))
                        if p == 1:
                            mm.then_inc(slot_used[k], 1)
                    if p == 0:
                        mm.then_inc(up_done, 1)
            pe.wait_ge(up_saved, 4)
            for b in range(8):
                for kk in range(2):
                    for p in range(NP):
                        last = pe.transpose(ps[:, b, (2 * kk + p) * P:(2 * kk + p + 1) * P],
                                            mixed[:, p, (2 * b + kk) * P:(2 * b + kk + 1) * P], ident)
            last.then_inc(mix_T, 1)

            def spread_gate(n, sem_done):
                for p in range(NP):
                    for b in range(4):
                        last = pe.matmul(ps[:, 4 * p + b, :], sel_row[p], gate_rows[:, n, b * 512:(b + 1) * 512],
                                         start=True, stop=True)
                last.then_inc(sem_done, 1)

            pe.wait_ge(mix_Ts, 1)
            spread_gate(0, gt_done)
            pe.wait_ge(gt_saved, 1)
            for k in range(KT):
                full(k % SLOTS, R_O + k // SLOTS)
                for p in range(NP):
                    for n in range(4):
                        mm = pe.matmul(ps[:, 4 * p + n, :], hT[:, k, p * P:(p + 1) * P],
                                       ring[:, k % SLOTS, n * 512:(n + 1) * 512], start=(k == 0), stop=(k == KT - 1))
                mm.then_inc(slot_used[k % SLOTS], 1)

            pe.wait_ge(xn_ready, 2)
            turn_norm(1)
            pe.wait_ge(hT_saved, 16)
            for p in range(NP):
                for k in range(KT):
                    last = pe.transpose(ps[:, 4 * p + k // 4, (k % 4) * P:(k % 4 + 1) * P],
                                        hT[:, k, p * P:(p + 1) * P], ident)
            last.then_inc(h2_T, 1)
            pe.wait_ge(h2_saved, 1)
            for p in range(NP):
                for k in range(KT):
                    last = pe.matmul(ps[:, 0, 36 * p:36 * p + 36], hT[:, k, p * P:(p + 1) * P], w_rt[:, k, :],
                                     start=(k == 0), stop=(k == KT - 1))
            last.then_inc(rt_done, 1)
            pe.wait_ge(rt_mask, 1)
            pe.matmul(ps[:, 1, 0:32], strict, r_mask[:, 0, :], start=True, stop=True)
            pe.matmul(ps[:, 1, 32:64], ones, r_mask[:, 0, :], start=True, stop=False)
            pe.matmul(ps[:, 1, 32:64], strict, r_mask[:, 1, :], start=False, stop=True)
            pe.matmul(ps[:, 1, 64:96], ones, r_mask[:, 0, :], start=True, stop=False)
            pe.matmul(ps[:, 1, 64:96], ones, r_mask[:, 1, :], start=False, stop=True).then_inc(rt_pos, 1)
            pe.wait_ge(rt_ready, 1)
            spread_gate(1, gt_done)
            pe.wait_ge(gt_saved, 2)
            n_slabs = pe.value_load(n_slab[0:1, 0:1], min_val=1, max_val=MAX_SLABS)
            seen = pe.alloc_register("pe_seen")
            turn = pe.alloc_register("pe_turn")
            pe.reg_mov(seen, 1)
            pe.reg_mov(turn, 1)

            def gather(half, t):
                if half == 0:
                    pe.wait_ge(mo_P, t)
                for k in range(8 * half, 8 * half + 8):
                    for p in range(NP):
                        mm = pe.matmul(ps[:, 3 + k // 4, (k % 4) * P:(k % 4 + 1) * P], h2[:, p, k * P:(k + 1) * P],
                                       onehot[:, p, :], start=(p == 0), stop=(p == 1))
                mm.then_inc(mo_gath, 1)

            def scatter(v):
                pe.wait_ge(mo_dns, v)
                pe.wait_ge(mo_PTs, v)
                for j in range(8):
                    if j >= 4:
                        pe.wait_ge(mo_ys, v * 8 + (j - 3))
                    pe.matmul(ps[:, 3 + j % 4, :], ohT[:, j // 4, :], oe[:, (j % 4) * 512:(j % 4 + 1) * 512],
                              start=True, stop=True).then_inc(mo_y, 1)

            def expand(part, v):
                for q in range(4):
                    for e in range(2):
                        pe.wait_ge(slot_full[2 * q + e], (v * 3 + (R_MOE - 3 + part + 1)) * 16)
                    for kk in range(4):
                        for e in range(2):
                            k = 4 * q + kk
                            mm = pe.matmul(ps[CAP * e:CAP * e + CAP, part, :], hg[:, k, CAP * e:CAP * e + CAP],
                                           ring[:, 2 * q + e, kk * 512:(kk + 1) * 512],
                                           start=(k == 0), stop=(k == KT - 1))
                            if kk == 3:
                                mm.then_inc(slot_used[2 * q + e], 1)

            with pe.Fori(0, n_slabs):
                t = pe.snap(turn)
                pe.wait_ge(mo_dns, pe.snap(seen))
                for half in range(2):
                    gather(half, t)
                pe.reg_add(turn, turn, 1)
                with pe.Fori(0, PAIRS):
                    v, t = pe.snap(seen), pe.snap(turn)
                    pe.wait_ge(mo_gaths, t * 2 - 2)
                    expand(0, v)
                    scatter(v)
                    for p in range(NP):
                        last = pe.transpose(ps[:, 7, p * P:(p + 1) * P], onehot_c[:, p, :], ident)
                    last.then_inc(mo_PT, 1)
                    expand(1, v)
                    pe.wait_ge(mo_ys, v * 8 + 8)
                    gather(0, t)
                    pe.wait_ge(mo_act, v)
                    for f in range(4):
                        last = pe.transpose(ps[:, 2, f * P:(f + 1) * P], a_act[:, f * P:(f + 1) * P], ident)
                    last.then_inc(mo_aT, 1)
                    gather(1, t)
                    pe.wait_ge(mo_aTs, v)
                    pe.wait_ge(mo_gaths, t * 2)
                    for f in range(4):
                        for e in range(2):
                            pe.wait_ge(slot_full[2 * f + e], (v * 3 + R_MOE) * 16)
                        for n in range(4):
                            for e in range(2):
                                mm = pe.matmul(ps[CAP * e:CAP * e + CAP, 3 + n, :], aT[:, f, CAP * e:CAP * e + CAP],
                                               ring[:, 2 * f + e, n * 512:(n + 1) * 512],
                                               start=(f == 0), stop=(f == 3))
                                if n == 3:
                                    mm.then_inc(slot_used[2 * f + e], 1)
                    pe.reg_add(seen, seen, 1)
                    pe.reg_add(turn, turn, 1)
            scatter(pe.snap(seen))

        @block.vector
        def _(dve):
            count = [0]

            def step(ins):
                ins.then_inc(dve_step, 1)
                count[0] += 1
                dve.wait_ge(dve_step, count[0])

            tt, ts, stt, red = dve.tensor_tensor, dve.tensor_scalar, dve.scalar_tensor_tensor, dve.tensor_reduce
            MUL, ADD, SUB, MAX, EQ = ALU.mult, ALU.add, ALU.subtract, ALU.max, ALU.is_equal
            roots = [0]

            def rsqrt_mean(ssq, out, n):
                w = ssq.shape[1]
                ts(ms[:, 0:w], ssq, 1.0 / n, EPS, MUL, ADD).then_inc(ms_ready, 1)
                roots[0] += 1
                dve.wait_ge(root_ready, roots[0])
                step(dve.reciprocal(out, rs[:, 0:w]))

            dve.memset(silu_cT[:, :, :], 0.0).then_inc(vec_saved, 1)
            dve.memset(eps[:, :], EPS).then_inc(vec_saved, 1)
            dve.wait_ge(vec_turned, 1)
            dve.tensor_copy(vecT[:, :], ps[:, 7, 0:P])
            dve.tensor_copy(cw[:, :, :], ps[:, 7, P:P + 72].rearrange("p (i m) -> p i m", i=3)).then_inc(vec_saved, 1)
            dve.wait_ge(ssq_ready, 2)
            rsqrt_mean(mx[:, 0:2], den[:, 0:2], D)
            for p in range(NP):
                last = ts(xin[:, p, :], xin[:, p, :], den[:, p:p + 1], None, MUL)
            last.then_inc(xn_ready, 1)

            for n, s in enumerate((0, 1, 3, 4)):
                dve.wait_ge(mod_turned, n + 1)
                tt(mod[:, s, :, :], ps[:, 4 * (s % 2), 0:32].rearrange("p (k a) -> p k a", a=NP),
                   vecT[:, 16 * s:16 * s + 16].unsqueeze(2).to_broadcast([P, KT, NP]), ADD).then_inc(mod_saved, 1)
            dve.wait_ge(mod_saved, 4)
            for n, s in enumerate((1, 4)):
                gain = vecT[:, 96 + 16 * n:112 + 16 * n].unsqueeze(2).to_broadcast([P, KT, NP])
                step(stt(modA[:, n, :, :], mod[:, s, :, :], 1.0, gain, ADD, MUL))

            def modulate(n):
                for b in range(8):
                    out = hT[:, 2 * b:2 * b + 2, :].rearrange("p k (a t) -> p (k a) t", a=NP)
                    a = modA[:, n, 2 * b:2 * b + 2, :].rearrange("p k a -> p (k a)")
                    s = mod[:, 3 * n, 2 * b:2 * b + 2, :].rearrange("p k a -> p (k a)")
                    dve.wait_ge(xn_turned, 8 * n + b + 1)
                    step(tt(out, heads(ps[:, b, :]), per_head(a), MUL))
                    tt(out, out, per_head(s), ADD).then_inc(hT_saved, 1)

            modulate(0)

            dve.wait_ge(ba_done, 1)
            dve.tensor_copy(ba[:, :, :], ps[:, 7, 0:64].rearrange("p (a n) -> p a n", a=NP)).then_inc(ba_saved, 1)
            dve.wait_ge(ba_saved, 1)
            dve.wait_ge(small_in, 16 * 10)
            al = ba[:, :, 16:32]
            sp_ = sc[:, 1, 0:32].rearrange("p (a n) -> p a n", a=NP)
            sg_ = sc[:, 0, 0:32].rearrange("p (a n) -> p a n", a=NP)
            step(tt(al, al, over_heads(dtb[:, :], NP), ADD))
            step(tt(lamv[:, 0, :], lamv[:, 0, :], lamv[:, 1, :], MUL))
            step(tt(lamv[:, 2, :], lamv[:, 2, :], lamv[:, 3, :], MUL))
            step(red(lam_t[:, 0:1], lamv[:, 0, :], AX, ADD))
            step(red(lam_t[:, 1:2], lamv[:, 2, :], AX, ADD))
            step(ts(subln[:, :], subln[:, :], 1.0 - LAM_INIT, None, MUL))
            stt(sp_, al, -1.0, al, MUL, MAX).then_inc(bag_dve, 1)
            def conv(n):
                dve.wait_ge(conv_mid, n + 1)
                for m in range(8):
                    src = ps[:, 4 * (n % 2) + m // 2, 256 * (m % 2):256 * (m % 2) + 256].rearrange("p (a t) -> p a t", a=NP)
                    dst = convT[:, 8 * n + m, :].rearrange("p (a t) -> p a t", a=NP)
                    step(stt(dst[:, :, 1:P], src[:, :, 0:P - 1], cw[:, 0, 8 * n + m:8 * n + m + 1], dst[:, :, 1:P], MUL, ADD))
                    last = stt(dst[:, :, 0:P - 1], src[:, :, 1:P], cw[:, 2, 8 * n + m:8 * n + m + 1], dst[:, :, 0:P - 1], MUL, ADD)
                last.then_inc(in_saved, 1)

            for n in range(3):
                conv(n)
            dve.wait_ge(bag_exp, 1)
            step(ts(sc[:, :, 0:32], sc[:, :, 0:32], 1.0, None, ADD))
            step(tt(lam_t[:, 2:3], lam_t[:, 0:1], lam_t[:, 1:2], SUB))
            step(ts(lam_t[:, 2:3], lam_t[:, 2:3], LAM_INIT, None, ADD))
            dve.reciprocal(beta[:, :, :], sg_).then_inc(bag_dve, 1)
            dve.wait_ge(bag_exp, 2)
            step(stt(al, al, 0.0, sp_, MAX, ADD))
            step(stt(g[:, :, :], al, -1.0, over_heads(alog[:, :], NP), MUL, MUL))
            dve.tensor_copy(sc[:, 0, 32:33], g[:, 0, 0:1]).then_inc(bag_ready, 1)

            for p in range(NP):
                nk = 1 + p
                dve.wait_ge(in_saved, 7)
                if p == 1:
                    dve.wait_ge(at_pT, 1)
                    for s in range(2):
                        if s:
                            dve.wait_ge(rope_done, 1)
                        x = qkvb[:, s, 1, :]
                        x64 = x.rearrange("p (m d) -> p m d", d=64)
                        cos = over_heads(cst[:, C_COS:C_COS + 64], 16)
                        step(tt(rope_a.rearrange("p (m d) -> p m d", d=64), x64, cos, MUL))
                        x4 = x.rearrange("p (m f x n) -> p m f x n", m=16, f=2, x=2)
                        b4 = rope_b.rearrange("p (m f x n) -> p m f x n", m=16, f=2, x=2)
                        sn = cst[:, C_SIN:C_SIN + 64].rearrange("p (f x n) -> p f x n", f=2, x=2)
                        for h in range(2):
                            sin = sn[:, :, h, :].unsqueeze(1).to_broadcast([P, 16, 2, 16])
                            step(tt(b4[:, :, :, h, :], x4[:, :, :, 1 - h, :], sin, MUL))
                        tt(x, rope_a, rope_b, ADD).then_inc(rope_done, 1)
                K = nk * P
                c4 = cent[:, 0:16 * K].rearrange("p (m n) -> p m n", m=16)
                dve.wait_ge(at_scores, p + 1)
                scores = banks(0, 4 * nk).rearrange("p (m n) -> p m n", m=16)
                step(red(mx[:, :], scores, AX, MAX))
                tt(c4, scores, per_head(mx[:, :], K), SUB).then_inc(at_cent, 1)
                dve.wait_ge(at_exp, p + 1)
                step(red(den[:, :], c4, AX, ADD))
                step(dve.reciprocal(den[:, :], den[:, :]))
                step(ts(den[:, 8:16], den[:, 8:16], lam_t[:, 2:3], None, MUL))
                step(tt(c4, c4, per_head(den[:, :], K), MUL))
                tt(c4[:, 0:8, :], c4[:, 0:8, :], c4[:, 8:16, :], SUB).then_inc(at_prob, 1)
                dve.wait_ge(at_o_saved, p + 1)
                step(tt(o_sq, o_b, o_b, MUL))
                step(red(mx[:, 0:8], heads(o_sq), AX, ADD))
                rsqrt_mean(mx[:, 0:8], den[:, 0:8], P)
                step(tt(heads(o_b), heads(o_b), per_head(den[:, 0:8]), MUL))
                tt(heads(o_b), heads(o_b), over_heads(subln[:, :]), MUL).then_inc(at_on, 1)

            dve.wait_ge(conv_done, 3)
            dve.wait_ge(at_scores, 2)
            dve.wait_ge(kv_out, 32)
            dve.wait_ge(at_oT, 2)
            tt(l2_buf, convT[:, 0:16, :].rearrange("p m t -> p (m t)"), convT[:, 0:16, :].rearrange("p m t -> p (m t)"),
               MUL).then_inc(l2_sq, 1)
            dve.wait_ge(l2_root, 1)
            step(dve.reciprocal(l2_buf, l2_buf))
            q2 = convT[:, 0:8, :].rearrange("p m t -> p (m t)")
            k2 = convT[:, 8:16, :].rearrange("p m t -> p (m t)")
            stt(q2, l2_buf[:, 0:2048], float(P) ** -0.5, q2, MUL, MUL)
            tt(k2, k2, l2_buf[:, 2048:4096], MUL).then_inc(l2_done, 1)
            dve.wait_ge(gc_done, 1)
            step(dve.tensor_copy(gc[:, :], ps[:, 0, 0:48]))
            tt(gc[:, 32:48], gc[:, 32:48], gc[:, 0:16], SUB).then_inc(gc_saved, 1)
            dve.wait_ge(gc_saved, 1)
            dve.wait_ge(gc_exp, 1)
            dve.wait_ge(lv_in, 16)
            for p in range(NP):
                for d in range(2):
                    n = 2 * p + d
                    hd = slice(8 * d, 8 * d + 8)
                    if n:
                        dve.wait_ge(dl_O, n)
                    if n in (1, 2):
                        dve.wait_ge(dl_S, n)
                    elif n == 0:
                        dve.wait_ge(l2_done, 1)
                    step(tt(At[:, :, :], over_heads(U[d]), per_head(g[:, p, hd]), MUL))
                    tt(Aqk[:, :, :], over_heads(ident), per_head(beta[:, p, hd]), MUL).then_inc(dl_rhs, 1)
                    dve.wait_ge(dl_gram, n + 1)
                    gcp = gc[:, 16 * p + 8 * d:16 * p + 8 * d + 8]
                    step(tt(E_, heads(banks(0, 2)), per_head(gcp), SUB))
                    ts(E_, E_, 0.0, None, ALU.min).then_inc(dl_diff, 1)
                    dve.wait_ge(dl_dec, n + 1)
                    step(tt(E_, E_, over_heads(U[d]), MUL))
                    tt(Aqk, heads(banks(6, 2)), E_, MUL)
                    step(tt(At, heads(banks(4, 2)), E_, MUL))
                    tt(At, At, heads(banks(2, 2)), MUL).then_inc(dl_A, 1)
                    dve.wait_ge(dl_A, n + 1)
                    if p == 0:
                        dve.wait_ge(tok_saved, 1)
                        tt(E_, V_, per_head(beta[:, p, hd]), MUL).then_inc(dl_R, 1)
                    else:
                        egcp = per_head(egc[:, 16 + 8 * d:24 + 8 * d])
                        dve.wait_ge(tok_saved, 2)
                        dve.wait_ge(dl_S0, 2 * d + 1)
                        tt(E_, heads(banks(6, 2)), egcp, MUL).then_inc(dl_S0r, 1)
                        dve.wait_ge(dl_S0r, 2 * d + 1)
                        step(tt(E_, V_, E_, SUB))
                        tt(E_, E_, per_head(beta[:, p, hd]), MUL).then_inc(dl_R, 1)
                        dve.wait_ge(dl_S0, 2 * d + 2)
                        if d == 0:
                            tt(O_, heads(banks(6, 2)), egcp, MUL).then_inc(dl_S0r, 1)
                        else:
                            step(tt(M_, heads(banks(6, 2)), egcp, MUL))
                            tt(O_, O_, M_, ADD).then_inc(dl_S0r, 1)
                        dve.wait_ge(dl_S0r, 2 * d + 2)
                    if n in (1, 2):
                        dve.wait_ge(st_out, 16 * n)
                    for lv in range(LEVELS):
                        tt(M_, At, over_heads(lvl[:, lv, d, :]), MUL).then_inc(dl_M, 1)
                        dve.wait_ge(dl_X, LEVELS * n + lv + 1)
                        if lv == 0:
                            dve.wait_ge(dl_M, LEVELS * n + 1)
                            tt(T_, over_heads(ident), heads(banks(0, 2)), SUB)
                            step(tt(Tt, over_heads(ident), M_, SUB))
                        else:
                            dve.wait_ge(dl_Y, (LEVELS - 1) * n + lv)
                            if lv < LEVELS - 1:
                                tt(T_, T_, heads(banks(2, 2)), SUB)
                                step(tt(Tt, Tt, heads(banks(4, 2)), SUB))
                            else:
                                tt(Tt, Tt, heads(banks(4, 2)), SUB).then_inc(dl_T, 1)
                    if p == 0:
                        dve.wait_ge(dl_Vs, n + 1)
                        tt(X_, M_, per_head(egl[:, hd]), MUL).then_inc(dl_Vd, 1)
                    dve.wait_ge(dl_O, n + 1)
                    if n == 0:
                        step(dve.tensor_copy(O_, heads(banks(0, 2))))
                    else:
                        step(tt(O_, O_, heads(banks(0, 2)), ADD))
                sq = E_
                step(tt(sq, O_, O_, MUL))
                step(red(mx[:, 0:8], sq, AX, ADD))
                rsqrt_mean(mx[:, 0:8], den[:, 0:8], P)
                step(tt(O_, O_, per_head(den[:, 0:8]), MUL))
                step(tt(O_, O_, over_heads(onorm[:, :]), MUL))
                tt(O_, O_, heads(gateS[:, p, :]), MUL).then_inc(dl_on, 1)
                if p == 0:
                    dve.wait_ge(dl_oT, 1)

            for br in range(2):
                for p in range(NP):
                    if p == 0:
                        dve.wait_ge(up_done, br + 1)
                    else:
                        dve.wait_ge(round_done, R_UPA + br + 1)
                    dve.wait_ge(gm_saved, 4)
                    up = banks(4 * p, 4).rearrange("p (s n) -> p s n", s=2)
                    mix = mixed[:, p, :].rearrange("p (s n) -> p s n", s=2)
                    if br == 0:
                        tt(mix, up, gm[:, 0:2, p, :], MUL).then_inc(up_saved, 1)
                    else:
                        t = gm_tmp.rearrange("p (s n) -> p s n", s=2)
                        dve.wait_ge(up_saved, 1 + 2 + p - 1)
                        step(tt(t, up, gm[:, 2:4, p, :], MUL))
                        tt(mix, mix, t, ADD).then_inc(up_saved, 1)
            dve.wait_ge(gt_done, 1)
            dve.wait_ge(gt_in, 32)
            gt_flat = gt_b.rearrange("p a n -> p (a n)")
            tt(gt_flat, gt_flat, banks(0, 8), ADD).then_inc(gt_saved, 1)
            dve.wait_ge(gt_saved, 1)
            dve.wait_ge(round_done, R_O + 2)
            dve.wait_ge(x_in, 32)
            for p in range(NP):
                step(tt(gt_b[:, p, :], banks(4 * p, 4), gt_b[:, p, :], MUL))
                tt(xres[:, p, :], xres[:, p, :], gt_b[:, p, :], ADD).then_inc(x_saved, 1)
            dve.wait_ge(ssq_ready, 4)
            rsqrt_mean(mx[:, 0:2], den[:, 0:2], D)
            for p in range(NP):
                last = ts(xn2[:, p, :], xres[:, p, :], den[:, p:p + 1], None, MUL)
            last.then_inc(xn_ready, 1)
            modulate(1)

            dve.wait_ge(rt_done, 1)
            step(tt(r_log, ps[:, 0, 0:72].rearrange("p (a n) -> p a n", a=NP), over_heads(b_rt[:, :], NP), ADD))
            le = r_log[:, :, NG:].rearrange("p a (g e) -> p a g e", g=NG)
            gl = r_log[:, :, 0:NG]

            def first_max(out, vals, top, t, n):
                step(red(top, vals, AX, MAX))
                step(tt(t, vals, per_head(top, n), EQ))
                step(tt(t, t, over_heads(cst[:, C_TIE:C_TIE + n], NP), MUL))
                step(red(r_tm, t, AX, MAX))
                step(tt(out, t, per_head(r_tm, n), EQ))

            first_max(r_goh, gl, r_gmax, r_t4, NG)
            step(tt(r_ge, gl, per_head(r_gmax, NG), SUB))
            big4 = r_big.rearrange("p a (g e) -> p a g e", g=NG)
            step(tt(big4, le, r_goh.unsqueeze(3).to_broadcast([P, NP, NG, EG]), MUL))
            step(red(r_les, r_big.rearrange("p a (g e) -> p a e g", g=NG), AX, ADD))
            first_max(r_oh1, r_les, r_m1, r_t8, EG)
            step(stt(r_les2, r_oh1, -1e30, r_les, MUL, ADD))
            first_max(r_oh2, r_les2, r_m2, r_t8, EG)
            step(tt(r_s8, r_oh1, r_oh2, ADD))
            mask4 = r_mask.rearrange("p a (g e) -> p a g e", g=NG)
            goh4 = r_goh.unsqueeze(3).to_broadcast([P, NP, NG, EG])
            tt(mask4, goh4, r_s8.unsqueeze(2).to_broadcast([P, NP, NG, EG]), MUL).then_inc(rt_mask, 1)
            tt(r_e2, r_m2, r_m1, SUB).then_inc(rt_dve, 1)
            dve.wait_ge(rt_exp, 1)
            step(red(r_pg, r_ge, AX, ADD))
            step(ts(r_w1, r_e2, 1.0, None, ADD))
            step(tt(r_w1, r_w1, r_pg, MUL))
            step(dve.reciprocal(r_w1, r_w1))
            step(tt(r_w2, r_w1, r_e2, MUL))
            step(tt(r_c8, r_oh1, per_head(r_w1, EG), MUL))
            step(tt(r_t8, r_oh2, per_head(r_w2, EG), MUL))
            step(tt(r_c8, r_c8, r_t8, ADD))
            step(dve.memset(r_comb, 0.0))
            step(dve.memset(r_pos, 1024.0))
            step(tt(r_comb[:, :, 0:NE].rearrange("p a (g e) -> p a g e", g=NG), goh4,
                    r_c8.unsqueeze(2).to_broadcast([P, NP, NG, EG]), MUL))
            step(ts(r_big, r_mask, -1024.0, 1024.0, MUL, ADD))
            dve.wait_ge(rt_pos, 1)
            tt(r_pos[:, :, 0:NE], r_big, ps[:, 1, 0:64].rearrange("p (a n) -> p a n", a=NP), ADD).then_inc(places, 1)
            step(red(r_cnt, ps[:, 1, 64:96], AX, MAX))
            step(tt(r_gt, r_cnt.to_broadcast([P, 3]), cst[:, C_THR:C_THR + 3], ALU.is_gt))
            step(red(r_cnt, r_gt, AX, ADD))
            ts(n_slab[:, :], r_cnt, 1.0, None, ADD).then_inc(rt_ready, 1)
            for b in range(8):
                dve.memset(yacc_b[:, b, :], 0.0).then_inc(mo_ys, 1)
            dve.memset(ohT, 0.0).then_inc(mo_PTs, 1)
            dve.memset(oe, 0.0).then_inc(mo_dns, 1)
            dve.wait_ge(gt_done, 2)
            dve.wait_ge(gt_in, 64)
            gt2_flat = gt2_b.rearrange("p a n -> p (a n)")
            tt(gt2_flat, gt2_flat, banks(0, 8), ADD).then_inc(gt_saved, 1)
            dve.wait_ge(gt_saved, 2)
            dve.wait_ge(rt_ready, 1)
            n_slabs = dve.value_load(n_slab[0:1, 0:1], min_val=1, max_val=MAX_SLABS)
            seen = dve.alloc_register("dve_seen")
            turn = dve.alloc_register("dve_turn")
            dve.reg_mov(seen, 1)
            dve.reg_mov(turn, 1)
            oh4 = onehot.rearrange("p a (e s) -> p a e s", e=2)
            ohc4 = onehot_c.rearrange("p a (e s) -> p a e s", e=2)
            iota4 = cst[:, C_IOTA:C_IOTA + CAP].unsqueeze(1).unsqueeze(1).to_broadcast([P, NP, 2, CAP])

            def one_hots(at, t):
                pos4 = r_pos[:, :, bass.ds(at, 2)].unsqueeze(3).to_broadcast([P, NP, 2, CAP])
                comb4 = r_comb[:, :, bass.ds(at, 2)].unsqueeze(3).to_broadcast([P, NP, 2, CAP])
                tt(oh4, iota4, pos4, EQ).then_inc(mo_oh, 1)
                dve.wait_ge(mo_oh, t)
                tt(ohc4, oh4, comb4, MUL).then_inc(mo_P, 1)

            def gathered_back(v):
                dve.wait_ge(mo_ys, v * 8)
                for j in range(8):
                    dve.wait_ge(mo_y, v * 8 + (j - 7))
                    tt(yacc_b[:, j, :], yacc_b[:, j, :], ps[:, 3 + j % 4, :], ADD).then_inc(mo_ys, 1)

            with dve.Fori(0, n_slabs) as slab:
                t = dve.snap(turn)
                dve.wait_ge(places, slab + 1)
                one_hots(0, t)
                dve.reg_add(turn, turn, 1)
                with dve.Fori(0, PAIRS) as i:
                    v, t = dve.snap(seen), dve.snap(turn)
                    gathered_back(v)
                    dve.wait_ge(mo_PT, v)
                    one_hots(i * 2 + 2, t)
                    dve.wait_ge(mo_silu, v)
                    dve.wait_ge(round_done, v * 3 + (R_MOE - 1))
                    tt(a_act, a_silu, ps[:, 1, :], MUL).then_inc(mo_act, 1)
                    dve.reg_add(seen, seen, 1)
                    dve.reg_add(turn, turn, 1)
                t = dve.snap(turn)
                dve.wait_ge(mo_P, t - 1)
                dve.wait_ge(mo_gath, t * 2 - 2)
                ts(r_pos, r_pos, -float(CAP), None, ADD).then_inc(places, 1)
            v = dve.snap(seen)
            gathered_back(v)
            dve.wait_ge(mo_ys, v * 8 + 8)
            step(tt(yacc.rearrange("p a n -> p (a n)"), yacc.rearrange("p a n -> p (a n)"), gt2_flat, MUL))
            for p in range(NP):
                tt(xres[:, p, :], xres[:, p, :], yacc[:, p, :], ADD).then_inc(x_saved, 1)
            dve.wait_ge(ssq_ready, 6)
            rsqrt_mean(mx[:, 0:2], den[:, 0:2], D)
            dve.wait_ge(nf_in, 16)
            for p in range(NP):
                stt(yacc[:, p, :], xres[:, p, :], den[:, p:p + 1], nf_b, MUL, MUL).then_inc(y_ready, 1)

        @block.scalar
        def _(act):
            A = act.activation
            roots = [0]

            def root(w):
                roots[0] += 1
                act.wait_ge(ms_ready, roots[0])
                A(rs[:, 0:w], ms[:, 0:w], ACT.Sqrt).then_inc(root_ready, 1)

            def bcast(row):
                return row.partition_broadcast(P)

            act.dma_start(cst[:, :], consts).then_inc(boot_in, 16)
            for p, src in enumerate((c_ctx, c[0])):
                act.dma_start(cT[:, p, :], src.rearrange("(p k) -> p k", k=KT)).then_inc(boot_in, 16)
            act.dma_start(vec_rows[0:96, :], b_ada[0].rearrange("(r q) -> r q", q=P)).then_inc(boot_in, 16)
            act.dma_start(vec_rows[96:112, :], norm_mix[0].rearrange("(r q) -> r q", q=P)).then_inc(boot_in, 16)
            act.dma_start(vec_rows[112:128, :], norm_ffn[0].rearrange("(r q) -> r q", q=P)).then_inc(boot_in, 16)
            act.dma_start(conv_rows[0:72, :], conv_a[0].rearrange("i (m q) -> (i m) q", q=P)).then_inc(boot_in, 16)
            for p in range(NP):
                act.dma_start(xin[:, p, :], x_dram[p]).then_inc(boot_in, 16)
            act.dma_start(w_ba[:, :, :], in_dram[:, :, 4096:4128]).then_inc(small_in, 16)
            act.dma_start(w_rt[:, :, 0:NG], w_rg[0].rearrange("(k p) n -> p k n", p=P)).then_inc(small_in, 16)
            act.dma_start(w_rt[:, :, NG:], w_re[0].rearrange("(k p) n -> p k n", p=P)).then_inc(small_in, 16)
            for dst, src in ((alog[:, :], a_log[0].rearrange("a h -> (a h)")), (dtb[:, :], dt_bias[0].rearrange("a h -> (a h)")),
                             (lamv[:, :, :].rearrange("p a b -> p (a b)"), lam[0].rearrange("a h -> (a h)")),
                             (onorm[:, :], onorm_a[0]), (subln[:, :], subln_b[0]),
                             (b_rt[:, 0:NG], b_rg[0]), (b_rt[:, NG:], b_re[0])):
                act.dma_start(dst, bcast(src)).then_inc(small_in, 16)

            act.wait_ge(boot_in, 16 * 9)
            act.wait_ge(vec_saved, 1)
            for p in range(NP):
                A(silu_cT[:, :, p], cT[:, p, :], ACT.Silu).then_inc(silu_ready, 1)
            for p in range(NP):
                A(ar(8192 + 2048 * p, 2048), xin[:, p, :], ACT.Square, accum_out=mx[:, p:p + 1]).then_inc(ssq_ready, 1)
            root(2)
            for s in range(6):
                act.wait_ge(round_done, 2 * s + 2)
                if s >= 3:
                    act.wait_ge(mod_turned, 2)
                dst = {2: gate_rows[:, 0, :], 5: gate_rows[:, 1, :]}.get(s, ada_rows[:, s % 2, :])
                A(dst, banks(4 * (s % 2), 4), ACT.Copy).then_inc(ada_saved, 1)

            act.wait_ge(hT_saved, 8)
            act.dma_start(heads(cv), cache_v[0, 0].rearrange("h t d -> t h d")).then_inc(at_in, 16)
            act.wait_ge(vec_saved, 3)
            for n in range(3):
                act.wait_ge(round_done, R_IN + n + 1)
                for m in range(8):
                    last = A(convT[:, 8 * n + m, :], ps[:, 4 * (n % 2) + m // 2, 256 * (m % 2):256 * (m % 2) + 256],
                             ACT.Identity, scale=cw[:, 1, 8 * n + m:8 * n + m + 1])
                last.then_inc(conv_mid, 1)
                act.wait_ge(in_saved, n + 1)
                y = convT[:, 8 * n:8 * n + 8, :].rearrange("p m t -> p (m t)")
                A(y, y, ACT.Silu).then_inc(conv_done, 1)
            act.wait_ge(round_done, R_IN + 4)
            A(gateS.rearrange("p a n -> p (a n)"), banks(4, 4), ACT.Silu).then_inc(in_saved, 1)
            act.wait_ge(bag_dve, 1)
            A(sc[:, 0, 0:32].rearrange("p (a n) -> p a n", a=NP), ba[:, :, 0:16], ACT.Exp, scale=-1.0)
            A(sc[:, 1, 0:32], sc[:, 1, 0:32], ACT.Exp, scale=-1.0)
            A(alog[:, :], alog[:, :], ACT.Exp)
            A(lam_t[:, 0:2], lam_t[:, 0:2], ACT.Exp).then_inc(bag_exp, 1)
            act.wait_ge(bag_dve, 2)
            A(sc[:, 1, 0:32], sc[:, 1, 0:32], ACT.Ln).then_inc(bag_exp, 1)
            for n in range(4, 7):
                act.wait_ge(round_done, R_IN + n + 1)
                A(qkvb[:, n - 4, :, :].rearrange("p a n -> p (a n)"), banks(4 * (n % 2), 4), ACT.Copy).then_inc(in_saved, 1)
            act.wait_ge(in_saved, 7)
            act.dma_start(new_k[0, 0].rearrange("h t d -> t h d"), heads(qkvb[:, 1, 0, :])).then_inc(kv_out, 16)
            act.dma_start(new_v[0, 0].rearrange("h t d -> t h d"), heads(qkvb[:, 2, 0, :])).then_inc(kv_out, 16)

            for p in range(NP):
                nk = 1 + p
                if p == 1:
                    act.wait_ge(at_on, 1)
                    act.dma_start(heads(ck), cache_k[0, 0].rearrange("h t d -> t h d")).then_inc(at_in, 16)
                act.wait_ge(at_turned, p + 1)
                A(qT.rearrange("p h t -> p (h t)"), banks(0, 2), ACT.Copy)
                if p == 1:
                    A(kcT.rearrange("p h t -> p (h t)"), banks(4, 2), ACT.Copy)
                A(kT.rearrange("p h t -> p (h t)"), banks(2, 2), ACT.Copy).then_inc(at_saved, 1)
                act.wait_ge(at_cent, p + 1)
                n = 16 * nk * P
                A(cent[:, 0:n], cent[:, 0:n], ACT.Exp, scale=64.0 ** -0.5).then_inc(at_exp, 1)
                act.wait_ge(at_pT, p + 1)
                A(pT.rearrange("p k h q -> p (k h q)")[:, 0:1024 * nk], banks(0, 2 * nk), ACT.Copy).then_inc(at_pT_saved, 1)
                act.wait_ge(at_o, p + 1)
                A(o_b, banks(4, 2), ACT.Copy).then_inc(at_o_saved, 1)
                root(8)
                act.wait_ge(at_oT, p + 1)
                A(obT[:, :, p * P:(p + 1) * P], heads(banks(6, 2)), ACT.Copy).then_inc(at_oT_saved, 1)

            act.dma_start(lvl.rearrange("p n d i -> p (n d i)"), level_masks).then_inc(lv_in, 16)
            act.wait_ge(l2_sum, 1)
            A(l2_buf, banks(0, 8), ACT.Sqrt, bias=eps[:, :]).then_inc(l2_root, 1)
            act.wait_ge(gc_saved, 1)
            A(egc[:, :], gc[:, 0:32], ACT.Exp)
            A(egl[:, :], gc[:, 32:48], ACT.Exp).then_inc(gc_exp, 1)
            flat = lambda t: t.rearrange("p h t -> p (h t)")
            for p in range(NP):
                act.wait_ge(tok_turned, p + 1)
                if p == 0:
                    A(flat(K_), banks(2, 2), ACT.Copy)
                A(flat(V_), banks(0, 2), ACT.Copy).then_inc(tok_saved, 1)
                for d in range(2):
                    n = 2 * p + d
                    if p == 1:
                        act.wait_ge(*((dl_S, 2) if d == 0 else (dl_S0, 2)))
                        act.dma_start(K_, state_delta[0, 0, d].rearrange("h k v -> k h v")).then_inc(s0_in, 16)
                    act.wait_ge(dl_diff, n + 1)
                    A(flat(E_), flat(E_), ACT.Exp).then_inc(dl_dec, 1)
                    for lv in range(1, LEVELS):
                        act.wait_ge(dl_X, LEVELS * n + lv + 1)
                        A(flat(X_), banks(0, 2), ACT.Copy).then_inc(dl_Xs, 1)
                    act.wait_ge(dl_V, n + 1)
                    A(flat(M_), banks(6, 2), ACT.Copy).then_inc(dl_Vs, 1)
                    if p == 0:
                        act.wait_ge(dl_S, n + 1)
                        A(flat(T_), banks(2, 2), ACT.Copy).then_inc(dl_Ss, 1)
                        act.wait_ge(dl_Ss, n + 1)
                        act.dma_start(new_state[0, 0, d].rearrange("h k v -> k h v"), T_).then_inc(st_out, 16)
                root(8)
                act.wait_ge(dl_oT, p + 1)
                A(oaT[:, :, p * P:(p + 1) * P], heads(banks(6, 2)), ACT.Copy).then_inc(dl_oTs, 1)

            def load_gate_bias(section, dst):
                for p in range(NP):
                    act.dma_start(dst[:, p, :], bcast(b_ada[0, section * D:(section + 1) * D])).then_inc(gt_in, 16)

            act.wait_ge(dl_on, 2)
            load_gate_bias(2, gt_b)
            for n in range(4):
                act.wait_ge(round_done, R_GM + n + 1)
                A(gm[:, n, :, :].rearrange("p a n -> p (a n)"), banks(4 * (n % 2), 4), ACT.Sigmoid).then_inc(gm_saved, 1)
            act.wait_ge(up_saved, 4)
            for p in range(NP):
                act.dma_start(xres[:, p, :], x_dram[p]).then_inc(x_in, 16)
            act.wait_ge(mix_T, 1)
            A(hT[:, :, :].rearrange("p k t -> p (k t)"), banks(0, 8), ACT.Copy).then_inc(mix_Ts, 1)
            for p in range(NP):
                act.wait_ge(x_saved, p + 1)
                A(yacc[:, p, :], xres[:, p, :], ACT.Square, accum_out=mx[:, p:p + 1]).then_inc(ssq_ready, 1)
            root(2)
            load_gate_bias(5, gt2_b)
            act.wait_ge(h2_T, 1)
            A(h2.rearrange("p a n -> p (a n)"), banks(0, 8), ACT.Copy).then_inc(h2_saved, 1)
            act.wait_ge(rt_dve, 1)
            A(r_ge, r_ge, ACT.Exp)
            A(r_e2, r_e2, ACT.Exp).then_inc(rt_exp, 1)
            act.wait_ge(rt_ready, 1)
            n_slabs = act.value_load(n_slab[0:1, 0:1], min_val=1, max_val=MAX_SLABS)
            seen = act.alloc_register("act_seen")
            turn = act.alloc_register("act_turn")
            act.reg_mov(seen, 1)
            act.reg_mov(turn, 1)

            def save_gathered(half, t):
                act.wait_ge(mo_gath, t * 2 + (half - 1))
                A(hg[:, 8 * half:8 * half + 8, :].rearrange("p k s -> p (k s)"), banks(3 + 2 * half, 2),
                  ACT.Copy).then_inc(mo_gaths, 1)

            with act.Fori(0, n_slabs):
                t = act.snap(turn)
                save_gathered(0, t)
                save_gathered(1, t)
                act.reg_add(turn, turn, 1)
                with act.Fori(0, PAIRS):
                    v, t = act.snap(seen), act.snap(turn)
                    act.wait_ge(round_done, v * 3 + (R_MOE - 2))
                    A(a_silu, ps[:, 0, :], ACT.Silu).then_inc(mo_silu, 1)
                    act.wait_ge(mo_PT, v)
                    A(ohT.rearrange("p a t -> p (a t)"), ps[:, 7, 0:256], ACT.Copy).then_inc(mo_PTs, 1)
                    save_gathered(0, t)
                    act.wait_ge(mo_aT, v)
                    A(aT.rearrange("p k s -> p (k s)"), ps[:, 2, :], ACT.Copy).then_inc(mo_aTs, 1)
                    save_gathered(1, t)
                    act.wait_ge(round_done, v * 3 + R_MOE)
                    A(oe, banks(3, 4), ACT.Copy).then_inc(mo_dns, 1)
                    act.reg_add(seen, seen, 1)
                    act.reg_add(turn, turn, 1)
            act.dma_start(nf_b, bcast(norm_final)).then_inc(nf_in, 16)
            for p in range(NP):
                act.wait_ge(x_saved, p + 3)
                A(h2[:, p, :], xres[:, p, :], ACT.Square, accum_out=mx[:, p:p + 1]).then_inc(ssq_ready, 1)
            root(2)


_INS = ['x_prompt', 'x_sample', 'c', 'state_delta', 'cache_k', 'cache_v', 'c_ctx', 'w_ada', 'b_ada', 'norm_mix',
        'norm_ffn', 'w_in', 'conv_a', 'a_log', 'dt_bias', 'onorm_a', 'lam', 'subln_b', 'w_up_a', 'w_up_b', 'w_o',
        'w_rg', 'b_rg', 'w_re', 'b_re', 'w_e_gate', 'w_e_up', 'w_e_down', 'norm_final']
_OUTS = [(1, P, D), (1, P, D), (1, 1, 2, H, P, P), (1, 1, H, P, P), (1, 1, H, P, P)]


def kernel(**inputs):
    import concourse.bacc as _bacc
    from concourse.bass_utils import run_bass_kernel_spmd as _run

    nc = _bacc.Bacc("TRN2", target_bir_lowering=False, num_devices=1)
    arrays, args = {}, []
    given = {name: np.ascontiguousarray(inputs[name]) for name in _INS}
    given["constants"], given["level_masks"] = constants()
    for name, a in given.items():
        arrays[f"in_{name}_dram"] = a
        args.append(nc.dram_tensor(f"in_{name}_dram", a.shape, mybir.dt.from_np(a.dtype), kind="ExternalInput").ap())
    for i, shape in enumerate(_OUTS):
        args.append(nc.dram_tensor(f"out_{i}_dram", shape, F32, kind="ExternalOutput").ap())
    program(nc, *args)
    r = _run(nc, [arrays], core_ids=[0])
    return tuple(r.results[0][f"out_{i}_dram"] for i in range(len(_OUTS)))
```

```python
from contextlib import ExitStack

import numpy as np
import concourse.bass as bass
from concourse import mybir

F32 = mybir.dt.float32
I32 = mybir.dt.int32
ALU = mybir.AluOpType
ACT = mybir.ActivationFunctionType
AX = mybir.AxisListType.X

P = 128
NP = 2
D = 2048
KT = D // P
H = 8
HD = H * P
GW = 64
NG, EG = 4, 8
NE = NG * EG
FF = 512
EPS = 1e-6
LAM_INIT = 0.2
SLOTS = 8
SW = 2048
CAP = 64
PAIRS = NE // 2
MAX_SLABS = NP * P // CAP
LEVELS = 7
QKV_A = 3 * HD

R_IN = 4
R_BG = R_IN + 7
BG_ADA = [3, 3, 4, 4, 2, 2, 5, 5]
R_GM = R_BG + 16
R_UPA, R_UPB, R_O, R_MOE = R_GM + 8, R_GM + 10, R_GM + 12, R_GM + 16
HW = SW // 2
UNITS = 96

C_ID, C_ONE, C_U, C_SU, C_IOTA, C_SEL, C_COS, C_SIN, C_TIE, C_THR, C_SEL2 = (
    0, 128, 256, 512, 640, 704, 960, 1024, 1088, 1096, 1099)
C_N = 1104
A_CONV, A_GATE, A_QB, A_OBT, A_OAT, A_TMP, A_N = 0, 6144, 8192, 14336, 16384, 18432, 24324


def constants():
    i = np.arange(P)
    c = np.zeros((P, C_N), np.float32)
    c[:, C_ID:C_ID + P] = np.eye(P)
    c[:, C_ONE:C_ONE + P] = 1.0
    c[:, C_U:C_U + P] = i[:, None] <= i[None]
    c[:, C_U + P:C_U + 2 * P] = i[:, None] >= i[None]
    c[:, C_SU:C_SU + P] = i[:, None] < i[None]
    c[:, C_IOTA:C_IOTA + CAP] = np.arange(CAP)
    for p in range(NP):
        c[p::32, C_SEL + p * P:C_SEL + (p + 1) * P] = 1.0
        c[p::32, C_SEL2 + p] = 1.0
    nf = 16
    inv = (10000.0 ** (-np.arange(nf, dtype=np.float32) / nf)).astype(np.float32)
    for half, pos in enumerate((i // GW, i % GW)):
        ang = pos.astype(np.float32)[:, None] * inv
        for x in range(2):
            at = half * 32 + x * 16
            c[:, C_COS + at:C_COS + at + nf] = np.cos(ang)
            c[:, C_SIN + at:C_SIN + at + nf] = np.sin(ang) * (-1 if x == 0 else 1)
    c[:, C_TIE:C_TIE + 8] = 8 - np.arange(8)
    c[:, C_THR:C_THR + 3] = CAP * np.arange(1, 4)
    lv = np.zeros((P, LEVELS, 2, P), np.float32)
    for n in range(LEVELS):
        s = 1 << n
        same = (i[:, None] // (2 * s)) == (i[None] // (2 * s))
        lo, hi = (i // s) % 2 == 0, (i // s) % 2 == 1
        lv[:, n, 0] = same & lo[:, None] & hi[None]
        lv[:, n, 1] = same & hi[:, None] & lo[None]
    return c, lv.reshape(P, -1)


def program(nc, x_prompt, x_sample, c, state_delta, cache_k, cache_v, c_ctx, w_ada, b_ada, norm_mix, norm_ffn,
            w_in, conv_a, a_log, dt_bias, onorm_a, lam, subln_b, w_up_a, w_up_b, w_o, w_rg, b_rg, w_re, b_re,
            w_e_gate, w_e_up, w_e_down, norm_final, consts, level_masks,
            y_prompt, y_sample, new_state, new_k, new_v):
    ctx = ExitStack()
    with ctx:
        sb = lambda name, *shape, dt=F32: ctx.enter_context(nc.sbuf_tensor(name, [P, *shape], dt))
        sem = lambda name: ctx.enter_context(nc.semaphore(name))

        ring = sb("ring", SLOTS, SW)
        hT = sb("hT", KT, NP * P)
        gate_rows = sb("gate_rows", 2, D)
        cst = sb("cst", C_N)
        arena = sb("arena", A_N)
        silu_cT = sb("silu_cT", KT, 32)
        cT = sb("cT", NP, KT)
        vecT = sb("vecT", P)
        cw = sb("cw", 3, 24)
        mod = sb("mod", 6, KT, NP)
        modA = sb("modA", 2, KT, NP)
        w_ba = sb("w_ba", KT, 32)
        w_rt = sb("w_rt", KT, NG + NE)
        alog = sb("alog", 16)
        dtb = sb("dtb", 16)
        lamv = sb("lamv", 4, 64)
        onorm = sb("onorm", P)
        subln = sb("subln", P)
        b_rt = sb("b_rt", NG + NE)
        eps = sb("eps", 1)
        ba = sb("ba", NP, 32)
        sc = sb("sc", 2, 48)
        beta = sb("beta", NP, 16)
        g = sb("g", NP, 16)
        gc = sb("gc", 48)
        egc = sb("egc", 32)
        egl = sb("egl", 16)
        lam_t = sb("lam_t", 8)
        ms = sb("ms", 16)
        rs = sb("rs", 16)
        mx = sb("mx", 16)
        den = sb("den", 16)
        ps = ctx.enter_context(nc.psum_tensor("ps", [P, 8, 512], F32))

        ident = cst[:, C_ID:C_ID + P]
        ones = cst[:, C_ONE:C_ONE + P]
        U = [cst[:, C_U + d * P:C_U + (d + 1) * P] for d in range(2)]
        strict = cst[:, C_SU:C_SU + P]
        sel_row = [cst[:, C_SEL + p * P:C_SEL + (p + 1) * P] for p in range(NP)]
        sel2 = cst[:, C_SEL2:C_SEL2 + 2]

        def ar(at, n):
            return arena[:, at:at + n]

        def heads(ap):
            return ap.rearrange("p (h d) -> p h d", d=P)

        def per_head(ap, n=P):
            return ap.unsqueeze(2).to_broadcast([P, ap.shape[1], n])

        def over_heads(ap, m=H):
            return ap.unsqueeze(1).to_broadcast([P, m, ap.shape[1]])

        def banks(a, n):
            return ps[:, a:a + n, :].rearrange("p b n -> p (b n)")

        vec_rows = ar(4096, P)
        conv_rows = ar(4096 + P, P)
        xin = ar(A_TMP, 4096).rearrange("p (a d) -> p a d", a=NP)
        ada_rows = ar(0, 4096).rearrange("p (a d) -> p a d", a=2)
        convT = ar(A_CONV, 6144).rearrange("p (m t) -> p m t", t=NP * P)
        gateS = ar(A_GATE, 2048).rearrange("p (a n) -> p a n", a=NP)
        qkvb = ar(A_QB, 6144).rearrange("p (s a n) -> p s a n", s=3, a=NP)
        obT = ar(A_OBT, 2048).rearrange("p (h t) -> p h t", t=NP * P)
        oaT = ar(A_OAT, 2048).rearrange("p (h t) -> p h t", t=NP * P)

        slot_full = [sem(f"slot_full{j}") for j in range(SLOTS)]
        slot_used = [sem(f"slot_used{j}") for j in range(SLOTS)]
        round_done = slot_used[SLOTS - 1]
        boot_in = sem("boot_in")
        small_in = sem("small_in")
        vec_turned = sem("vec_turned")
        vec_saved = sem("vec_saved")
        silu_ready = sem("silu_ready")
        ada_saved = sem("ada_saved")
        mod_turned = sem("mod_turned")
        mod_saved = sem("mod_saved")
        ssq_ready = sem("ssq_ready")
        ms_ready = sem("ms_ready")
        root_ready = sem("root_ready")
        xn_ready = sem("xn_ready")
        xn_turned = sem("xn_turned")
        hT_saved = sem("hT_saved")
        ba_done = sem("ba_done")
        ba_saved = sem("ba_saved")
        conv_mid = sem("conv_mid")
        in_saved = sem("in_saved")
        conv_done = sem("conv_done")
        dve_step = sem("dve_step")
        act_step = sem("act_step")
        kv_out = sem("kv_out")
        bag_exp = sem("bag_exp")
        bag_dve = sem("bag_dve")
        bag_ready = sem("bag_ready")
        at_in = sem("at_in")
        rope_done = sem("rope_done")
        at_turned = sem("at_turned")
        at_saved = sem("at_saved")
        at_scores = sem("at_scores")
        at_cent = sem("at_cent")
        at_exp = sem("at_exp")
        at_prob = sem("at_prob")
        at_pT = sem("at_pT")
        at_pT_saved = sem("at_pT_saved")
        at_o = sem("at_o")
        at_o_saved = sem("at_o_saved")
        at_on = sem("at_on")
        at_oT = sem("at_oT")
        at_oT_saved = sem("at_oT_saved")
        l2_sq = sem("l2_sq")
        l2_sum = sem("l2_sum")
        l2_root = sem("l2_root")
        l2_done = sem("l2_done")
        gc_done = sem("gc_done")
        gc_saved = sem("gc_saved")
        gc_exp = sem("gc_exp")
        lv_in = sem("lv_in")
        tok_turned = sem("tok_turned")
        tok_saved = sem("tok_saved")
        s0_in = sem("s0_in")
        dl_rhs = sem("dl_rhs")
        dl_gcb = sem("dl_gcb")
        dl_gram = sem("dl_gram")
        dl_diff = sem("dl_diff")
        dl_dec = sem("dl_dec")
        dl_A = sem("dl_A")
        dl_M = sem("dl_M")
        dl_X = sem("dl_X")
        dl_Xs = sem("dl_Xs")
        dl_Y = sem("dl_Y")
        dl_T = sem("dl_T")
        dl_S0 = sem("dl_S0")
        dl_S0r = sem("dl_S0r")
        dl_R = sem("dl_R")
        dl_V = sem("dl_V")
        dl_Vs = sem("dl_Vs")
        dl_O = sem("dl_O")
        dl_Os = sem("dl_Os")
        dl_Vd = sem("dl_Vd")
        dl_S = sem("dl_S")
        dl_Ss = sem("dl_Ss")
        st_out = sem("st_out")
        dl_on = sem("dl_on")
        dl_oT = sem("dl_oT")
        dl_oTs = sem("dl_oTs")
        bg_saved = sem("bg_saved")
        bg_turned = sem("bg_turned")
        bg_kept = sem("bg_kept")
        gm_ready = sem("gm_ready")
        up_done = sem("up_done")
        up_saved = sem("up_saved")
        mix_T = sem("mix_T")
        mix_Ts = sem("mix_Ts")
        gt_in = sem("gt_in")
        gt_done = sem("gt_done")
        gt_saved = sem("gt_saved")
        x_saved = sem("x_saved")
        x_in = sem("x_in")
        h2_T = sem("h2_T")
        h2_saved = sem("h2_saved")
        rt_done = sem("rt_done")
        rt_exp = sem("rt_exp")
        rt_dve = sem("rt_dve")
        rt_mask = sem("rt_mask")
        rt_pos = sem("rt_pos")
        rt_ready = sem("rt_ready")
        places = sem("places")
        mo_oh = sem("mo_oh")
        mo_P = sem("mo_P")
        mo_gath = sem("mo_gath")
        mo_gaths = sem("mo_gaths")
        mo_PT = sem("mo_PT")
        mo_PTs = sem("mo_PTs")
        mo_silu = sem("mo_silu")
        mo_act = sem("mo_act")
        mo_aT = sem("mo_aT")
        mo_aTs = sem("mo_aTs")
        mo_dns = sem("mo_dns")
        mo_y = sem("mo_y")
        mo_ys = sem("mo_ys")
        nf_in = sem("nf_in")
        y_ready = sem("y_ready")
        y_out = sem("y_out")

        cent = ar(A_OAT, 4096)
        qT = heads(ar(A_OAT + 4096, 1024))
        kT = heads(ar(A_OAT + 5120, 1024))
        pT = ar(A_OAT + 4096, 2048).rearrange("p (k h q) -> p k h q", k=2, h=H)
        cv = ar(A_OAT + 6144, 1024)
        ck = ar(A_OAT + 2048, 1024)
        kcT = heads(ar(A_QB, 1024))
        rope_a = ar(A_OAT, 1024)
        rope_b = ar(A_OAT + 1024, 1024)
        o_b = ar(A_OAT + 3072, 1024)
        o_sq = ar(A_OAT + 2048, 1024)
        l2_buf = ar(A_QB, 4096)
        E_, Aqk, At, X_, T_, Tt = (heads(ar(A_QB + n * 1024, 1024)) for n in range(6))
        M_, V_, O_, K_ = (heads(ar(A_TMP + n * 1024, 1024)) for n in range(4))
        lvl = ar(A_TMP + 4096, LEVELS * 256).rearrange("p (n d i) -> p n d i", n=LEVELS, d=2)
        gm = ring[:, :, HW:SW].rearrange("p n (a m) -> p n a m", a=NP)
        mixed = ar(8192, 4096).rearrange("p (a n) -> p a n", a=NP)
        gt_b = ar(A_TMP, 4096).rearrange("p (a n) -> p a n", a=NP)
        gm_tmp = ar(12288, 2048)
        xres = ar(0, 4096).rearrange("p (a n) -> p a n", a=NP)
        xn2 = ar(4096, 4096).rearrange("p (a n) -> p a n", a=NP)
        h2 = xn2
        yacc = ar(8192, 4096).rearrange("p (a n) -> p a n", a=NP)
        yacc_b = ar(8192, 4096).rearrange("p (b n) -> p b n", b=8)
        hg = ar(12288, 2048).rearrange("p (k s) -> p k s", k=KT)
        oe = ar(14336, 2048)
        a_silu = ar(16384, 512)
        a_act = ar(16896, 512)
        aT = ar(17408, 512).rearrange("p (k s) -> p k s", k=4)
        onehot = ar(17920, 256).rearrange("p (a s) -> p a s", a=NP)
        onehot_c = ar(18176, 256).rearrange("p (a s) -> p a s", a=NP)
        ohT = ar(18432, 256).rearrange("p (a t) -> p a t", a=NP)
        gt2_b = ar(18688, 4096).rearrange("p (a n) -> p a n", a=NP)
        rt = ar(22784, 1400)
        nf_b = ar(12288, 2048)
        rt_at = [0]

        def router(*shape):
            n = int(np.prod(shape))
            rt_at[0] += n
            t = rt[:, rt_at[0] - n:rt_at[0]]
            return t.rearrange("p (a b) -> p a b", a=shape[0]) if len(shape) > 1 else t

        r_log = router(NP, NG + NE)
        r_gmax, r_tm, r_pg, r_m1, r_m2, r_e2, r_w1, r_w2 = (router(NP) for _ in range(8))
        r_t4, r_goh, r_ge = (router(NP, NG) for _ in range(3))
        r_les, r_les2, r_t8, r_oh1, r_oh2, r_c8, r_s8 = (router(NP, EG) for _ in range(7))
        r_big = router(NP, NE)
        r_mask = router(NP, NE)
        r_comb = router(NP, NE + 2)
        r_pos = router(NP, NE + 2)
        r_cnt = router(1)
        r_gt = router(3)
        n_slab = sb("n_slab", 1, dt=I32)

        x_dram = [x_prompt[0], x_sample[0]]
        row_q = gate_rows.rearrange("p a (h n) -> p (a h) n", h=2)
        ada_dram = w_ada[0].rearrange("(p k) n -> p k n", k=KT)
        in_dram = w_in[0].rearrange("(k p) n -> p k n", p=P)
        wo_dram = w_o[0].rearrange("(k p) n -> p k n", p=P)
        IN_COLS = [0, 1024, 2048, 3072, 4128, 5152, 6176]
        GM_COL = 7200

        block = ctx.enter_context(nc.Block())

        @block.sync
        def _(sp):
            def load(j, r, dst, src):
                if r > 0:
                    sp.wait_ge(slot_used[j], r)
                sp.dma_start(dst, src).then_inc(slot_full[j], 16)

            for s in range(2):
                for h in range(2):
                    for j in range(SLOTS):
                        load(j, 2 * s + h, ring[:, j, :], ada_dram[:, 8 * h + j, s * D:(s + 1) * D])
            for n, col in enumerate(IN_COLS):
                for j in range(SLOTS):
                    load(j, R_IN + n, ring[:, j, :].rearrange("p (k n) -> p k n", k=2),
                         in_dram[:, 2 * j:2 * j + 2, col:col + 1024])
            for n, sec in enumerate(BG_ADA):
                col = sec * D + HW * (n % 2)
                for h in range(2):
                    for j in range(SLOTS):
                        load(j, R_BG + 2 * n + h, ring[:, j, 0:HW], ada_dram[:, 8 * h + j, col:col + HW])
            for n in range(8):
                col = GM_COL + 512 * n
                for j in range(SLOTS):
                    load(j, R_GM + n, ring[:, j, 0:HW].rearrange("p (k n) -> p k n", k=2),
                         in_dram[:, 2 * j:2 * j + 2, col:col + 512])
            for r, w in ((R_UPA, w_up_a), (R_UPB, w_up_b)):
                for c in range(2):
                    for j in range(SLOTS):
                        load(j, r + c, ring[:, j, 0:HW], w[0, j * P:(j + 1) * P, c * HW:(c + 1) * HW])
            for c in range(2):
                for h in range(2):
                    for j in range(SLOTS):
                        load(j, R_O + 2 * c + h, ring[:, j, 0:HW], wo_dram[:, 8 * h + j, c * HW:(c + 1) * HW])
            sp.wait_ge(up_saved, 8)
            sp.wait_ge(rt_ready, 1)
            n_slabs = sp.value_load(n_slab[0:1, 0:1], min_val=1, max_val=MAX_SLABS)
            seen = sp.alloc_register("sp_seen")
            sp.reg_mov(seen, R_MOE)
            with sp.Fori(0, n_slabs):
                with sp.Fori(0, PAIRS) as i:
                    for part in range(3):
                        r = sp.snap(seen)
                        for j in range(SLOTS):
                            sp.wait_ge(slot_used[j], r)
                            if part < 2:
                                w = (w_e_gate, w_e_up)[part]
                                kq, e = j // 2, j % 2
                                src = w[0, bass.ds(i * 2 + e, 1), 512 * kq:512 * kq + 512, :].rearrange(
                                    "a (k p) n -> (a p) k n", p=P)
                                dst = ring[:, j, :].rearrange("p (k n) -> p k n", k=4)
                            else:
                                fk, e = j // 2, j % 2
                                src = w_e_down[0, bass.ds(i * 2 + e, 1), P * fk:P * fk + P, :].rearrange(
                                    "a p n -> (a p) n")
                                dst = ring[:, j, :]
                            sp.dma_start(dst, src).then_inc(slot_full[j], 16)
                        sp.reg_add(seen, seen, 1)
            sp.wait_ge(y_ready, 1)
            sp.dma_start(y_prompt[0], yacc[:, 0, :]).then_inc(y_out, 16)
            sp.wait_ge(y_ready, 2)
            sp.dma_start(y_sample[0], yacc[:, 1, :]).then_inc(y_out, 16)
            sp.wait_ge(y_out, 32)

        @block.tensor
        def _(pe):
            def full(j, r):
                pe.wait_ge(slot_full[j], 16 * (r + 1))

            def turn_norm(n):
                src = (xin, xn2)[n]
                for b in range(8):
                    for kk in range(2):
                        for p in range(NP):
                            last = pe.transpose(ps[:, b, (2 * kk + p) * P:(2 * kk + p + 1) * P],
                                                src[:, p, (2 * b + kk) * P:(2 * b + kk + 1) * P], ident)
                    last.then_inc(xn_turned, 1)

            pe.wait_ge(boot_in, 16 * 9)
            pe.transpose(ps[:, 7, 0:P], vec_rows, ident)
            pe.transpose(ps[:, 7, P:P + 72], conv_rows[0:72, :], ident[0:72, 0:72]).then_inc(vec_turned, 1)

            def turn_mod(s):
                pe.wait_ge(ada_saved, s + 1)
                for k in range(KT):
                    last = pe.matmul(ps[:, 4 * s, 2 * k:2 * k + 2], ada_rows[:, s, k * P:(k + 1) * P], sel2,
                                     start=True, stop=True)
                last.then_inc(mod_turned, 1)

            pe.wait_ge(silu_ready, 2)
            for s in range(2):
                if s == 1:
                    pe.wait_ge(vec_saved, 3)
                for q in range(4):
                    for j in range(4):
                        full((4 * q + j) % SLOTS, 2 * s + q // 2)
                    for n in range(4):
                        for j in range(4):
                            k = 4 * q + j
                            mm = pe.matmul(ps[32 * j:32 * j + 32, 4 * s + n, :], silu_cT[:, k, :],
                                           ring[:, k % SLOTS, n * 512:(n + 1) * 512], start=(q == 0), stop=(q == 3),
                                           tile_position=(0, 32 * j))
                            if n == 3:
                                mm.then_inc(slot_used[k % SLOTS], 1)
                if s == 1:
                    turn_mod(0)
            turn_mod(1)

            pe.wait_ge(mod_saved, 2)
            pe.wait_ge(ada_saved, 2)
            pe.wait_ge(xn_ready, 1)
            turn_norm(0)

            pe.wait_ge(hT_saved, 8)
            pe.wait_ge(small_in, 16 * 10)
            for p in range(NP):
                for k in range(KT):
                    mm = pe.matmul(ps[:, 7, 32 * p:32 * p + 32], hT[:, k, p * P:(p + 1) * P], w_ba[:, k, :],
                                   start=(k == 0), stop=(k == KT - 1))
            mm.then_inc(ba_done, 1)

            def in_group(n, r, turned):
                b0 = 4 * (n % 2)
                for j in range(SLOTS):
                    full(j, r)
                    w = ring[:, j, :].rearrange("p (k n) -> p k n", k=2)
                    for kk in range(2):
                        k = 2 * j + kk
                        if turned:
                            for m in range(8):
                                mm = pe.matmul(ps[:, b0 + m // 2, 256 * (m % 2):256 * (m % 2) + 256],
                                               w[:, kk, m * P:(m + 1) * P], hT[:, k, :],
                                               start=(k == 0 and m % 2 == 0), stop=(k == KT - 1),
                                               skip_group_check=True)
                        else:
                            for p in range(NP):
                                for h in range(2):
                                    mm = pe.matmul(ps[:, b0 + 2 * p + h, :], hT[:, k, p * P:(p + 1) * P],
                                                   w[:, kk, h * 512:(h + 1) * 512], start=(k == 0), stop=(k == KT - 1))
                    mm.then_inc(slot_used[j], 1)
                return mm

            for n in range(7):
                if n == 1:
                    pe.wait_ge(ba_saved, 1)
                if n >= 2:
                    pe.wait_ge(in_saved, n - 1)
                in_group(n, R_IN + n, n < 3)

            unit = [0]

            def stream(n):
                for u in range(unit[0], min(unit[0] + n, UNITS)):
                    grp, part = (u // 4, u % 4) if u < 32 else (8 + (u - 32) // 8, (u - 32) % 8)
                    b0 = 4 + 2 * (grp % 2)
                    if part == 0:
                        if grp == 0:
                            pe.wait_ge(in_saved, 6)
                        elif grp == 1:
                            pe.wait_ge(in_saved, 7)
                        else:
                            pe.wait_ge(bg_saved, grp - 1)
                        if 2 <= grp < 6:
                            pe.wait_ge(bg_kept, grp - 1)
                    if grp < 8:
                        for j in range(4):
                            full((4 * part + j) % SLOTS, R_BG + 2 * grp + part // 2)
                        for n2 in range(2):
                            for j in range(4):
                                k = 4 * part + j
                                mm = pe.matmul(ps[32 * j:32 * j + 32, b0 + n2, :], silu_cT[:, k, :],
                                               ring[:, k % SLOTS, n2 * 512:(n2 + 1) * 512], start=(part == 0),
                                               stop=(part == 3), tile_position=(0, 32 * j))
                                if n2 == 1:
                                    mm.then_inc(slot_used[k % SLOTS], 1)
                        if part == 2 and 1 <= grp < 5:
                            pe.wait_ge(bg_saved, grp)
                            for k in range(8):
                                mm = pe.matmul(ps[:, 4 + 2 * ((grp - 1) % 2), 2 * k:2 * k + 2],
                                               row_q[:, grp - 1, k * P:(k + 1) * P], sel2, start=True, stop=True)
                            mm.then_inc(bg_turned, 1)
                    else:
                        full(part, R_GM + grp - 8)
                        w = ring[:, part, 0:HW].rearrange("p (k n) -> p k n", k=2)
                        for kk in range(2):
                            for p in range(NP):
                                k = 2 * part + kk
                                mm = pe.matmul(ps[:, b0 + p, :], hT[:, k, p * P:(p + 1) * P], w[:, kk, :],
                                               start=(k == 0), stop=(k == KT - 1))
                        mm.then_inc(slot_used[part], 1)
                unit[0] += n

            stream(1)
            pe.wait_ge(in_saved, 7)
            for p in range(NP):
                if p == 1:
                    pe.wait_ge(rope_done, 2)
                    pe.wait_ge(at_in, 32)
                for h in range(H):
                    last = pe.transpose(ps[:, h // 4, (h % 4) * P:(h % 4 + 1) * P],
                                        qkvb[:, 0, p, h * P:(h + 1) * P], ident)
                last.then_inc(at_turned, 1)
                if p == 1:
                    pe.wait_ge(at_oT_saved, 1)
                for h in range(H):
                    last = pe.transpose(ps[:, 2 + h // 4, (h % 4) * P:(h % 4 + 1) * P],
                                        qkvb[:, 1, p, h * P:(h + 1) * P], ident)
                last.then_inc(at_turned, 1)
                stream(1)
                if p == 1:
                    pe.wait_ge(at_saved, 3)
                    for h in range(H):
                        last = pe.transpose(ps[:, h // 4, (h % 4) * P:(h % 4 + 1) * P], ck[:, h * P:(h + 1) * P], ident)
                    last.then_inc(at_turned, 1)
                    stream(1)
                pe.wait_ge(at_saved, 2 if p == 0 else 5)
                nk = 1 + p
                for r in range(nk):
                    if r == 1:
                        pe.wait_ge(at_cent, 2)
                    for h in range(H // nk * r, H // nk * (r + 1)):
                        for m in range(2):
                            rows = slice(64 * m, 64 * m + 64)
                            for s, keys in enumerate((kT,) if p == 0 else (kcT, kT)):
                                at = (h % (H // nk)) * nk * P + P * s
                                last = pe.matmul(ps[:, 2 * m + at // 512, at % 512:at % 512 + P], qT[rows, h, :],
                                                 keys[rows, h, :], start=True, stop=True)
                    last.then_inc(at_scores, 1)
                    stream(2)
                pe.wait_ge(at_prob, p + 1)
                pr = cent[:, 0:H * nk * P].rearrange("p (h k n) -> p h k n", h=H, n=P)
                for s in range(nk):
                    for h in range(H):
                        last = pe.transpose(ps[:, 2 * s + h // 4, (h % 4) * P:(h % 4 + 1) * P], pr[:, h, s, :], ident)
                last.then_inc(at_pT, 1)
                stream(1)
                pe.wait_ge(at_pT_saved, p + 1)
                for h in range(H):
                    for s in range(nk):
                        v = cv if (p == 1 and s == 0) else qkvb[:, 2, p, :]
                        last = pe.matmul(ps[:, h // 4, (h % 4) * P:(h % 4 + 1) * P], pT[:, s, h, :],
                                         v[:, h * P:(h + 1) * P], start=(s == 0), stop=(s == nk - 1))
                last.then_inc(at_o, 1)
                stream(3)
                pe.wait_ge(at_on, p + 1)
                for h in range(H):
                    last = pe.transpose(ps[:, 2 + h // 4, (h % 4) * P:(h % 4 + 1) * P], o_b[:, h * P:(h + 1) * P], ident)
                last.then_inc(at_oT, 1)
                stream(1)

            pe.wait_ge(l2_sq, 1)
            pe.wait_ge(at_oT_saved, 2)
            for r in range(2):
                if r == 1:
                    pe.wait_ge(l2_root, 1)
                for b in range(4):
                    last = pe.matmul(ps[:, b, :], ones, l2_buf[:, (4 * r + b) * 512:(4 * r + b + 1) * 512],
                                     start=True, stop=True)
                last.then_inc(l2_sum, 1)
                stream(1)
            pe.wait_ge(l2_root, 2)
            pe.wait_ge(bag_ready, 1)
            for p in range(NP):
                for d in range(2):
                    pe.matmul(ps[:, 0, 16 * p + 8 * d:16 * p + 8 * d + 8], U[d], g[:, p, 8 * d:8 * d + 8],
                              start=True, stop=True)
            pe.matmul(ps[:, 0, 32:48], ones, g[:, 0, :], start=True, stop=True).then_inc(gc_done, 1)
            stream(2)
            pe.wait_ge(l2_done, 1)
            pe.wait_ge(gc_saved, 1)

            def each_head(bank, lhs, rhs):
                for h in range(H):
                    mm = pe.matmul(ps[:, bank + h // 4, (h % 4) * P:(h % 4 + 1) * P], lhs(h), rhs(h),
                                   start=True, stop=True)
                return mm

            for p in range(NP):
                tok = slice(p * P, (p + 1) * P)
                kTh = lambda h: convT[:, H + h, tok]
                qTh = lambda h: convT[:, h, tok]
                if p == 1:
                    pe.wait_ge(dl_oTs, 1)
                for h in range(H):
                    last = pe.transpose(ps[:, h // 4, (h % 4) * P:(h % 4 + 1) * P], convT[:, 2 * H + h, tok], ident)
                if p == 0:
                    for h in range(H):
                        last = pe.transpose(ps[:, 2 + h // 4, (h % 4) * P:(h % 4 + 1) * P], kTh(h), ident)
                last.then_inc(tok_turned, 1)
                pe.wait_ge(tok_saved, p + 1)
                for d in range(2):
                    n = 2 * p + d
                    pe.wait_ge(dl_rhs, n + 1)
                    if n in (1, 2):
                        pe.wait_ge(dl_Ss, n)
                    for b in range(2):
                        mm = pe.matmul(ps[:, b, :], ones, At[:, 4 * b:4 * b + 4, :], start=True, stop=True)
                    mm.then_inc(dl_gcb, 1)
                    for b in range(2):
                        pe.matmul(ps[:, 2 + b, :], ones, Aqk[:, 4 * b:4 * b + 4, :], start=True, stop=True)
                    pe.wait_ge(dl_diff, n + 1)
                    each_head(0, kTh, kTh).then_inc(dl_gram, 1)
                    stream(1)
                    pe.wait_ge(dl_A, 2 * n + 1)
                    each_head(0, kTh, qTh).then_inc(dl_gram, 1)
                    if p == 1:
                        pe.wait_ge(dl_A, 2 * n + 1)
                        pe.wait_ge(s0_in, 16 * (d + 1))
                        each_head(2, kTh, lambda h: K_[:, h, :]).then_inc(dl_S0, 1)
                        pe.wait_ge(dl_A, 2 * n + 2)
                        each_head(0, qTh, lambda h: K_[:, h, :]).then_inc(dl_S0, 1)
                        stream(1)
                        pe.wait_ge(dl_S0r, 2 * d + 2)
                    else:
                        pe.wait_ge(dl_A, 2 * n + 2)
                    for lv in range(LEVELS):
                        pe.wait_ge(dl_M, LEVELS * n + lv + 1)
                        each_head(0, lambda h: M_[:, h, :], lambda h: ident if lv == 0 else T_[:, h, :]).then_inc(dl_X, 1)
                        if lv:
                            pe.wait_ge(dl_Xs, (LEVELS - 1) * n + lv)
                            if lv < LEVELS - 1:
                                each_head(2, lambda h: Tt[:, h, :], lambda h: X_[:, h, :])
                            each_head(0, lambda h: X_[:, h, :], lambda h: Tt[:, h, :]).then_inc(dl_Y, 1)
                        stream(1)
                    pe.wait_ge(dl_T, n + 1)
                    pe.wait_ge(dl_R, n + 1)
                    each_head(2, lambda h: Tt[:, h, :], lambda h: E_[:, h, :]).then_inc(dl_V, 1)
                    stream(1)
                    pe.wait_ge(dl_Vs, n + 1)
                    each_head(0, lambda h: Aqk[:, h, :], lambda h: M_[:, h, :]).then_inc(dl_O, 1)
                    if p == 0:
                        stream(1)
                        pe.wait_ge(dl_Vd, d + 1)
                        each_head(2, lambda h: K_[:, h, :], lambda h: X_[:, h, :]).then_inc(dl_S, 1)
                stream(2)
                pe.wait_ge(dl_on, p + 1)
                for h in range(H):
                    last = pe.transpose(ps[:, 2 + h // 4, (h % 4) * P:(h % 4 + 1) * P], O_[:, h, :], ident)
                last.then_inc(dl_oT, 1)

            def spread_gate(n, first, bank, done):
                for p in range(NP):
                    if first + p > 0:
                        pe.wait_ge(gt_saved, first + p)
                    for b in range(4):
                        last = pe.matmul(ps[:, bank + b, :], sel_row[p], gate_rows[:, n, b * 512:(b + 1) * 512],
                                         start=True, stop=True)
                    last.then_inc(done, 1)
                    stream(2)

            pe.wait_ge(dl_oTs, 2)
            pe.wait_ge(dl_Ss, 2)
            pe.wait_ge(bg_saved, 8)
            spread_gate(0, 0, 0, gt_done)
            stream(UNITS - unit[0])

            for br, r in ((0, R_UPA), (1, R_UPB)):
                src = (oaT, obT)[br]
                for c in range(2):
                    for p in range(NP):
                        if br == 0 and c == 0:
                            pe.wait_ge(gt_saved, 2)
                        elif br == 0:
                            pe.wait_ge(bg_saved, 16)
                        else:
                            pe.wait_ge(up_saved, 2 * c + p + 1)
                        for k in range(H):
                            if p == 0:
                                full(k, r + c)
                            for n in range(2):
                                mm = pe.matmul(ps[:, 4 * c + 2 * p + n, :], src[:, k, p * P:(p + 1) * P],
                                               ring[:, k, n * 512:(n + 1) * 512], start=(k == 0), stop=(k == H - 1))
                            if p == 1:
                                mm.then_inc(slot_used[k], 1)
                        if p == 0:
                            mm.then_inc(up_done, 1)
            pe.wait_ge(up_saved, 8)
            for b in range(8):
                for kk in range(2):
                    for p in range(NP):
                        last = pe.transpose(ps[:, b, (2 * kk + p) * P:(2 * kk + p + 1) * P],
                                            mixed[:, p, (2 * b + kk) * P:(2 * b + kk + 1) * P], ident)
            last.then_inc(mix_T, 1)

            pe.wait_ge(mix_Ts, 1)
            for c in range(2):
                for k in range(KT):
                    full(k % SLOTS, R_O + 2 * c + k // SLOTS)
                    for p in range(NP):
                        for n in range(2):
                            mm = pe.matmul(ps[:, 4 * c + 2 * p + n, :], hT[:, k, p * P:(p + 1) * P],
                                           ring[:, k % SLOTS, n * 512:(n + 1) * 512], start=(k == 0), stop=(k == KT - 1))
                    mm.then_inc(slot_used[k % SLOTS], 1)

            pe.wait_ge(xn_ready, 2)
            turn_norm(1)
            pe.wait_ge(hT_saved, 16)
            for p in range(NP):
                for k in range(KT):
                    last = pe.transpose(ps[:, 4 * p + k // 4, (k % 4) * P:(k % 4 + 1) * P],
                                        hT[:, k, p * P:(p + 1) * P], ident)
            last.then_inc(h2_T, 1)
            pe.wait_ge(h2_saved, 1)
            for p in range(NP):
                for k in range(KT):
                    last = pe.matmul(ps[:, 0, 36 * p:36 * p + 36], hT[:, k, p * P:(p + 1) * P], w_rt[:, k, :],
                                     start=(k == 0), stop=(k == KT - 1))
            last.then_inc(rt_done, 1)
            pe.wait_ge(rt_mask, 1)
            pe.matmul(ps[:, 1, 0:32], strict, r_mask[:, 0, :], start=True, stop=True)
            pe.matmul(ps[:, 1, 32:64], ones, r_mask[:, 0, :], start=True, stop=False)
            pe.matmul(ps[:, 1, 32:64], strict, r_mask[:, 1, :], start=False, stop=True)
            pe.matmul(ps[:, 1, 64:96], ones, r_mask[:, 0, :], start=True, stop=False)
            pe.matmul(ps[:, 1, 64:96], ones, r_mask[:, 1, :], start=False, stop=True).then_inc(rt_pos, 1)
            pe.wait_ge(rt_ready, 1)
            spread_gate(1, 2, 4, gt_done)
            pe.wait_ge(gt_saved, 4)
            n_slabs = pe.value_load(n_slab[0:1, 0:1], min_val=1, max_val=MAX_SLABS)
            seen = pe.alloc_register("pe_seen")
            turn = pe.alloc_register("pe_turn")
            pe.reg_mov(seen, 1)
            pe.reg_mov(turn, 1)

            def gather(half, t):
                if half == 0:
                    pe.wait_ge(mo_P, t)
                for k in range(8 * half, 8 * half + 8):
                    for p in range(NP):
                        mm = pe.matmul(ps[:, 3 + k // 4, (k % 4) * P:(k % 4 + 1) * P], h2[:, p, k * P:(k + 1) * P],
                                       onehot[:, p, :], start=(p == 0), stop=(p == 1))
                mm.then_inc(mo_gath, 1)

            def scatter(v):
                pe.wait_ge(mo_dns, v)
                pe.wait_ge(mo_PTs, v)
                for j in range(8):
                    if j >= 4:
                        pe.wait_ge(mo_ys, v * 8 + (j - 3))
                    pe.matmul(ps[:, 3 + j % 4, :], ohT[:, j // 4, :], oe[:, (j % 4) * 512:(j % 4 + 1) * 512],
                              start=True, stop=True).then_inc(mo_y, 1)

            def expand(part, v):
                for q in range(4):
                    for e in range(2):
                        pe.wait_ge(slot_full[2 * q + e], (v * 3 + (R_MOE - 3 + part + 1)) * 16)
                    for kk in range(4):
                        for e in range(2):
                            k = 4 * q + kk
                            mm = pe.matmul(ps[CAP * e:CAP * e + CAP, part, :], hg[:, k, CAP * e:CAP * e + CAP],
                                           ring[:, 2 * q + e, kk * 512:(kk + 1) * 512],
                                           start=(k == 0), stop=(k == KT - 1))
                            if kk == 3:
                                mm.then_inc(slot_used[2 * q + e], 1)

            with pe.Fori(0, n_slabs):
                t = pe.snap(turn)
                pe.wait_ge(mo_dns, pe.snap(seen))
                for half in range(2):
                    gather(half, t)
                pe.reg_add(turn, turn, 1)
                with pe.Fori(0, PAIRS):
                    v, t = pe.snap(seen), pe.snap(turn)
                    pe.wait_ge(mo_gaths, t * 2 - 2)
                    expand(0, v)
                    scatter(v)
                    for p in range(NP):
                        last = pe.transpose(ps[:, 7, p * P:(p + 1) * P], onehot_c[:, p, :], ident)
                    last.then_inc(mo_PT, 1)
                    expand(1, v)
                    pe.wait_ge(mo_ys, v * 8 + 8)
                    gather(0, t)
                    pe.wait_ge(mo_act, v)
                    for f in range(4):
                        last = pe.transpose(ps[:, 2, f * P:(f + 1) * P], a_act[:, f * P:(f + 1) * P], ident)
                    last.then_inc(mo_aT, 1)
                    gather(1, t)
                    pe.wait_ge(mo_aTs, v)
                    pe.wait_ge(mo_gaths, t * 2)
                    for f in range(4):
                        for e in range(2):
                            pe.wait_ge(slot_full[2 * f + e], (v * 3 + R_MOE) * 16)
                        for n in range(4):
                            for e in range(2):
                                mm = pe.matmul(ps[CAP * e:CAP * e + CAP, 3 + n, :], aT[:, f, CAP * e:CAP * e + CAP],
                                               ring[:, 2 * f + e, n * 512:(n + 1) * 512],
                                               start=(f == 0), stop=(f == 3))
                                if n == 3:
                                    mm.then_inc(slot_used[2 * f + e], 1)
                    pe.reg_add(seen, seen, 1)
                    pe.reg_add(turn, turn, 1)
            scatter(pe.snap(seen))

        @block.vector
        def _(dve):
            count = [0]

            def step(ins):
                ins.then_inc(dve_step, 1)
                count[0] += 1
                dve.wait_ge(dve_step, count[0])

            tt, ts, stt, red = dve.tensor_tensor, dve.tensor_scalar, dve.scalar_tensor_tensor, dve.tensor_reduce
            MUL, ADD, SUB, MAX, EQ = ALU.mult, ALU.add, ALU.subtract, ALU.max, ALU.is_equal
            roots = [0]

            def rsqrt_mean(ssq, out, n):
                w = ssq.shape[1]
                ts(ms[:, 0:w], ssq, 1.0 / n, EPS, MUL, ADD).then_inc(ms_ready, 1)
                roots[0] += 1
                dve.wait_ge(root_ready, roots[0])
                step(dve.reciprocal(out, rs[:, 0:w]))

            dve.memset(silu_cT[:, :, :], 0.0).then_inc(vec_saved, 1)
            dve.memset(eps[:, :], EPS).then_inc(vec_saved, 1)
            dve.wait_ge(vec_turned, 1)
            dve.tensor_copy(vecT[:, :], ps[:, 7, 0:P])
            dve.tensor_copy(cw[:, :, :], ps[:, 7, P:P + 72].rearrange("p (i m) -> p i m", i=3)).then_inc(vec_saved, 1)
            dve.wait_ge(ssq_ready, 2)
            rsqrt_mean(mx[:, 0:2], den[:, 0:2], D)
            for p in range(NP):
                last = ts(xin[:, p, :], xin[:, p, :], den[:, p:p + 1], None, MUL)
            last.then_inc(xn_ready, 1)

            for s in range(2):
                dve.wait_ge(mod_turned, s + 1)
                tt(mod[:, s, :, :], ps[:, 4 * s, 0:32].rearrange("p (k a) -> p k a", a=NP),
                   vecT[:, 16 * s:16 * s + 16].unsqueeze(2).to_broadcast([P, KT, NP]), ADD).then_inc(mod_saved, 1)
            dve.wait_ge(mod_saved, 2)

            def scaled_gain(n):
                gain = vecT[:, 96 + 16 * n:112 + 16 * n].unsqueeze(2).to_broadcast([P, KT, NP])
                step(stt(modA[:, n, :, :], mod[:, 3 * n + 1, :, :], 1.0, gain, ADD, MUL))

            scaled_gain(0)

            def modulate(n):
                for b in range(8):
                    out = hT[:, 2 * b:2 * b + 2, :].rearrange("p k (a t) -> p (k a) t", a=NP)
                    a = modA[:, n, 2 * b:2 * b + 2, :].rearrange("p k a -> p (k a)")
                    s = mod[:, 3 * n, 2 * b:2 * b + 2, :].rearrange("p k a -> p (k a)")
                    dve.wait_ge(xn_turned, 8 * n + b + 1)
                    step(tt(out, heads(ps[:, b, :]), per_head(a), MUL))
                    tt(out, out, per_head(s), ADD).then_inc(hT_saved, 1)

            modulate(0)

            dve.wait_ge(ba_done, 1)
            dve.tensor_copy(ba[:, :, :], ps[:, 7, 0:64].rearrange("p (a n) -> p a n", a=NP)).then_inc(ba_saved, 1)
            dve.wait_ge(ba_saved, 1)
            dve.wait_ge(small_in, 16 * 10)
            al = ba[:, :, 16:32]
            sp_ = sc[:, 1, 0:32].rearrange("p (a n) -> p a n", a=NP)
            sg_ = sc[:, 0, 0:32].rearrange("p (a n) -> p a n", a=NP)
            step(tt(al, al, over_heads(dtb[:, :], NP), ADD))
            step(tt(lamv[:, 0, :], lamv[:, 0, :], lamv[:, 1, :], MUL))
            step(tt(lamv[:, 2, :], lamv[:, 2, :], lamv[:, 3, :], MUL))
            step(red(lam_t[:, 0:1], lamv[:, 0, :], AX, ADD))
            step(red(lam_t[:, 1:2], lamv[:, 2, :], AX, ADD))
            step(ts(subln[:, :], subln[:, :], 1.0 - LAM_INIT, None, MUL))
            stt(sp_, al, -1.0, al, MUL, MAX).then_inc(bag_dve, 1)
            def conv(n):
                dve.wait_ge(conv_mid, n + 1)
                for m in range(8):
                    src = ps[:, 4 * (n % 2) + m // 2, 256 * (m % 2):256 * (m % 2) + 256].rearrange("p (a t) -> p a t", a=NP)
                    dst = convT[:, 8 * n + m, :].rearrange("p (a t) -> p a t", a=NP)
                    step(stt(dst[:, :, 1:P], src[:, :, 0:P - 1], cw[:, 0, 8 * n + m:8 * n + m + 1], dst[:, :, 1:P], MUL, ADD))
                    last = stt(dst[:, :, 0:P - 1], src[:, :, 1:P], cw[:, 2, 8 * n + m:8 * n + m + 1], dst[:, :, 0:P - 1], MUL, ADD)
                last.then_inc(in_saved, 1)

            for n in range(3):
                conv(n)
            dve.wait_ge(bag_exp, 1)
            step(ts(sc[:, :, 0:32], sc[:, :, 0:32], 1.0, None, ADD))
            step(tt(lam_t[:, 2:3], lam_t[:, 0:1], lam_t[:, 1:2], SUB))
            step(ts(lam_t[:, 2:3], lam_t[:, 2:3], LAM_INIT, None, ADD))
            dve.reciprocal(beta[:, :, :], sg_).then_inc(bag_dve, 1)
            dve.wait_ge(bag_exp, 2)
            step(stt(al, al, 0.0, sp_, MAX, ADD))
            step(stt(g[:, :, :], al, -1.0, over_heads(alog[:, :], NP), MUL, MUL))
            dve.tensor_copy(sc[:, 0, 32:33], g[:, 0, 0:1]).then_inc(bag_ready, 1)

            for p in range(NP):
                nk = 1 + p
                dve.wait_ge(in_saved, 7)
                if p == 1:
                    dve.wait_ge(at_pT, 1)
                    for s in range(2):
                        if s:
                            dve.wait_ge(rope_done, 1)
                        x = qkvb[:, s, 1, :]
                        x64 = x.rearrange("p (m d) -> p m d", d=64)
                        cos = over_heads(cst[:, C_COS:C_COS + 64], 16)
                        step(tt(rope_a.rearrange("p (m d) -> p m d", d=64), x64, cos, MUL))
                        x4 = x.rearrange("p (m f x n) -> p m f x n", m=16, f=2, x=2)
                        b4 = rope_b.rearrange("p (m f x n) -> p m f x n", m=16, f=2, x=2)
                        sn = cst[:, C_SIN:C_SIN + 64].rearrange("p (f x n) -> p f x n", f=2, x=2)
                        for h in range(2):
                            sin = sn[:, :, h, :].unsqueeze(1).to_broadcast([P, 16, 2, 16])
                            step(tt(b4[:, :, :, h, :], x4[:, :, :, 1 - h, :], sin, MUL))
                        tt(x, rope_a, rope_b, ADD).then_inc(rope_done, 1)
                K = nk * P
                hn = H // nk
                c5 = cent[:, 0:16 * K].rearrange("p (m h n) -> p m h n", m=2, h=H)
                mx3 = mx[:, 0:2 * hn].rearrange("p (m h) -> p m h", m=2)
                c4 = cent[:, 0:16 * K].rearrange("p (m n) -> p m n", m=16)
                for r in range(nk):
                    dve.wait_ge(at_scores, p + r + 1)
                    if r:
                        dve.wait_ge(at_cent, 2)
                    scores = banks(0, 4).rearrange("p (m h n) -> p m h n", m=2, n=K)
                    step(red(mx3, scores, AX, MAX))
                    tt(c5[:, :, hn * r:hn * (r + 1), :], scores, mx3.unsqueeze(3).to_broadcast([P, 2, hn, K]),
                       SUB).then_inc(at_cent, 1)
                dve.wait_ge(at_exp, p + 1)
                step(red(den[:, :], c4, AX, ADD))
                step(dve.reciprocal(den[:, :], den[:, :]))
                step(ts(den[:, 8:16], den[:, 8:16], lam_t[:, 2:3], None, MUL))
                step(tt(c4, c4, per_head(den[:, :], K), MUL))
                tt(c4[:, 0:8, :], c4[:, 0:8, :], c4[:, 8:16, :], SUB).then_inc(at_prob, 1)
                dve.wait_ge(at_o_saved, p + 1)
                step(tt(o_sq, o_b, o_b, MUL))
                step(red(mx[:, 0:8], heads(o_sq), AX, ADD))
                rsqrt_mean(mx[:, 0:8], den[:, 0:8], P)
                step(tt(heads(o_b), heads(o_b), per_head(den[:, 0:8]), MUL))
                tt(heads(o_b), heads(o_b), over_heads(subln[:, :]), MUL).then_inc(at_on, 1)

            dve.wait_ge(conv_done, 3)
            dve.wait_ge(at_scores, 3)
            dve.wait_ge(kv_out, 32)
            dve.wait_ge(at_oT, 2)
            tt(l2_buf, convT[:, 0:16, :].rearrange("p m t -> p (m t)"), convT[:, 0:16, :].rearrange("p m t -> p (m t)"),
               MUL).then_inc(l2_sq, 1)
            dve.wait_ge(l2_root, 2)
            step(dve.reciprocal(l2_buf, l2_buf))
            q2 = convT[:, 0:8, :].rearrange("p m t -> p (m t)")
            k2 = convT[:, 8:16, :].rearrange("p m t -> p (m t)")
            stt(q2, l2_buf[:, 0:2048], float(P) ** -0.5, q2, MUL, MUL)
            tt(k2, k2, l2_buf[:, 2048:4096], MUL).then_inc(l2_done, 1)
            dve.wait_ge(gc_done, 1)
            step(dve.tensor_copy(gc[:, :], ps[:, 0, 0:48]))
            tt(gc[:, 32:48], gc[:, 32:48], gc[:, 0:16], SUB).then_inc(gc_saved, 1)
            dve.wait_ge(gc_saved, 1)
            dve.wait_ge(gc_exp, 1)
            dve.wait_ge(lv_in, 16)
            for p in range(NP):
                for d in range(2):
                    n = 2 * p + d
                    hd = slice(8 * d, 8 * d + 8)
                    if n:
                        dve.wait_ge(dl_O, n)
                    if n in (1, 2):
                        dve.wait_ge(dl_S, n)
                    elif n == 0:
                        dve.wait_ge(l2_done, 1)
                    step(tt(At[:, :, :], over_heads(U[d]), per_head(g[:, p, hd]), MUL))
                    tt(Aqk[:, :, :], over_heads(ident), per_head(beta[:, p, hd]), MUL).then_inc(dl_rhs, 1)
                    dve.wait_ge(dl_gcb, n + 1)
                    gcp = gc[:, 16 * p + 8 * d:16 * p + 8 * d + 8]
                    step(tt(E_, heads(banks(0, 2)), per_head(gcp), SUB))
                    ts(E_, E_, 0.0, None, ALU.min).then_inc(dl_diff, 1)
                    dve.wait_ge(dl_dec, n + 1)
                    step(tt(E_, E_, over_heads(U[d]), MUL))
                    dve.wait_ge(dl_gram, 2 * n + 1)
                    step(tt(At, heads(banks(0, 2)), E_, MUL))
                    tt(At, At, heads(banks(2, 2)), MUL).then_inc(dl_A, 1)
                    dve.wait_ge(dl_gram, 2 * n + 2)
                    tt(Aqk, heads(banks(0, 2)), E_, MUL).then_inc(dl_A, 1)
                    dve.wait_ge(dl_A, 2 * n + 2)
                    if p == 0:
                        dve.wait_ge(tok_saved, 1)
                        tt(E_, V_, per_head(beta[:, p, hd]), MUL).then_inc(dl_R, 1)
                    else:
                        egcp = per_head(egc[:, 16 + 8 * d:24 + 8 * d])
                        dve.wait_ge(tok_saved, 2)
                        dve.wait_ge(dl_S0, 2 * d + 1)
                        tt(E_, heads(banks(2, 2)), egcp, MUL).then_inc(dl_S0r, 1)
                        dve.wait_ge(dl_S0r, 2 * d + 1)
                        step(tt(E_, V_, E_, SUB))
                        tt(E_, E_, per_head(beta[:, p, hd]), MUL).then_inc(dl_R, 1)
                        dve.wait_ge(dl_S0, 2 * d + 2)
                        if d == 0:
                            tt(O_, heads(banks(0, 2)), egcp, MUL).then_inc(dl_S0r, 1)
                        else:
                            step(tt(M_, heads(banks(0, 2)), egcp, MUL))
                            tt(O_, O_, M_, ADD).then_inc(dl_S0r, 1)
                        dve.wait_ge(dl_S0r, 2 * d + 2)
                    if n in (1, 2):
                        dve.wait_ge(st_out, 16 * n)
                    for lv in range(LEVELS):
                        tt(M_, At, over_heads(lvl[:, lv, d, :]), MUL).then_inc(dl_M, 1)
                        dve.wait_ge(dl_X, LEVELS * n + lv + 1)
                        if lv == 0:
                            dve.wait_ge(dl_M, LEVELS * n + 1)
                            tt(T_, over_heads(ident), heads(banks(0, 2)), SUB)
                            step(tt(Tt, over_heads(ident), M_, SUB))
                        else:
                            dve.wait_ge(dl_Y, (LEVELS - 1) * n + lv)
                            if lv < LEVELS - 1:
                                tt(T_, T_, heads(banks(2, 2)), SUB)
                                step(tt(Tt, Tt, heads(banks(0, 2)), SUB))
                            else:
                                tt(Tt, Tt, heads(banks(0, 2)), SUB).then_inc(dl_T, 1)
                    if p == 0:
                        dve.wait_ge(dl_Vs, n + 1)
                        tt(X_, M_, per_head(egl[:, hd]), MUL).then_inc(dl_Vd, 1)
                    dve.wait_ge(dl_O, n + 1)
                    if n == 0:
                        step(dve.tensor_copy(O_, heads(banks(0, 2))))
                    else:
                        step(tt(O_, O_, heads(banks(0, 2)), ADD))
                sq = E_
                step(tt(sq, O_, O_, MUL))
                step(red(mx[:, 0:8], sq, AX, ADD))
                rsqrt_mean(mx[:, 0:8], den[:, 0:8], P)
                step(tt(O_, O_, per_head(den[:, 0:8]), MUL))
                step(tt(O_, O_, over_heads(onorm[:, :]), MUL))
                tt(O_, O_, heads(gateS[:, p, :]), MUL).then_inc(dl_on, 1)
                if p == 0:
                    dve.wait_ge(dl_oT, 1)

            def spread(n, first, bank, dst):
                for p in range(NP):
                    dve.wait_ge(gt_done, first + p + 1)
                    dve.wait_ge(gt_in, 16 * (first + 2))
                    tt(dst[:, p, :], dst[:, p, :], banks(bank, 4), ADD).then_inc(gt_saved, 1)

            spread(0, 0, 0, gt_b)
            dve.wait_ge(bg_kept, 4)
            for s in (3, 4):
                step(tt(mod[:, s, :, :], mod[:, s, :, :],
                        vecT[:, 16 * s:16 * s + 16].unsqueeze(2).to_broadcast([P, KT, NP]), ADD))
            scaled_gain(1)
            dve.wait_ge(gm_ready, 1)
            for br in range(2):
                for c in range(2):
                    for p in range(NP):
                        if p == 0:
                            dve.wait_ge(up_done, 2 * br + c + 1)
                        else:
                            dve.wait_ge(round_done, R_UPA + 2 * br + c + 1)
                        up = banks(4 * c + 2 * p, 2).rearrange("p (s n) -> p s n", s=2)
                        mix = mixed[:, p, c * HW:(c + 1) * HW].rearrange("p (s n) -> p s n", s=2)
                        gates = gm[:, 4 * br + 2 * c:4 * br + 2 * c + 2, p, :]
                        if br == 0:
                            tt(mix, up, gates, MUL).then_inc(up_saved, 1)
                        else:
                            t = gm_tmp[:, 0:HW].rearrange("p (s n) -> p s n", s=2)
                            dve.wait_ge(up_saved, 4 + 2 * c + p)
                            step(tt(t, up, gates, MUL))
                            tt(mix, mix, t, ADD).then_inc(up_saved, 1)
            dve.wait_ge(gt_saved, 2)
            dve.wait_ge(x_in, 32)
            for c in range(2):
                dve.wait_ge(round_done, R_O + 2 * c + 2)
                for p in range(NP):
                    cols = slice(c * HW, (c + 1) * HW)
                    step(tt(gt_b[:, p, cols], banks(4 * c + 2 * p, 2), gt_b[:, p, cols], MUL))
                    tt(xres[:, p, cols], xres[:, p, cols], gt_b[:, p, cols], ADD).then_inc(x_saved, 1)
            dve.wait_ge(ssq_ready, 4)
            rsqrt_mean(mx[:, 0:2], den[:, 0:2], D)
            for p in range(NP):
                last = ts(xn2[:, p, :], xres[:, p, :], den[:, p:p + 1], None, MUL)
            last.then_inc(xn_ready, 1)
            modulate(1)

            dve.wait_ge(rt_done, 1)
            step(tt(r_log, ps[:, 0, 0:72].rearrange("p (a n) -> p a n", a=NP), over_heads(b_rt[:, :], NP), ADD))
            le = r_log[:, :, NG:].rearrange("p a (g e) -> p a g e", g=NG)
            gl = r_log[:, :, 0:NG]

            def first_max(out, vals, top, t, n):
                step(red(top, vals, AX, MAX))
                step(tt(t, vals, per_head(top, n), EQ))
                step(tt(t, t, over_heads(cst[:, C_TIE:C_TIE + n], NP), MUL))
                step(red(r_tm, t, AX, MAX))
                step(tt(out, t, per_head(r_tm, n), EQ))

            first_max(r_goh, gl, r_gmax, r_t4, NG)
            step(tt(r_ge, gl, per_head(r_gmax, NG), SUB))
            big4 = r_big.rearrange("p a (g e) -> p a g e", g=NG)
            step(tt(big4, le, r_goh.unsqueeze(3).to_broadcast([P, NP, NG, EG]), MUL))
            step(red(r_les, r_big.rearrange("p a (g e) -> p a e g", g=NG), AX, ADD))
            first_max(r_oh1, r_les, r_m1, r_t8, EG)
            step(stt(r_les2, r_oh1, -1e30, r_les, MUL, ADD))
            first_max(r_oh2, r_les2, r_m2, r_t8, EG)
            step(tt(r_s8, r_oh1, r_oh2, ADD))
            mask4 = r_mask.rearrange("p a (g e) -> p a g e", g=NG)
            goh4 = r_goh.unsqueeze(3).to_broadcast([P, NP, NG, EG])
            tt(mask4, goh4, r_s8.unsqueeze(2).to_broadcast([P, NP, NG, EG]), MUL).then_inc(rt_mask, 1)
            tt(r_e2, r_m2, r_m1, SUB).then_inc(rt_dve, 1)
            dve.wait_ge(rt_exp, 1)
            step(red(r_pg, r_ge, AX, ADD))
            step(ts(r_w1, r_e2, 1.0, None, ADD))
            step(tt(r_w1, r_w1, r_pg, MUL))
            step(dve.reciprocal(r_w1, r_w1))
            step(tt(r_w2, r_w1, r_e2, MUL))
            step(tt(r_c8, r_oh1, per_head(r_w1, EG), MUL))
            step(tt(r_t8, r_oh2, per_head(r_w2, EG), MUL))
            step(tt(r_c8, r_c8, r_t8, ADD))
            step(dve.memset(r_comb, 0.0))
            step(dve.memset(r_pos, 1024.0))
            step(tt(r_comb[:, :, 0:NE].rearrange("p a (g e) -> p a g e", g=NG), goh4,
                    r_c8.unsqueeze(2).to_broadcast([P, NP, NG, EG]), MUL))
            step(ts(r_big, r_mask, -1024.0, 1024.0, MUL, ADD))
            dve.wait_ge(rt_pos, 1)
            tt(r_pos[:, :, 0:NE], r_big, ps[:, 1, 0:64].rearrange("p (a n) -> p a n", a=NP), ADD).then_inc(places, 1)
            step(red(r_cnt, ps[:, 1, 64:96], AX, MAX))
            step(tt(r_gt, r_cnt.to_broadcast([P, 3]), cst[:, C_THR:C_THR + 3], ALU.is_gt))
            step(red(r_cnt, r_gt, AX, ADD))
            ts(n_slab[:, :], r_cnt, 1.0, None, ADD).then_inc(rt_ready, 1)
            for b in range(8):
                dve.memset(yacc_b[:, b, :], 0.0).then_inc(mo_ys, 1)
            dve.memset(ohT, 0.0).then_inc(mo_PTs, 1)
            dve.memset(oe, 0.0).then_inc(mo_dns, 1)
            gt2_flat = gt2_b.rearrange("p a n -> p (a n)")
            spread(1, 2, 4, gt2_b)
            dve.wait_ge(gt_saved, 4)
            dve.wait_ge(rt_ready, 1)
            n_slabs = dve.value_load(n_slab[0:1, 0:1], min_val=1, max_val=MAX_SLABS)
            seen = dve.alloc_register("dve_seen")
            turn = dve.alloc_register("dve_turn")
            dve.reg_mov(seen, 1)
            dve.reg_mov(turn, 1)
            oh4 = onehot.rearrange("p a (e s) -> p a e s", e=2)
            ohc4 = onehot_c.rearrange("p a (e s) -> p a e s", e=2)
            iota4 = cst[:, C_IOTA:C_IOTA + CAP].unsqueeze(1).unsqueeze(1).to_broadcast([P, NP, 2, CAP])

            def one_hots(at, t):
                pos4 = r_pos[:, :, bass.ds(at, 2)].unsqueeze(3).to_broadcast([P, NP, 2, CAP])
                comb4 = r_comb[:, :, bass.ds(at, 2)].unsqueeze(3).to_broadcast([P, NP, 2, CAP])
                tt(oh4, iota4, pos4, EQ).then_inc(mo_oh, 1)
                dve.wait_ge(mo_oh, t)
                tt(ohc4, oh4, comb4, MUL).then_inc(mo_P, 1)

            def gathered_back(v):
                dve.wait_ge(mo_ys, v * 8)
                for j in range(8):
                    dve.wait_ge(mo_y, v * 8 + (j - 7))
                    tt(yacc_b[:, j, :], yacc_b[:, j, :], ps[:, 3 + j % 4, :], ADD).then_inc(mo_ys, 1)

            with dve.Fori(0, n_slabs) as slab:
                t = dve.snap(turn)
                dve.wait_ge(places, slab + 1)
                one_hots(0, t)
                dve.reg_add(turn, turn, 1)
                with dve.Fori(0, PAIRS) as i:
                    v, t = dve.snap(seen), dve.snap(turn)
                    gathered_back(v)
                    dve.wait_ge(mo_PT, v)
                    one_hots(i * 2 + 2, t)
                    dve.wait_ge(mo_silu, v)
                    dve.wait_ge(round_done, v * 3 + (R_MOE - 1))
                    tt(a_act, a_silu, ps[:, 1, :], MUL).then_inc(mo_act, 1)
                    dve.reg_add(seen, seen, 1)
                    dve.reg_add(turn, turn, 1)
                t = dve.snap(turn)
                dve.wait_ge(mo_P, t - 1)
                dve.wait_ge(mo_gath, t * 2 - 2)
                ts(r_pos, r_pos, -float(CAP), None, ADD).then_inc(places, 1)
            v = dve.snap(seen)
            gathered_back(v)
            dve.wait_ge(mo_ys, v * 8 + 8)
            step(tt(yacc.rearrange("p a n -> p (a n)"), yacc.rearrange("p a n -> p (a n)"), gt2_flat, MUL))
            for p in range(NP):
                tt(xres[:, p, :], xres[:, p, :], yacc[:, p, :], ADD).then_inc(x_saved, 1)
            dve.wait_ge(ssq_ready, 6)
            rsqrt_mean(mx[:, 0:2], den[:, 0:2], D)
            dve.wait_ge(nf_in, 16)
            for p in range(NP):
                stt(yacc[:, p, :], xres[:, p, :], den[:, p:p + 1], nf_b, MUL, MUL).then_inc(y_ready, 1)

        @block.scalar
        def _(act):
            A = act.activation
            roots = [0]

            def root(w):
                roots[0] += 1
                act.wait_ge(ms_ready, roots[0])
                A(rs[:, 0:w], ms[:, 0:w], ACT.Sqrt).then_inc(root_ready, 1)

            def bcast(row):
                return row.partition_broadcast(P)

            act.dma_start(cst[:, :], consts).then_inc(boot_in, 16)
            for p, src in enumerate((c_ctx, c[0])):
                act.dma_start(cT[:, p, :], src.rearrange("(p k) -> p k", k=KT)).then_inc(boot_in, 16)
            act.dma_start(vec_rows[0:96, :], b_ada[0].rearrange("(r q) -> r q", q=P)).then_inc(boot_in, 16)
            act.dma_start(vec_rows[96:112, :], norm_mix[0].rearrange("(r q) -> r q", q=P)).then_inc(boot_in, 16)
            act.dma_start(vec_rows[112:128, :], norm_ffn[0].rearrange("(r q) -> r q", q=P)).then_inc(boot_in, 16)
            act.dma_start(conv_rows[0:72, :], conv_a[0].rearrange("i (m q) -> (i m) q", q=P)).then_inc(boot_in, 16)
            for p in range(NP):
                act.dma_start(xin[:, p, :], x_dram[p]).then_inc(boot_in, 16)
            act.dma_start(w_ba[:, :, :], in_dram[:, :, 4096:4128]).then_inc(small_in, 16)
            act.dma_start(w_rt[:, :, 0:NG], w_rg[0].rearrange("(k p) n -> p k n", p=P)).then_inc(small_in, 16)
            act.dma_start(w_rt[:, :, NG:], w_re[0].rearrange("(k p) n -> p k n", p=P)).then_inc(small_in, 16)
            for dst, src in ((alog[:, :], a_log[0].rearrange("a h -> (a h)")), (dtb[:, :], dt_bias[0].rearrange("a h -> (a h)")),
                             (lamv[:, :, :].rearrange("p a b -> p (a b)"), lam[0].rearrange("a h -> (a h)")),
                             (onorm[:, :], onorm_a[0]), (subln[:, :], subln_b[0]),
                             (b_rt[:, 0:NG], b_rg[0]), (b_rt[:, NG:], b_re[0])):
                act.dma_start(dst, bcast(src)).then_inc(small_in, 16)

            act.wait_ge(boot_in, 16 * 9)
            act.wait_ge(vec_saved, 1)
            for p in range(NP):
                A(silu_cT[:, :, p], cT[:, p, :], ACT.Silu).then_inc(silu_ready, 1)
            for p in range(NP):
                A(ar(8192 + 2048 * p, 2048), xin[:, p, :], ACT.Square, accum_out=mx[:, p:p + 1]).then_inc(ssq_ready, 1)
            root(2)
            for s in range(2):
                act.wait_ge(round_done, 2 * s + 2)
                A(ada_rows[:, s, :], banks(4 * s, 4), ACT.Copy).then_inc(ada_saved, 1)

            act.wait_ge(hT_saved, 8)
            act.dma_start(heads(cv), cache_v[0, 0].rearrange("h t d -> t h d")).then_inc(at_in, 16)
            act.wait_ge(vec_saved, 3)
            for n in range(3):
                act.wait_ge(round_done, R_IN + n + 1)
                for m in range(8):
                    last = A(convT[:, 8 * n + m, :], ps[:, 4 * (n % 2) + m // 2, 256 * (m % 2):256 * (m % 2) + 256],
                             ACT.Identity, scale=cw[:, 1, 8 * n + m:8 * n + m + 1])
                last.then_inc(conv_mid, 1)
                act.wait_ge(in_saved, n + 1)
                y = convT[:, 8 * n:8 * n + 8, :].rearrange("p m t -> p (m t)")
                A(y, y, ACT.Silu).then_inc(conv_done, 1)
            act.wait_ge(round_done, R_IN + 4)
            A(gateS.rearrange("p a n -> p (a n)"), banks(4, 4), ACT.Silu).then_inc(in_saved, 1)
            act.wait_ge(bag_dve, 1)
            A(sc[:, 0, 0:32].rearrange("p (a n) -> p a n", a=NP), ba[:, :, 0:16], ACT.Exp, scale=-1.0)
            A(sc[:, 1, 0:32], sc[:, 1, 0:32], ACT.Exp, scale=-1.0)
            A(alog[:, :], alog[:, :], ACT.Exp)
            A(lam_t[:, 0:2], lam_t[:, 0:2], ACT.Exp).then_inc(bag_exp, 1)
            act.wait_ge(bag_dve, 2)
            A(sc[:, 1, 0:32], sc[:, 1, 0:32], ACT.Ln).then_inc(bag_exp, 1)
            for n in range(4, 7):
                act.wait_ge(round_done, R_IN + n + 1)
                A(qkvb[:, n - 4, :, :].rearrange("p a n -> p (a n)"), banks(4 * (n % 2), 4), ACT.Copy).then_inc(in_saved, 1)
            act.wait_ge(in_saved, 7)
            act.dma_start(new_k[0, 0].rearrange("h t d -> t h d"), heads(qkvb[:, 1, 0, :])).then_inc(kv_out, 16)
            act.dma_start(new_v[0, 0].rearrange("h t d -> t h d"), heads(qkvb[:, 2, 0, :])).then_inc(kv_out, 16)

            unit = [0]

            def keep(n):
                for u in range(unit[0], min(unit[0] + n, UNITS)):
                    grp, part = (u // 4, u % 4) if u < 32 else (8 + (u - 32) // 8, (u - 32) % 8)
                    if grp < 8 and part == 2 and 1 <= grp < 5:
                        act.wait_ge(bg_turned, grp)
                        half = (grp - 1) % 2
                        A(mod[:, 3 + (grp - 1) // 2, 8 * half:8 * half + 8, :].rearrange("p k a -> p (k a)"),
                          ps[:, 4 + 2 * ((grp - 1) % 2), 0:16], ACT.Copy).then_inc(bg_kept, 1)
                    if grp < 8 and part == 3:
                        act.wait_ge(round_done, R_BG + 2 * grp + 2)
                        A(row_q[:, grp % 4, :], banks(4 + 2 * (grp % 2), 2), ACT.Copy).then_inc(bg_saved, 1)
                    elif grp >= 8 and part == 7:
                        act.wait_ge(round_done, R_GM + grp - 8 + 1)
                        A(ring[:, grp - 8, HW:SW], banks(4 + 2 * (grp % 2), 2), ACT.Copy).then_inc(bg_saved, 1)
                unit[0] += n

            keep(1)
            for p in range(NP):
                nk = 1 + p
                if p == 1:
                    act.wait_ge(at_on, 1)
                    act.dma_start(heads(ck), cache_k[0, 0].rearrange("h t d -> t h d")).then_inc(at_in, 16)
                t0 = 2 * p
                act.wait_ge(at_turned, t0 + 1)
                A(qT.rearrange("p h t -> p (h t)"), banks(0, 2), ACT.Copy).then_inc(at_saved, 1)
                act.wait_ge(at_turned, t0 + 2)
                A(kT.rearrange("p h t -> p (h t)"), banks(2, 2), ACT.Copy).then_inc(at_saved, 1)
                if p == 1:
                    act.wait_ge(at_turned, 5)
                    A(kcT.rearrange("p h t -> p (h t)"), banks(0, 2), ACT.Copy).then_inc(at_saved, 1)
                    keep(1)
                keep(1)
                act.wait_ge(at_cent, 1 + 2 * p)
                n = 16 * nk * P
                A(cent[:, 0:n], cent[:, 0:n], ACT.Exp, scale=64.0 ** -0.5).then_inc(at_exp, 1)
                keep(2 * nk)
                act.wait_ge(at_pT, p + 1)
                A(pT.rearrange("p k h q -> p (k h q)")[:, 0:1024 * nk], banks(0, 2 * nk), ACT.Copy).then_inc(at_pT_saved, 1)
                keep(1)
                act.wait_ge(at_o, p + 1)
                A(o_b, banks(0, 2), ACT.Copy).then_inc(at_o_saved, 1)
                root(8)
                keep(3)
                act.wait_ge(at_oT, p + 1)
                A(obT[:, :, p * P:(p + 1) * P], heads(banks(2, 2)), ACT.Copy).then_inc(at_oT_saved, 1)
                keep(1)

            act.dma_start(lvl.rearrange("p n d i -> p (n d i)"), level_masks).then_inc(lv_in, 16)
            for r in range(2):
                act.wait_ge(l2_sum, r + 1)
                A(l2_buf[:, 2048 * r:2048 * (r + 1)], banks(0, 4), ACT.Sqrt, bias=eps[:, :]).then_inc(l2_root, 1)
                keep(1)
            act.wait_ge(gc_saved, 1)
            A(egc[:, :], gc[:, 0:32], ACT.Exp)
            A(egl[:, :], gc[:, 32:48], ACT.Exp).then_inc(gc_exp, 1)
            keep(2)
            flat = lambda t: t.rearrange("p h t -> p (h t)")
            for p in range(NP):
                act.wait_ge(tok_turned, p + 1)
                if p == 0:
                    A(flat(K_), banks(2, 2), ACT.Copy)
                A(flat(V_), banks(0, 2), ACT.Copy).then_inc(tok_saved, 1)
                for d in range(2):
                    n = 2 * p + d
                    if p == 1:
                        act.wait_ge(*((dl_S, 2) if d == 0 else (dl_S0, 2)))
                        act.dma_start(K_, state_delta[0, 0, d].rearrange("h k v -> k h v")).then_inc(s0_in, 16)
                    act.wait_ge(dl_diff, n + 1)
                    A(flat(E_), flat(E_), ACT.Exp).then_inc(dl_dec, 1)
                    keep(1 + p)
                    for lv in range(LEVELS):
                        if lv:
                            act.wait_ge(dl_X, LEVELS * n + lv + 1)
                            A(flat(X_), banks(0, 2), ACT.Copy).then_inc(dl_Xs, 1)
                        keep(1)
                    act.wait_ge(dl_V, n + 1)
                    A(flat(M_), banks(2, 2), ACT.Copy).then_inc(dl_Vs, 1)
                    keep(1)
                    if p == 0:
                        keep(1)
                        act.wait_ge(dl_S, n + 1)
                        A(flat(T_), banks(2, 2), ACT.Copy).then_inc(dl_Ss, 1)
                        act.wait_ge(dl_Ss, n + 1)
                        act.dma_start(new_state[0, 0, d].rearrange("h k v -> k h v"), T_).then_inc(st_out, 16)
                root(8)
                keep(2)
                act.wait_ge(dl_oT, p + 1)
                A(oaT[:, :, p * P:(p + 1) * P], heads(banks(2, 2)), ACT.Copy).then_inc(dl_oTs, 1)

            def load_gate_bias(section, dst):
                for p in range(NP):
                    act.dma_start(dst[:, p, :], bcast(b_ada[0, section * D:(section + 1) * D])).then_inc(gt_in, 16)

            act.wait_ge(dl_on, 2)
            load_gate_bias(2, gt_b)
            for p in range(NP):
                act.dma_start(xres[:, p, :], x_dram[p]).then_inc(x_in, 16)
            keep(UNITS - unit[0])
            act.wait_ge(bg_saved, 16)
            A(ring[:, :, HW:SW], ring[:, :, HW:SW], ACT.Sigmoid).then_inc(gm_ready, 1)
            act.wait_ge(mix_T, 1)
            A(hT[:, :, :].rearrange("p k t -> p (k t)"), banks(0, 8), ACT.Copy).then_inc(mix_Ts, 1)
            for p in range(NP):
                act.wait_ge(x_saved, p + 3)
                A(yacc[:, p, :], xres[:, p, :], ACT.Square, accum_out=mx[:, p:p + 1]).then_inc(ssq_ready, 1)
            root(2)
            load_gate_bias(5, gt2_b)
            act.wait_ge(h2_T, 1)
            A(h2.rearrange("p a n -> p (a n)"), banks(0, 8), ACT.Copy).then_inc(h2_saved, 1)
            act.wait_ge(rt_dve, 1)
            A(r_ge, r_ge, ACT.Exp)
            A(r_e2, r_e2, ACT.Exp).then_inc(rt_exp, 1)
            act.wait_ge(rt_ready, 1)
            n_slabs = act.value_load(n_slab[0:1, 0:1], min_val=1, max_val=MAX_SLABS)
            seen = act.alloc_register("act_seen")
            turn = act.alloc_register("act_turn")
            act.reg_mov(seen, 1)
            act.reg_mov(turn, 1)

            def save_gathered(half, t):
                act.wait_ge(mo_gath, t * 2 + (half - 1))
                A(hg[:, 8 * half:8 * half + 8, :].rearrange("p k s -> p (k s)"), banks(3 + 2 * half, 2),
                  ACT.Copy).then_inc(mo_gaths, 1)

            with act.Fori(0, n_slabs):
                t = act.snap(turn)
                save_gathered(0, t)
                save_gathered(1, t)
                act.reg_add(turn, turn, 1)
                with act.Fori(0, PAIRS):
                    v, t = act.snap(seen), act.snap(turn)
                    act.wait_ge(round_done, v * 3 + (R_MOE - 2))
                    A(a_silu, ps[:, 0, :], ACT.Silu).then_inc(mo_silu, 1)
                    act.wait_ge(mo_PT, v)
                    A(ohT.rearrange("p a t -> p (a t)"), ps[:, 7, 0:256], ACT.Copy).then_inc(mo_PTs, 1)
                    save_gathered(0, t)
                    act.wait_ge(mo_aT, v)
                    A(aT.rearrange("p k s -> p (k s)"), ps[:, 2, :], ACT.Copy).then_inc(mo_aTs, 1)
                    save_gathered(1, t)
                    act.wait_ge(round_done, v * 3 + R_MOE)
                    A(oe, banks(3, 4), ACT.Copy).then_inc(mo_dns, 1)
                    act.reg_add(seen, seen, 1)
                    act.reg_add(turn, turn, 1)
            act.dma_start(nf_b, bcast(norm_final)).then_inc(nf_in, 16)
            for p in range(NP):
                act.wait_ge(x_saved, p + 5)
                A(h2[:, p, :], xres[:, p, :], ACT.Square, accum_out=mx[:, p:p + 1]).then_inc(ssq_ready, 1)
            root(2)


_INS = ['x_prompt', 'x_sample', 'c', 'state_delta', 'cache_k', 'cache_v', 'c_ctx', 'w_ada', 'b_ada', 'norm_mix',
        'norm_ffn', 'w_in', 'conv_a', 'a_log', 'dt_bias', 'onorm_a', 'lam', 'subln_b', 'w_up_a', 'w_up_b', 'w_o',
        'w_rg', 'b_rg', 'w_re', 'b_re', 'w_e_gate', 'w_e_up', 'w_e_down', 'norm_final']
_OUTS = [(1, P, D), (1, P, D), (1, 1, 2, H, P, P), (1, 1, H, P, P), (1, 1, H, P, P)]


def kernel(**inputs):
    import concourse.bacc as _bacc
    from concourse.bass_utils import run_bass_kernel_spmd as _run

    nc = _bacc.Bacc("TRN2", target_bir_lowering=False, num_devices=1)
    arrays, args = {}, []
    given = {name: np.ascontiguousarray(inputs[name]) for name in _INS}
    given["constants"], given["level_masks"] = constants()
    for name, a in given.items():
        arrays[f"in_{name}_dram"] = a
        args.append(nc.dram_tensor(f"in_{name}_dram", a.shape, mybir.dt.from_np(a.dtype), kind="ExternalInput").ap())
    for i, shape in enumerate(_OUTS):
        args.append(nc.dram_tensor(f"out_{i}_dram", shape, F32, kind="ExternalOutput").ap())
    program(nc, *args)
    r = _run(nc, [arrays], core_ids=[0])
    return tuple(r.results[0][f"out_{i}_dram"] for i in range(len(_OUTS)))
```

```python
from contextlib import ExitStack

import numpy as np
import concourse.bass as bass
from concourse import mybir

F32 = mybir.dt.float32
F32R = mybir.dt.float32r
I32 = mybir.dt.int32
ALU = mybir.AluOpType
ACT = mybir.ActivationFunctionType
AX = mybir.AxisListType.X

P = 128
NP = 2
D = 2048
KT = D // P
H = 8
HD = H * P
GW = 64
NG, EG = 4, 8
NE = NG * EG
FF = 512
EPS = 1e-6
LAM_INIT = 0.2
SLOTS = 8
SW = 2048
CAP = 64
PAIRS = NE // 2
MAX_SLABS = NP * P // CAP
LEVELS = 7

R_IN = 4
R_BG = R_IN + 7
ADA_HALVES = [3, 3, 4, 4, 2, 2, 5, 5]


def stream_items():
    items, r, count = [], R_BG, {"a": 0, "g": 0}
    for kind in "agagagagagagaagg":
        items.append((kind == "a", count[kind], r))
        count[kind] += 1
        r += 2 if kind == "a" else 1
    return items, r


STREAM, R_END = stream_items()
UNIT_LIST = [(n, part) for n, (is_ada, _, _) in enumerate(STREAM) for part in range(4 if is_ada else 8)]
UNITS = len(UNIT_LIST)
TURN_ITEMS = [min(n for n, item in enumerate(STREAM) if not item[0] and n > STREAM.index(last))
              for last in STREAM if last[0] and last[1] in (1, 3)]


def saved_count(is_ada, i):
    return [item[:2] for item in STREAM].index((is_ada, i)) + 1


R_UPA, R_UPB, R_O, R_MOE = R_END, R_END + 2, R_END + 4, R_END + 8
HW = SW // 2

C_ID, C_ONE, C_U, C_SU, C_IOTA, C_SEL, C_COS, C_SIN, C_TIE, C_THR, C_SEL2 = (
    0, 128, 256, 512, 640, 704, 960, 1024, 1088, 1096, 1099)
C_N = 1104
A_CONV, A_GATE, A_QB, A_OBT, A_OAT, A_TMP, A_N = 0, 6144, 8192, 14336, 16384, 18432, 24324


def constants():
    i = np.arange(P)
    c = np.zeros((P, C_N), np.float32)
    c[:, C_ID:C_ID + P] = np.eye(P)
    c[:, C_ONE:C_ONE + P] = 1.0
    c[:, C_U:C_U + P] = i[:, None] <= i[None]
    c[:, C_U + P:C_U + 2 * P] = i[:, None] >= i[None]
    c[:, C_SU:C_SU + P] = i[:, None] < i[None]
    c[:, C_IOTA:C_IOTA + CAP] = np.arange(CAP)
    for p in range(NP):
        c[p::32, C_SEL + p * P:C_SEL + (p + 1) * P] = 1.0
        c[p::32, C_SEL2 + p] = 1.0
    nf = 16
    inv = (10000.0 ** (-np.arange(nf, dtype=np.float32) / nf)).astype(np.float32)
    for half, pos in enumerate((i // GW, i % GW)):
        ang = pos.astype(np.float32)[:, None] * inv
        for x in range(2):
            at = half * 32 + x * 16
            c[:, C_COS + at:C_COS + at + nf] = np.cos(ang)
            c[:, C_SIN + at:C_SIN + at + nf] = np.sin(ang) * (-1 if x == 0 else 1)
    c[:, C_TIE:C_TIE + 8] = 8 - np.arange(8)
    c[:, C_THR:C_THR + 3] = CAP * np.arange(1, 4)
    lv = np.zeros((P, LEVELS, 2, P), np.float32)
    for n in range(LEVELS):
        s = 1 << n
        same = (i[:, None] // (2 * s)) == (i[None] // (2 * s))
        lo, hi = (i // s) % 2 == 0, (i // s) % 2 == 1
        lv[:, n, 0] = same & lo[:, None] & hi[None]
        lv[:, n, 1] = same & hi[:, None] & lo[None]
    return c, lv.reshape(P, -1)


def program(nc, x_prompt, x_sample, c, state_delta, cache_k, cache_v, c_ctx, w_ada, b_ada, norm_mix, norm_ffn,
            w_in, conv_a, a_log, dt_bias, onorm_a, lam, subln_b, w_up_a, w_up_b, w_o, w_rg, b_rg, w_re, b_re,
            w_e_gate, w_e_up, w_e_down, norm_final, consts, level_masks,
            y_prompt, y_sample, new_state, new_k, new_v):
    ctx = ExitStack()
    with ctx:
        sb = lambda name, *shape, dt=F32: ctx.enter_context(nc.sbuf_tensor(name, [P, *shape], dt))
        sem = lambda name: ctx.enter_context(nc.semaphore(name))

        ring = sb("ring", SLOTS, SW)
        with nc.sbuf_tensor("ob_hi", [P, H, NP * P], F32R) as ob_hi, nc.sbuf_tensor("ob_lo", [P, H, NP * P], F32R) as ob_lo:
            pass
        with nc.sbuf_tensor("mix_lo", [P, KT, NP * P], F32R) as mix_lo:
            pass
        hT = sb("hT", KT, NP * P)
        with nc.sbuf_tensor("w_hi", [P, 2, 1024], F32R) as w_hi, nc.sbuf_tensor("w_lo", [P, 2, 1024], F32R) as w_lo:
            pass
        gate_rows = sb("gate_rows", 2, D)
        cst = sb("cst", C_N)
        with nc.sbuf_tensor("arena_start", [P, A_OBT], F32), \
                nc.sbuf_tensor("hT_hi", [P, KT, NP * P], F32R) as hT_hi, \
                nc.sbuf_tensor("hT_lo", [P, KT, NP * P], F32R) as hT_lo:
            pass
        with nc.sbuf_tensor("oa_hi", [P, H, NP * P], F32R) as oa_hi, \
                nc.sbuf_tensor("oa_lo", [P, H, NP * P], F32R) as oa_lo, \
                nc.sbuf_tensor("wo_hi", [P, 2, HW], F32R) as wo_hi, nc.sbuf_tensor("wo_lo", [P, 2, HW], F32R) as wo_lo, \
                nc.sbuf_tensor("arena_mixed", [P, 4096], F32), \
                nc.sbuf_tensor("mix_hi", [P, KT, NP * P], F32R) as mix_hi:
            pass
        arena = sb("arena", A_N)
        silu_cT = sb("silu_cT", KT, 32)
        cT = sb("cT", NP, KT)
        vecT = sb("vecT", P)
        cw = sb("cw", 3, 24)
        mod = sb("mod", 6, KT, NP)
        modA = sb("modA", 2, KT, NP)
        w_ba = sb("w_ba", KT, 32)
        w_rt = sb("w_rt", KT, NG + NE)
        alog = sb("alog", 16)
        dtb = sb("dtb", 16)
        lamv = sb("lamv", 4, 64)
        onorm = sb("onorm", P)
        subln = sb("subln", P)
        b_rt = sb("b_rt", NG + NE)
        eps = sb("eps", 1)
        ba = sb("ba", NP, 32)
        sc = sb("sc", 2, 48)
        beta = sb("beta", NP, 16)
        g = sb("g", NP, 16)
        gc = sb("gc", 48)
        egc = sb("egc", 32)
        egl = sb("egl", 16)
        lam_t = sb("lam_t", 8)
        ms = sb("ms", 16)
        rs = sb("rs", 16)
        mx = sb("mx", 16)
        den = sb("den", 16)
        ps = ctx.enter_context(nc.psum_tensor("ps", [P, 8, 512], F32))

        ident = cst[:, C_ID:C_ID + P]
        ones = cst[:, C_ONE:C_ONE + P]
        U = [cst[:, C_U + d * P:C_U + (d + 1) * P] for d in range(2)]
        strict = cst[:, C_SU:C_SU + P]
        sel_row = [cst[:, C_SEL + p * P:C_SEL + (p + 1) * P] for p in range(NP)]
        sel2 = cst[:, C_SEL2:C_SEL2 + 2]

        def ar(at, n):
            return arena[:, at:at + n]

        def heads(ap):
            return ap.rearrange("p (h d) -> p h d", d=P)

        def per_head(ap, n=P):
            return ap.unsqueeze(2).to_broadcast([P, ap.shape[1], n])

        def over_heads(ap, m=H):
            return ap.unsqueeze(1).to_broadcast([P, m, ap.shape[1]])

        def banks(a, n):
            return ps[:, a:a + n, :].rearrange("p b n -> p (b n)")

        vec_rows = ar(4096, P)
        conv_rows = ar(4096 + P, P)
        xin = ar(A_TMP, 4096).rearrange("p (a d) -> p a d", a=NP)
        ada_rows = ar(0, 4096).rearrange("p (a d) -> p a d", a=2)
        convT = ar(A_CONV, 6144).rearrange("p (m t) -> p m t", t=NP * P)
        gateS = ar(A_GATE, 2048).rearrange("p (a n) -> p a n", a=NP)
        qkvb = ar(A_QB, 6144).rearrange("p (s a n) -> p s a n", s=3, a=NP)
        obT = ar(A_OBT, 2048).rearrange("p (h t) -> p h t", t=NP * P)
        oaT = ar(A_OAT, 2048).rearrange("p (h t) -> p h t", t=NP * P)

        slot_full = [sem(f"slot_full{j}") for j in range(SLOTS)]
        slot_used = [sem(f"slot_used{j}") for j in range(SLOTS)]
        round_done = slot_used[SLOTS - 1]
        boot_in = sem("boot_in")
        small_in = sem("small_in")
        vec_turned = sem("vec_turned")
        vec_saved = sem("vec_saved")
        silu_ready = sem("silu_ready")
        ada_saved = sem("ada_saved")
        mod_turned = sem("mod_turned")
        mod_saved = sem("mod_saved")
        ssq_ready = sem("ssq_ready")
        ms_ready = sem("ms_ready")
        root_ready = sem("root_ready")
        xn_ready = sem("xn_ready")
        xn_turned = sem("xn_turned")
        hT_even = sem("hT_even")
        hT_odd = sem("hT_odd")
        gain_ready = sem("gain_ready")
        hi_x = sem("hi_x")
        lo_x = sem("lo_x")
        hi_w = sem("hi_w")
        lo_w = sem("lo_w")
        even_used = sem("even_used")
        ba_done = sem("ba_done")
        ba_saved = sem("ba_saved")
        conv_mid = sem("conv_mid")
        in_saved = sem("in_saved")
        conv_done = sem("conv_done")
        dve_step = sem("dve_step")
        kv_out = sem("kv_out")
        bag_exp = sem("bag_exp")
        bag_dve = sem("bag_dve")
        bag_ready = sem("bag_ready")
        at_in = sem("at_in")
        rope_done = sem("rope_done")
        at_turned = sem("at_turned")
        at_saved = sem("at_saved")
        at_scores = sem("at_scores")
        at_cent = sem("at_cent")
        at_exp = sem("at_exp")
        at_prob = sem("at_prob")
        at_pT = sem("at_pT")
        at_pT_saved = sem("at_pT_saved")
        at_o = sem("at_o")
        at_o_saved = sem("at_o_saved")
        at_on = sem("at_on")
        at_oT = sem("at_oT")
        at_oT_saved = sem("at_oT_saved")
        l2_sq = sem("l2_sq")
        l2_sum = sem("l2_sum")
        l2_root = sem("l2_root")
        l2_diag = sem("l2_diag")
        l2_rep = sem("l2_rep")
        l2_done = sem("l2_done")
        gc_done = sem("gc_done")
        gc_saved = sem("gc_saved")
        gc_exp = sem("gc_exp")
        lv_in = sem("lv_in")
        tok_turned = sem("tok_turned")
        tok_saved = sem("tok_saved")
        s0_in = sem("s0_in")
        dl_rhs = sem("dl_rhs")
        dl_gcb = sem("dl_gcb")
        dl_gram = sem("dl_gram")
        dl_diff = sem("dl_diff")
        dl_dec = sem("dl_dec")
        dl_A = sem("dl_A")
        dl_M = sem("dl_M")
        dl_X = sem("dl_X")
        dl_Xs = sem("dl_Xs")
        dl_Y = sem("dl_Y")
        dl_Yt = sem("dl_Yt")
        dl_Tt = sem("dl_Tt")
        dl_T = sem("dl_T")
        dl_S0 = sem("dl_S0")
        dl_S0r = sem("dl_S0r")
        dl_R = sem("dl_R")
        dl_V = sem("dl_V")
        dl_Vs = sem("dl_Vs")
        dl_O = sem("dl_O")
        dl_Vd = sem("dl_Vd")
        dl_S = sem("dl_S")
        dl_Ss = sem("dl_Ss")
        st_out = sem("st_out")
        dl_on = sem("dl_on")
        dl_oT = sem("dl_oT")
        dl_oTs = sem("dl_oTs")
        bg_saved = sem("bg_saved")
        bg_turned = sem("bg_turned")
        bg_kept = sem("bg_kept")
        gm_ready = sem("gm_ready")
        up_saved = sem("up_saved")
        mix_T = sem("mix_T")
        src_hi = sem("src_hi")
        src_lo = sem("src_lo")
        mixed_hi = sem("mixed_hi")
        mixed_lo = sem("mixed_lo")
        gt_in = sem("gt_in")
        gt_done = sem("gt_done")
        gt_saved = sem("gt_saved")
        x_saved = sem("x_saved")
        x_in = sem("x_in")
        h2_T = sem("h2_T")
        h2_saved = sem("h2_saved")
        rt_done = sem("rt_done")
        rt_log = sem("rt_log")
        rt_exp = sem("rt_exp")
        rt_dve = sem("rt_dve")
        rt_mask = sem("rt_mask")
        rt_pos = sem("rt_pos")
        rt_ready = sem("rt_ready")
        places = sem("places")
        mo_oh = sem("mo_oh")
        mo_P = sem("mo_P")
        mo_gath = sem("mo_gath")
        mo_gaths = sem("mo_gaths")
        mo_PT = sem("mo_PT")
        mo_PTs = sem("mo_PTs")
        mo_silu = sem("mo_silu")
        mo_act = sem("mo_act")
        mo_aT = sem("mo_aT")
        mo_aTs = sem("mo_aTs")
        mo_dns = sem("mo_dns")
        mo_y = sem("mo_y")
        mo_ys = sem("mo_ys")
        nf_in = sem("nf_in")
        y_ready = sem("y_ready")
        y_out = sem("y_out")

        cent = ar(A_OAT, 4096)
        qT = heads(ar(A_OAT + 4096, 1024))
        kT = heads(ar(A_OAT + 5120, 1024))
        pT = ar(A_OAT + 4096, 2048).rearrange("p (k h q) -> p k h q", k=2, h=H)
        cv = ar(A_OAT + 6144, 1024)
        ck = ar(A_OAT + 2048, 1024)
        kcT = heads(ar(A_QB, 1024))
        rope_a = ar(A_OAT, 1024)
        rope_b = ar(A_OAT + 1024, 1024)
        o_b = ar(A_OAT + 3072, 1024)
        o_sq = ar(A_OAT + 2048, 1024)
        l2_buf = ar(A_QB, 4096)
        E_, Aqk, At, X_, T_, Tt = (heads(ar(A_QB + n * 1024, 1024)) for n in range(6))
        M_, V_, O_, K_ = (heads(ar(A_TMP + n * 1024, 1024)) for n in range(4))
        lvl = ar(A_TMP + 4096, LEVELS * 256).rearrange("p (n d i) -> p n d i", n=LEVELS, d=2)
        gm = ring[:, :, HW:SW].rearrange("p n (a m) -> p n a m", a=NP)
        mixed = ar(8192, 4096).rearrange("p (a n) -> p a n", a=NP)
        gt_b = ar(A_TMP, 4096).rearrange("p (a n) -> p a n", a=NP)
        gm_tmp = ar(22528, HW)
        xres = ar(0, 4096).rearrange("p (a n) -> p a n", a=NP)
        xn2 = ar(4096, 4096).rearrange("p (a n) -> p a n", a=NP)
        h2 = xn2
        gt2_b = ar(8192, 4096).rearrange("p (a n) -> p a n", a=NP)
        junk = ar(12288, 4096).rearrange("p (a n) -> p a n", a=NP)
        yacc = ar(18688, 4096).rearrange("p (a n) -> p a n", a=NP)
        yacc_b = ar(18688, 4096).rearrange("p (b n) -> p b n", b=8)
        hg = ar(12288, 2048).rearrange("p (k s) -> p k s", k=KT)
        oe = ar(14336, 2048)
        a_silu = ar(16384, 512)
        a_act = ar(16896, 512)
        aT = ar(17408, 512).rearrange("p (k s) -> p k s", k=4)
        onehot = ar(17920, 256).rearrange("p (a s) -> p a s", a=NP)
        onehot_c = ar(18176, 256).rearrange("p (a s) -> p a s", a=NP)
        ohT = ar(18432, 256).rearrange("p (a t) -> p a t", a=NP)
        rt = ar(22784, 1400)
        nf_b = ar(12288, 2048)
        rt_at = [0]

        def router(*shape):
            n = int(np.prod(shape))
            rt_at[0] += n
            t = rt[:, rt_at[0] - n:rt_at[0]]
            return t.rearrange("p (a b) -> p a b", a=shape[0]) if len(shape) > 1 else t

        r_log = router(NP, NG + NE)
        r_gmax, r_tm, r_pg, r_m1, r_m2, r_e2, r_w1, r_w2 = (router(NP) for _ in range(8))
        r_t4, r_goh, r_ge = (router(NP, NG) for _ in range(3))
        r_les, r_les2, r_t8, r_oh1, r_oh2, r_c8, r_s8 = (router(NP, EG) for _ in range(7))
        r_big = router(NP, NE)
        r_mask = router(NP, NE)
        r_comb = router(NP, NE + 2)
        r_pos = router(NP, NE + 2)
        r_cnt = router(1)
        r_gt = router(3)
        n_slab = sb("n_slab", 2, dt=I32)

        x_dram = [x_prompt[0], x_sample[0]]
        row_q = gate_rows.rearrange("p a (h n) -> p (a h) n", h=2)
        ada_dram = w_ada[0].rearrange("(p k) n -> p k n", k=KT)
        in_dram = w_in[0].rearrange("(k p) n -> p k n", p=P)
        wo_dram = w_o[0].rearrange("(k p) n -> p k n", p=P)
        IN_COLS = [0, 1024, 2048, 3072, 4128, 5152, 6176]
        GM_COL = 7200

        def modulated(n, b):
            return (hT_odd if b % 2 else hT_even), 4 * n + b // 2 + 1

        def split_piece(i):
            return i % SLOTS, R_UPA + i // SLOTS, 7 * KT + i + 1

        block = ctx.enter_context(nc.Block())

        @block.sync
        def _(sp):
            def load(j, r, dst, src):
                if r > 0:
                    sp.wait_ge(slot_used[j], r)
                sp.dma_start(dst, src).then_inc(slot_full[j], 16)

            for s in range(2):
                for h in range(2):
                    for j in range(SLOTS):
                        load(j, 2 * s + h, ring[:, j, :], ada_dram[:, 8 * h + j, s * D:(s + 1) * D])
            for n, col in enumerate(IN_COLS):
                for j in range(SLOTS):
                    load(j, R_IN + n, ring[:, j, :].rearrange("p (k n) -> p k n", k=2),
                         in_dram[:, 2 * j:2 * j + 2, col:col + 1024])

            def load_gates(g, r):
                col = GM_COL + 512 * g
                for j in range(SLOTS):
                    load(j, r, ring[:, j, 0:HW].rearrange("p (k n) -> p k n", k=2),
                         in_dram[:, 2 * j:2 * j + 2, col:col + 512])

            for is_ada, i, r in STREAM:
                if not is_ada:
                    load_gates(i, r)
                    continue
                col = ADA_HALVES[i] * D + HW * (i % 2)
                for h in range(2):
                    for j in range(SLOTS):
                        load(j, r + h, ring[:, j, 0:HW], ada_dram[:, 8 * h + j, col:col + HW])
            for r, w in ((R_UPA, w_up_a), (R_UPB, w_up_b)):
                for c in range(2):
                    for j in range(SLOTS):
                        load(j, r + c, ring[:, j, 0:HW], w[0, j * P:(j + 1) * P, c * HW:(c + 1) * HW])
            for c in range(2):
                for h in range(2):
                    for j in range(SLOTS):
                        load(j, R_O + 2 * c + h, ring[:, j, 0:HW], wo_dram[:, 8 * h + j, c * HW:(c + 1) * HW])
            sp.wait_ge(up_saved, 8)

            def expert_round(part, i, r):
                for j in range(SLOTS):
                    sp.wait_ge(slot_used[j], r)
                    q, e = j // 2, j % 2
                    one = bass.ds(i * 2 + e, 1)
                    if part < 2:
                        src = (w_e_gate, w_e_up)[part][0, one, 512 * q:512 * q + 512, :].rearrange(
                            "a (k p) n -> (a p) k n", p=P)
                        dst = ring[:, j, :].rearrange("p (k n) -> p k n", k=4)
                    else:
                        src = w_e_down[0, one, P * q:P * q + P, :].rearrange("a p n -> (a p) n")
                        dst = ring[:, j, :]
                    sp.dma_start(dst, src).then_inc(slot_full[j], 16)

            expert_round(0, 0, R_MOE)
            sp.wait_ge(rt_ready, 1)
            n_pairs = sp.value_load(n_slab[0:1, 1:2], min_val=PAIRS - 1, max_val=MAX_SLABS * PAIRS - 1)
            seen = sp.alloc_register("sp_seen")
            pair = sp.alloc_register("sp_pair")
            sp.reg_mov(seen, R_MOE + 1)
            sp.reg_mov(pair, 0)

            def next_round(part, i):
                expert_round(part, i, sp.snap(seen))
                sp.reg_add(seen, seen, 1)

            with sp.Fori(0, n_pairs):
                i = sp.snap(pair, min_val=0, max_val=PAIRS - 1)
                next_round(1, i)
                next_round(2, i)
                sp.reg_add(pair, pair, 1)
                sp.reg_alu(pair, pair, PAIRS - 1, op=ALU.bitwise_and)
                next_round(0, sp.snap(pair, min_val=0, max_val=PAIRS - 1))
            next_round(1, PAIRS - 1)
            next_round(2, PAIRS - 1)
            sp.wait_ge(y_ready, 1)
            sp.dma_start(y_prompt[0], yacc[:, 0, :]).then_inc(y_out, 16)
            sp.wait_ge(y_ready, 2)
            sp.dma_start(y_sample[0], yacc[:, 1, :]).then_inc(y_out, 16)
            sp.wait_ge(y_out, 32)

        @block.tensor
        def _(pe):
            def full(j, r):
                pe.wait_ge(slot_full[j], 16 * (r + 1))

            def turn_norm(n):
                src = (xin, xn2)[n]
                for b in range(8):
                    if n == 1 and b % 4 == 0:
                        pe.wait_ge(gt_saved, 3 + b // 4)
                    for kk in range(2):
                        for p in range(NP):
                            last = pe.transpose(ps[:, b, (2 * kk + p) * P:(2 * kk + p + 1) * P],
                                                src[:, p, (2 * b + kk) * P:(2 * b + kk + 1) * P], ident)
                    last.then_inc(xn_turned, 1)

            pe.wait_ge(boot_in, 16 * 9)
            pe.transpose(ps[:, 7, 0:P], vec_rows, ident)
            pe.transpose(ps[:, 7, P:P + 72], conv_rows[0:72, :], ident[0:72, 0:72]).then_inc(vec_turned, 1)

            def turn_mod(s):
                pe.wait_ge(ada_saved, s + 1)
                for k in range(KT):
                    last = pe.matmul(ps[:, 4 * s, 2 * k:2 * k + 2], ada_rows[:, s, k * P:(k + 1) * P], sel2,
                                     start=True, stop=True)
                last.then_inc(mod_turned, 1)

            pe.wait_ge(silu_ready, 2)
            for s in range(2):
                if s == 1:
                    pe.wait_ge(vec_saved, 3)
                for q in range(4):
                    for j in range(4):
                        full((4 * q + j) % SLOTS, 2 * s + q // 2)
                    for n in range(4):
                        for j in range(4):
                            k = 4 * q + j
                            mm = pe.matmul(ps[32 * j:32 * j + 32, 4 * s + n, :], silu_cT[:, k, :],
                                           ring[:, k % SLOTS, n * 512:(n + 1) * 512], start=(q == 0), stop=(q == 3),
                                           tile_position=(0, 32 * j))
                            if n == 3:
                                mm.then_inc(slot_used[k % SLOTS], 1)
                if s == 1:
                    turn_mod(0)
            turn_mod(1)

            pe.wait_ge(mod_saved, 2)
            pe.wait_ge(ada_saved, 2)
            pe.wait_ge(xn_ready, 1)
            turn_norm(0)

            def small_product(n, bank, w, width, done):
                pe.wait_ge(*modulated(n, bank))
                for k in range(KT):
                    if k % 2 == 0:
                        pe.wait_ge(*modulated(n, k // 2))
                    for p in range(NP):
                        mm = pe.matmul(ps[:, bank, width * p:width * (p + 1)], hT[:, k, p * P:(p + 1) * P], w[:, k, :],
                                       start=(k == 0 and p == 0), stop=(k == KT - 1), skip_group_check=True)
                mm.then_inc(done, 1)

            pe.wait_ge(small_in, 16 * 10)
            small_product(0, 4, w_ba, 32, ba_done)

            def in_group(n, turned):
                b0 = 4 * (n % 2)
                for j in range(SLOTS):
                    for kk in range(2):
                        k = 2 * j + kk
                        if n == 0 and kk == 0:
                            pe.wait_ge(lo_x, j + 1)
                        pe.wait_ge(hi_w, KT * n + k + 1)
                        terms = ((w_hi, hT_hi), (w_hi, hT_lo), (w_lo, hT_hi))
                        for t, (w, x) in enumerate(terms):
                            if t == 2:
                                pe.wait_ge(lo_w, KT * n + k + 1)
                            if turned:
                                for m in range(8):
                                    mm = pe.matmul(ps[:, b0 + m // 2, 256 * (m % 2):256 * (m % 2) + 256],
                                                   w[:, kk, m * P:(m + 1) * P], x[:, k, :],
                                                   start=(k == 0 and t == 0 and m % 2 == 0),
                                                   stop=(k == KT - 1 and t == 2), skip_group_check=True)
                            else:
                                for p in range(NP):
                                    for h in range(2):
                                        mm = pe.matmul(ps[:, b0 + 2 * p + h, :], x[:, k, p * P:(p + 1) * P],
                                                       w[:, kk, h * 512:(h + 1) * 512], start=(k == 0 and t == 0),
                                                       stop=(k == KT - 1 and t == 2))
                        if kk == 0:
                            mm.then_inc(even_used, 1)
                        else:
                            mm.then_inc(slot_used[j], 1)

            for n in range(7):
                if n == 1:
                    pe.wait_ge(ba_saved, 1)
                if n >= 2:
                    pe.wait_ge(in_saved, n - 1)
                in_group(n, n < 3)

            unit = [0]

            def stream(n):
                for item, part in UNIT_LIST[unit[0]:unit[0] + n]:
                    is_ada, _, r = STREAM[item]
                    b0 = 4 + 2 * (item % 2)
                    if part == 0:
                        if item < 2:
                            pe.wait_ge(in_saved, 6)
                        else:
                            pe.wait_ge(bg_saved, item - 1)
                        if item - 1 in TURN_ITEMS:
                            pe.wait_ge(bg_kept, TURN_ITEMS.index(item - 1) + 1)
                    if is_ada:
                        for j in range(4):
                            full((4 * part + j) % SLOTS, r + part // 2)
                        for n2 in range(2):
                            for j in range(4):
                                k = 4 * part + j
                                mm = pe.matmul(ps[32 * j:32 * j + 32, b0 + n2, :], silu_cT[:, k, :],
                                               ring[:, k % SLOTS, n2 * 512:(n2 + 1) * 512], start=(part == 0),
                                               stop=(part == 3), tile_position=(0, 32 * j))
                                if n2 == 1:
                                    mm.then_inc(slot_used[k % SLOTS], 1)
                        continue
                    if part == 4 and item in TURN_ITEMS:
                        pe.wait_ge(bg_saved, item)
                        for k in range(KT):
                            mm = pe.matmul(ps[:, 4 + 2 * ((item - 1) % 2), 2 * k:2 * k + 2],
                                           gate_rows[:, TURN_ITEMS.index(item), k * P:(k + 1) * P], sel2,
                                           start=True, stop=True)
                        mm.then_inc(bg_turned, 1)
                    full(part, r)
                    w = ring[:, part, 0:HW].rearrange("p (k n) -> p k n", k=2)
                    for kk in range(2):
                        for p in range(NP):
                            k = 2 * part + kk
                            mm = pe.matmul(ps[:, b0 + p, :], hT[:, k, p * P:(p + 1) * P], w[:, kk, :],
                                           start=(k == 0), stop=(k == KT - 1))
                    mm.then_inc(slot_used[part], 1)
                unit[0] += n

            stream(1)
            pe.wait_ge(in_saved, 7)
            for p in range(NP):
                if p == 1:
                    pe.wait_ge(rope_done, 2)
                    pe.wait_ge(at_in, 32)
                for h in range(H):
                    last = pe.transpose(ps[:, h // 4, (h % 4) * P:(h % 4 + 1) * P],
                                        qkvb[:, 0, p, h * P:(h + 1) * P], ident)
                last.then_inc(at_turned, 1)
                if p == 1:
                    pe.wait_ge(at_oT_saved, 1)
                for h in range(H):
                    last = pe.transpose(ps[:, 2 + h // 4, (h % 4) * P:(h % 4 + 1) * P],
                                        qkvb[:, 1, p, h * P:(h + 1) * P], ident)
                last.then_inc(at_turned, 1)
                stream(1)
                if p == 1:
                    pe.wait_ge(at_saved, 3)
                    for h in range(H):
                        last = pe.transpose(ps[:, h // 4, (h % 4) * P:(h % 4 + 1) * P], ck[:, h * P:(h + 1) * P], ident)
                    last.then_inc(at_turned, 1)
                    stream(1)
                pe.wait_ge(at_saved, 2 if p == 0 else 5)
                nk = 1 + p
                for r in range(nk):
                    if r == 1:
                        pe.wait_ge(at_cent, 2)
                    for h in range(H // nk * r, H // nk * (r + 1)):
                        for m in range(2):
                            rows = slice(64 * m, 64 * m + 64)
                            for s, keys in enumerate((kT,) if p == 0 else (kcT, kT)):
                                at = (h % (H // nk)) * nk * P + P * s
                                last = pe.matmul(ps[:, 2 * m + at // 512, at % 512:at % 512 + P], qT[rows, h, :],
                                                 keys[rows, h, :], start=True, stop=True)
                    last.then_inc(at_scores, 1)
                    stream(2)
                stream(1 + 3 * p)
                pe.wait_ge(at_prob, p + 1)
                pr = cent[:, 0:H * nk * P].rearrange("p (h k n) -> p h k n", h=H, n=P)
                for s in range(nk):
                    for h in range(H):
                        last = pe.transpose(ps[:, 2 * s + h // 4, (h % 4) * P:(h % 4 + 1) * P], pr[:, h, s, :], ident)
                last.then_inc(at_pT, 1)
                stream(1)
                pe.wait_ge(at_pT_saved, p + 1)
                for h in range(H):
                    for s in range(nk):
                        v = cv if (p == 1 and s == 0) else qkvb[:, 2, p, :]
                        last = pe.matmul(ps[:, h // 4, (h % 4) * P:(h % 4 + 1) * P], pT[:, s, h, :],
                                         v[:, h * P:(h + 1) * P], start=(s == 0), stop=(s == nk - 1))
                last.then_inc(at_o, 1)
                stream(3)
                pe.wait_ge(at_on, p + 1)
                for h in range(H):
                    last = pe.transpose(ps[:, 2 + h // 4, (h % 4) * P:(h % 4 + 1) * P], o_b[:, h * P:(h + 1) * P], ident)
                last.then_inc(at_oT, 1)
                stream(1)

            pe.wait_ge(at_oT_saved, 2)
            pe.wait_ge(bag_ready, 1)
            for p in range(NP):
                for d in range(2):
                    pe.matmul(ps[:, 3, 16 * p + 8 * d:16 * p + 8 * d + 8], U[d], g[:, p, 8 * d:8 * d + 8],
                              start=True, stop=True)
            pe.matmul(ps[:, 3, 32:48], ones, g[:, 0, :], start=True, stop=True).then_inc(gc_done, 1)
            pe.wait_ge(l2_sq, 2)
            for m in range(32):
                last = pe.matmul(ps[:, 2, m:m + 1], l2_buf[:, m * P:(m + 1) * P], ones[:, 0:1], start=True, stop=True)
            last.then_inc(l2_sum, 1)
            stream(2)
            pe.wait_ge(gc_saved, 1)
            for q in range(4):
                pe.wait_ge(l2_diag, q + 1)
                if q >= 2:
                    pe.wait_ge(l2_done, q - 1)
                for b in range(2):
                    last = pe.matmul(ps[:, 2 * (q % 2) + b, :], ones, l2_buf[:, 1024 * q + 512 * b:1024 * q + 512 * b + 512],
                                     start=True, stop=True)
                last.then_inc(l2_rep, 1)
                if q in (1, 3):
                    stream(1)
            pe.wait_ge(l2_done, 4)

            def each_head(bank, lhs, rhs):
                for h in range(H):
                    mm = pe.matmul(ps[:, bank + h // 4, (h % 4) * P:(h % 4 + 1) * P], lhs(h), rhs(h),
                                   start=True, stop=True)
                return mm

            for p in range(NP):
                tok = slice(p * P, (p + 1) * P)
                kTh = lambda h: convT[:, H + h, tok]
                qTh = lambda h: convT[:, h, tok]
                if p == 1:
                    pe.wait_ge(dl_oTs, 1)
                for h in range(H):
                    last = pe.transpose(ps[:, h // 4, (h % 4) * P:(h % 4 + 1) * P], convT[:, 2 * H + h, tok], ident)
                if p == 0:
                    for h in range(H):
                        last = pe.transpose(ps[:, 2 + h // 4, (h % 4) * P:(h % 4 + 1) * P], kTh(h), ident)
                last.then_inc(tok_turned, 1)
                pe.wait_ge(tok_saved, p + 1)
                for d in range(2):
                    n = 2 * p + d
                    if n:
                        stream(1)
                    pe.wait_ge(dl_rhs, n + 1)
                    if n in (1, 2):
                        pe.wait_ge(dl_Ss, n)
                    for b in range(2):
                        mm = pe.matmul(ps[:, b, :], ones, At[:, 4 * b:4 * b + 4, :], start=True, stop=True)
                    mm.then_inc(dl_gcb, 1)
                    for b in range(2):
                        pe.matmul(ps[:, 2 + b, :], ones, Aqk[:, 4 * b:4 * b + 4, :], start=True, stop=True)
                    pe.wait_ge(dl_diff, n + 1)
                    each_head(0, kTh, kTh).then_inc(dl_gram, 1)
                    stream(1)
                    pe.wait_ge(dl_A, 2 * n + 1)
                    each_head(0, kTh, qTh).then_inc(dl_gram, 1)
                    if p == 1:
                        pe.wait_ge(dl_A, 2 * n + 1)
                        pe.wait_ge(s0_in, 16 * (d + 1))
                        each_head(2, kTh, lambda h: K_[:, h, :]).then_inc(dl_S0, 1)
                        pe.wait_ge(dl_A, 2 * n + 2)
                        each_head(0, qTh, lambda h: K_[:, h, :]).then_inc(dl_S0, 1)
                        stream(2)
                        pe.wait_ge(dl_S0r, 2 * d + 2)
                    else:
                        stream(1)
                        pe.wait_ge(dl_A, 2 * n + 2)
                    for lv in range(LEVELS):
                        pe.wait_ge(dl_M, LEVELS * n + lv + 1)
                        if lv:
                            pe.wait_ge(dl_T, (LEVELS - 1) * n + lv)
                        each_head(0, lambda h: M_[:, h, :], lambda h: ident if lv == 0 else T_[:, h, :]).then_inc(dl_X, 1)
                        stream(1)
                        if lv:
                            pe.wait_ge(dl_Xs, (LEVELS - 1) * n + lv)
                            pe.wait_ge(dl_Tt, LEVELS * n + lv)
                            if lv < LEVELS - 1:
                                each_head(0, lambda h: Tt[:, h, :], lambda h: X_[:, h, :]).then_inc(dl_Y, 1)
                            each_head(2, lambda h: X_[:, h, :], lambda h: Tt[:, h, :]).then_inc(dl_Yt, 1)
                    pe.wait_ge(dl_Tt, LEVELS * (n + 1))
                    pe.wait_ge(dl_R, n + 1)
                    each_head(2, lambda h: Tt[:, h, :], lambda h: E_[:, h, :]).then_inc(dl_V, 1)
                    stream(1)
                    pe.wait_ge(dl_Vs, n + 1)
                    each_head(0, lambda h: Aqk[:, h, :], lambda h: M_[:, h, :]).then_inc(dl_O, 1)
                    if p == 0:
                        stream(1)
                        pe.wait_ge(dl_Vd, d + 1)
                        each_head(2, lambda h: K_[:, h, :], lambda h: X_[:, h, :]).then_inc(dl_S, 1)
                stream(2)
                pe.wait_ge(dl_on, p + 1)
                for h in range(H):
                    last = pe.transpose(ps[:, 2 + h // 4, (h % 4) * P:(h % 4 + 1) * P], O_[:, h, :], ident)
                last.then_inc(dl_oT, 1)

            pe.wait_ge(dl_oTs, 2)
            pe.wait_ge(dl_Ss, 2)
            assert unit[0] > UNIT_LIST.index((saved_count(True, 5) - 1, 3))
            pe.wait_ge(bg_saved, saved_count(True, 5))
            for p in range(NP):
                if p == 1:
                    pe.wait_ge(gt_saved, 1)
                for b in range(4):
                    last = pe.matmul(ps[:, b, :], sel_row[p], gate_rows[:, 0, b * 512:(b + 1) * 512],
                                     start=True, stop=True)
                last.then_inc(gt_done, 1)
                stream(2)
            stream(max(0, UNITS - unit[0]))

            def split_product(i, k, last_k, c, hi, lo):
                slot, _, count = split_piece(i)
                pe.wait_ge(hi_w, count)
                for t, (x, w) in enumerate(((hi, wo_hi), (lo, wo_hi), (hi, wo_lo))):
                    if t == 2:
                        pe.wait_ge(lo_w, count)
                    for p in range(NP):
                        for n in range(2):
                            mm = pe.matmul(ps[:, 4 * c + 2 * p + n, :], x[:, k, p * P:(p + 1) * P],
                                           w[:, i % 2, n * 512:(n + 1) * 512], start=(k == 0 and t == 0),
                                           stop=(k == last_k and t == 2))
                mm.then_inc(slot_used[slot], 1)

            for br in range(2):
                hi, lo = ((oa_hi, oa_lo), (ob_hi, ob_lo))[br]
                pe.wait_ge(src_lo, br + 1)
                for c in range(2):
                    if br == 1:
                        pe.wait_ge(up_saved, 2 * c + 2)
                    elif c == 0:
                        pe.wait_ge(gt_saved, 2)
                    else:
                        pe.wait_ge(bg_saved, len(STREAM))
                    for k in range(H):
                        split_product(16 * br + 8 * c + k, k, H - 1, c, hi, lo)
            for b in range(8):
                if b % 4 == 0:
                    pe.wait_ge(up_saved, 6 + b // 2)
                for kk in range(2):
                    for p in range(NP):
                        last = pe.transpose(ps[:, b, (2 * kk + p) * P:(2 * kk + p + 1) * P],
                                            mixed[:, p, (2 * b + kk) * P:(2 * b + kk + 1) * P], ident)
                last.then_inc(mix_T, 1)
            for c in range(2):
                pe.wait_ge(mixed_lo, 4 * c + 4)
                for k in range(KT):
                    if c == 0 and k >= 8 and k % 2 == 0:
                        pe.wait_ge(mixed_lo, k // 2 + 1)
                    split_product(32 + 16 * c + k, k, KT - 1, c, mix_hi, mix_lo)

            for p in range(NP):
                pe.wait_ge(x_saved, 2 * p + 2)
                for b in range(4):
                    last = pe.matmul(ps[:, 4 * p + b, :], sel_row[p], gate_rows[:, 1, b * 512:(b + 1) * 512],
                                     start=True, stop=True)
                last.then_inc(gt_done, 1)

            pe.wait_ge(xn_ready, 2)
            turn_norm(1)
            small_product(1, 0, w_rt, NG + NE, rt_done)
            for p in (1, 0):
                if p == 0:
                    pe.wait_ge(rt_log, 1)
                for k in range(KT):
                    last = pe.transpose(ps[:, 4 * p + k // 4, (k % 4) * P:(k % 4 + 1) * P],
                                        hT[:, k, p * P:(p + 1) * P], ident)
                last.then_inc(h2_T, 1)
            pe.wait_ge(h2_saved, 1)
            pe.wait_ge(rt_mask, 1)
            pe.matmul(ps[:, 4, 0:32], strict, r_mask[:, 0, :], start=True, stop=True)
            pe.matmul(ps[:, 4, 32:64], ones, r_mask[:, 0, :], start=True, stop=False)
            pe.matmul(ps[:, 4, 32:64], strict, r_mask[:, 1, :], start=False, stop=True)
            pe.matmul(ps[:, 4, 64:96], ones, r_mask[:, 0, :], start=True, stop=False)
            pe.matmul(ps[:, 4, 64:96], ones, r_mask[:, 1, :], start=False, stop=True).then_inc(rt_pos, 1)
            pe.wait_ge(rt_ready, 1)
            pe.wait_ge(h2_saved, 2)
            n_slabs = pe.value_load(n_slab[0:1, 0:1], min_val=1, max_val=MAX_SLABS)
            seen = pe.alloc_register("pe_seen")
            turn = pe.alloc_register("pe_turn")
            pe.reg_mov(seen, 1)
            pe.reg_mov(turn, 1)

            def gather(half, t):
                if half == 0:
                    pe.wait_ge(mo_P, t)
                for k in range(8 * half, 8 * half + 8):
                    for p in range(NP):
                        mm = pe.matmul(ps[:, 3 + k // 4, (k % 4) * P:(k % 4 + 1) * P], h2[:, p, k * P:(k + 1) * P],
                                       onehot[:, p, :], start=(p == 0), stop=(p == 1))
                mm.then_inc(mo_gath, 1)

            def scatter(v):
                pe.wait_ge(mo_dns, v)
                pe.wait_ge(mo_PTs, v)
                for j in range(8):
                    if j >= 4:
                        pe.wait_ge(mo_ys, v * 8 + (j - 3))
                    pe.matmul(ps[:, 3 + j % 4, :], ohT[:, j // 4, :], oe[:, (j % 4) * 512:(j % 4 + 1) * 512],
                              start=True, stop=True).then_inc(mo_y, 1)

            def expand(part, v):
                for q in range(4):
                    for e in range(2):
                        pe.wait_ge(slot_full[2 * q + e], (v * 3 + (R_MOE - 3 + part + 1)) * 16)
                    for kk in range(4):
                        for e in range(2):
                            k = 4 * q + kk
                            mm = pe.matmul(ps[CAP * e:CAP * e + CAP, part, :], hg[:, k, CAP * e:CAP * e + CAP],
                                           ring[:, 2 * q + e, kk * 512:(kk + 1) * 512],
                                           start=(k == 0), stop=(k == KT - 1))
                            if kk == 3:
                                mm.then_inc(slot_used[2 * q + e], 1)

            with pe.Fori(0, n_slabs):
                t = pe.snap(turn)
                pe.wait_ge(mo_dns, pe.snap(seen))
                for half in range(2):
                    gather(half, t)
                pe.reg_add(turn, turn, 1)
                with pe.Fori(0, PAIRS):
                    v, t = pe.snap(seen), pe.snap(turn)
                    pe.wait_ge(mo_gaths, t * 2 - 2)
                    expand(0, v)
                    scatter(v)
                    for p in range(NP):
                        last = pe.transpose(ps[:, 7, p * P:(p + 1) * P], onehot_c[:, p, :], ident)
                    last.then_inc(mo_PT, 1)
                    expand(1, v)
                    pe.wait_ge(mo_ys, v * 8 + 8)
                    gather(0, t)
                    pe.wait_ge(mo_act, v)
                    for f in range(4):
                        last = pe.transpose(ps[:, 2, f * P:(f + 1) * P], a_act[:, f * P:(f + 1) * P], ident)
                    last.then_inc(mo_aT, 1)
                    gather(1, t)
                    pe.wait_ge(mo_aTs, v)
                    pe.wait_ge(mo_gaths, t * 2)
                    for f in range(4):
                        for e in range(2):
                            pe.wait_ge(slot_full[2 * f + e], (v * 3 + R_MOE) * 16)
                        for n in range(4):
                            for e in range(2):
                                mm = pe.matmul(ps[CAP * e:CAP * e + CAP, 3 + n, :], aT[:, f, CAP * e:CAP * e + CAP],
                                               ring[:, 2 * f + e, n * 512:(n + 1) * 512],
                                               start=(f == 0), stop=(f == 3))
                                if n == 3:
                                    mm.then_inc(slot_used[2 * f + e], 1)
                    pe.reg_add(seen, seen, 1)
                    pe.reg_add(turn, turn, 1)
            scatter(pe.snap(seen))

        @block.vector
        def _(dve):
            count = [0]

            def step(ins):
                ins.then_inc(dve_step, 1)
                count[0] += 1
                dve.wait_ge(dve_step, count[0])

            tt, ts, stt, red = dve.tensor_tensor, dve.tensor_scalar, dve.scalar_tensor_tensor, dve.tensor_reduce
            MUL, ADD, SUB, MAX, EQ = ALU.mult, ALU.add, ALU.subtract, ALU.max, ALU.is_equal
            roots = [0]

            def rsqrt_mean(ssq, out, n):
                w = ssq.shape[1]
                ts(ms[:, 0:w], ssq, 1.0 / n, EPS, MUL, ADD).then_inc(ms_ready, 1)
                roots[0] += 1
                dve.wait_ge(root_ready, roots[0])
                step(dve.reciprocal(out, rs[:, 0:w]))

            dve.memset(silu_cT[:, :, :], 0.0).then_inc(vec_saved, 1)
            dve.memset(eps[:, :], EPS).then_inc(vec_saved, 1)
            dve.wait_ge(vec_turned, 1)
            dve.tensor_copy(vecT[:, :], ps[:, 7, 0:P])
            dve.tensor_copy(cw[:, :, :], ps[:, 7, P:P + 72].rearrange("p (i m) -> p i m", i=3)).then_inc(vec_saved, 1)
            dve.wait_ge(ssq_ready, 2)
            rsqrt_mean(mx[:, 0:2], den[:, 0:2], D)
            for p in range(NP):
                last = ts(xin[:, p, :], xin[:, p, :], den[:, p:p + 1], None, MUL)
            last.then_inc(xn_ready, 1)

            for s in range(2):
                dve.wait_ge(mod_turned, s + 1)
                tt(mod[:, s, :, :], ps[:, 4 * s, 0:32].rearrange("p (k a) -> p k a", a=NP),
                   vecT[:, 16 * s:16 * s + 16].unsqueeze(2).to_broadcast([P, KT, NP]), ADD).then_inc(mod_saved, 1)
            dve.wait_ge(mod_saved, 2)

            def scaled_gain(n):
                gain = vecT[:, 96 + 16 * n:112 + 16 * n].unsqueeze(2).to_broadcast([P, KT, NP])
                stt(modA[:, n, :, :], mod[:, 3 * n + 1, :, :], 1.0, gain, ADD, MUL).then_inc(gain_ready, 1)
                dve.wait_ge(gain_ready, n + 1)

            scaled_gain(0)

            def modulate(n):
                for b in range(0, 8, 2):
                    out = hT[:, 2 * b:2 * b + 2, :].rearrange("p k (a t) -> p (k a) t", a=NP)
                    a = modA[:, n, 2 * b:2 * b + 2, :].rearrange("p k a -> p (k a)")
                    s = mod[:, 3 * n, 2 * b:2 * b + 2, :].rearrange("p k a -> p (k a)")
                    dve.wait_ge(xn_turned, 8 * n + b + 1)
                    step(tt(out, heads(ps[:, b, :]), per_head(a), MUL))
                    tt(out, out, per_head(s), ADD).then_inc(hT_even, 1)

            modulate(0)

            al = ba[:, :, 16:32]
            sp_ = sc[:, 1, 0:32].rearrange("p (a n) -> p a n", a=NP)
            sg_ = sc[:, 0, 0:32].rearrange("p (a n) -> p a n", a=NP)

            def bag_inputs():
                dve.wait_ge(ba_done, 1)
                dve.tensor_copy(ba[:, :, :], ps[:, 4, 0:64].rearrange("p (a n) -> p a n", a=NP)).then_inc(ba_saved, 1)
                dve.wait_ge(ba_saved, 1)
                dve.wait_ge(small_in, 16 * 10)
                step(tt(al, al, over_heads(dtb[:, :], NP), ADD))
                step(tt(lamv[:, 0, :], lamv[:, 0, :], lamv[:, 1, :], MUL))
                step(tt(lamv[:, 2, :], lamv[:, 2, :], lamv[:, 3, :], MUL))
                step(red(lam_t[:, 0:1], lamv[:, 0, :], AX, ADD))
                step(red(lam_t[:, 1:2], lamv[:, 2, :], AX, ADD))
                step(ts(subln[:, :], subln[:, :], 1.0 - LAM_INIT, None, MUL))
                stt(sp_, al, -1.0, al, MUL, MAX).then_inc(bag_dve, 1)

            def conv(n, b):
                dve.wait_ge(conv_mid, 4 * n + b + 1)
                for m in (2 * b, 2 * b + 1):
                    conv_taps(n, m)

            def conv_taps(n, m):
                src = ps[:, 4 * (n % 2) + m // 2, 256 * (m % 2):256 * (m % 2) + 256].rearrange("p (a t) -> p a t", a=NP)
                dst = convT[:, 8 * n + m, :].rearrange("p (a t) -> p a t", a=NP)
                step(stt(dst[:, :, 1:P], src[:, :, 0:P - 1], cw[:, 0, 8 * n + m:8 * n + m + 1], dst[:, :, 1:P], MUL, ADD))
                last = stt(dst[:, :, 0:P - 1], src[:, :, 1:P], cw[:, 2, 8 * n + m:8 * n + m + 1], dst[:, :, 0:P - 1], MUL, ADD)
                if m == 7:
                    last.then_inc(in_saved, 1)

            def bag():
                dve.wait_ge(bag_exp, 1)
                step(ts(sc[:, :, 0:32], sc[:, :, 0:32], 1.0, None, ADD))
                step(tt(lam_t[:, 2:3], lam_t[:, 0:1], lam_t[:, 1:2], SUB))
                step(ts(lam_t[:, 2:3], lam_t[:, 2:3], LAM_INIT, None, ADD))
                dve.reciprocal(beta[:, :, :], sg_).then_inc(bag_dve, 1)
                dve.wait_ge(bag_exp, 2)
                step(stt(al, al, 0.0, sp_, MAX, ADD))
                step(stt(g[:, :, :], al, -1.0, over_heads(alog[:, :], NP), MUL, MUL))
                dve.tensor_copy(sc[:, 0, 32:33], g[:, 0, 0:1]).then_inc(bag_ready, 1)

            for n in range(7):
                for k in range(KT):
                    j, kk = k // 2, k % 2
                    if n == 0 and kk == 0:
                        dve.wait_ge(hi_x, j + 1)
                        tt(hT_lo[:, k:k + 2, :], hT[:, k:k + 2, :], hT_hi[:, k:k + 2, :].bitcast(F32), SUB).then_inc(lo_x, 1)
                    dve.wait_ge(hi_w, KT * n + k + 1)
                    tt(w_lo[:, kk, :], ring[:, j, kk * 1024:(kk + 1) * 1024], w_hi[:, kk, :].bitcast(F32),
                       SUB).then_inc(lo_w, 1)
                    if 1 <= n <= 3 and k % 4 == 3:
                        conv(n - 1, k // 4)
                    if n == 0 and k == 3:
                        bag_inputs()
                if n == 4:
                    bag()

            for p in range(NP):
                nk = 1 + p
                dve.wait_ge(in_saved, 7)
                if p == 1:
                    dve.wait_ge(at_pT, 1)
                    for s in range(2):
                        if s:
                            dve.wait_ge(rope_done, 1)
                        x = qkvb[:, s, 1, :]
                        x64 = x.rearrange("p (m d) -> p m d", d=64)
                        cos = over_heads(cst[:, C_COS:C_COS + 64], 16)
                        step(tt(rope_a.rearrange("p (m d) -> p m d", d=64), x64, cos, MUL))
                        x4 = x.rearrange("p (m f x n) -> p m f x n", m=16, f=2, x=2)
                        b4 = rope_b.rearrange("p (m f x n) -> p m f x n", m=16, f=2, x=2)
                        sn = cst[:, C_SIN:C_SIN + 64].rearrange("p (f x n) -> p f x n", f=2, x=2)
                        for h in range(2):
                            sin = sn[:, :, h, :].unsqueeze(1).to_broadcast([P, 16, 2, 16])
                            step(tt(b4[:, :, :, h, :], x4[:, :, :, 1 - h, :], sin, MUL))
                        tt(x, rope_a, rope_b, ADD).then_inc(rope_done, 1)
                K = nk * P
                hn = H // nk
                c5 = cent[:, 0:16 * K].rearrange("p (m h n) -> p m h n", m=2, h=H)
                mx3 = mx[:, 0:2 * hn].rearrange("p (m h) -> p m h", m=2)
                c4 = cent[:, 0:16 * K].rearrange("p (m n) -> p m n", m=16)
                for r in range(nk):
                    dve.wait_ge(at_scores, p + r + 1)
                    if r:
                        dve.wait_ge(at_cent, 2)
                    scores = banks(0, 4).rearrange("p (m h n) -> p m h n", m=2, n=K)
                    step(red(mx3, scores, AX, MAX))
                    tt(c5[:, :, hn * r:hn * (r + 1), :], scores, mx3.unsqueeze(3).to_broadcast([P, 2, hn, K]),
                       SUB).then_inc(at_cent, 1)
                dve.wait_ge(at_exp, p + 1)
                step(red(den[:, :], c4, AX, ADD))
                step(dve.reciprocal(den[:, :], den[:, :]))
                step(ts(den[:, 8:16], den[:, 8:16], lam_t[:, 2:3], None, MUL))
                step(tt(c4, c4, per_head(den[:, :], K), MUL))
                tt(c4[:, 0:8, :], c4[:, 0:8, :], c4[:, 8:16, :], SUB).then_inc(at_prob, 1)
                dve.wait_ge(at_o_saved, p + 1)
                step(tt(o_sq, o_b, o_b, MUL))
                step(red(mx[:, 0:8], heads(o_sq), AX, ADD))
                rsqrt_mean(mx[:, 0:8], den[:, 0:8], P)
                step(tt(heads(o_b), heads(o_b), per_head(den[:, 0:8]), MUL))
                tt(heads(o_b), heads(o_b), over_heads(subln[:, :]), MUL).then_inc(at_on, 1)

            dve.wait_ge(conv_done, 6)
            dve.wait_ge(at_scores, 3)
            dve.wait_ge(kv_out, 32)
            dve.wait_ge(at_oT, 2)
            qk = convT[:, 0:16, :].rearrange("p m t -> p (m t)")
            tt(l2_buf[:, 2048:4096], qk[:, 2048:4096], qk[:, 2048:4096], MUL).then_inc(l2_sq, 1)
            dve.wait_ge(gc_done, 1)
            step(dve.tensor_copy(gc[:, :], ps[:, 3, 0:48]))
            tt(gc[:, 32:48], gc[:, 32:48], gc[:, 0:16], SUB).then_inc(gc_saved, 1)
            dve.wait_ge(l2_root, 1)
            step(dve.reciprocal(sc[:, 1, 0:32], sc[:, 0, 0:32]))
            step(ts(sc[:, 1, 0:16], sc[:, 1, 0:16], float(P) ** -0.5, None, MUL))

            def diagonals(q):
                tt(heads(l2_buf[:, 1024 * q:1024 * (q + 1)]), over_heads(ident), per_head(sc[:, 1, 8 * q:8 * q + 8]),
                   MUL).then_inc(l2_diag, 1)

            diagonals(0)
            for q in range(4):
                if q < 3:
                    diagonals(q + 1)
                dve.wait_ge(l2_rep, q + 1)
                part = qk[:, 1024 * q:1024 * (q + 1)]
                tt(part, part, banks(2 * (q % 2), 2), MUL).then_inc(l2_done, 1)
            dve.wait_ge(gc_saved, 1)
            dve.wait_ge(gc_exp, 1)
            dve.wait_ge(lv_in, 16)
            for p in range(NP):
                for d in range(2):
                    n = 2 * p + d
                    hd = slice(8 * d, 8 * d + 8)
                    if n:
                        dve.wait_ge(dl_O, n)
                    if n in (1, 2):
                        dve.wait_ge(dl_S, n)
                    elif n == 0:
                        dve.wait_ge(l2_done, 4)
                    step(tt(At[:, :, :], over_heads(U[d]), per_head(g[:, p, hd]), MUL))
                    tt(Aqk[:, :, :], over_heads(ident), per_head(beta[:, p, hd]), MUL).then_inc(dl_rhs, 1)
                    dve.wait_ge(dl_gcb, n + 1)
                    gcp = gc[:, 16 * p + 8 * d:16 * p + 8 * d + 8]
                    step(tt(E_, heads(banks(0, 2)), per_head(gcp), SUB))
                    ts(E_, E_, 0.0, None, ALU.min).then_inc(dl_diff, 1)
                    dve.wait_ge(dl_dec, n + 1)
                    step(tt(E_, E_, over_heads(U[d]), MUL))
                    dve.wait_ge(dl_gram, 2 * n + 1)
                    step(tt(At, heads(banks(0, 2)), E_, MUL))
                    tt(At, At, heads(banks(2, 2)), MUL).then_inc(dl_A, 1)
                    dve.wait_ge(dl_gram, 2 * n + 2)
                    tt(Aqk, heads(banks(0, 2)), E_, MUL).then_inc(dl_A, 1)
                    dve.wait_ge(dl_A, 2 * n + 2)
                    if p == 0:
                        dve.wait_ge(tok_saved, 1)
                        tt(E_, V_, per_head(beta[:, p, hd]), MUL).then_inc(dl_R, 1)
                    else:
                        egcp = per_head(egc[:, 16 + 8 * d:24 + 8 * d])
                        dve.wait_ge(tok_saved, 2)
                        dve.wait_ge(dl_S0, 2 * d + 1)
                        tt(E_, heads(banks(2, 2)), egcp, MUL).then_inc(dl_S0r, 1)
                        dve.wait_ge(dl_S0r, 2 * d + 1)
                        step(tt(E_, V_, E_, SUB))
                        tt(E_, E_, per_head(beta[:, p, hd]), MUL).then_inc(dl_R, 1)
                        dve.wait_ge(dl_S0, 2 * d + 2)
                        if d == 0:
                            tt(O_, heads(banks(0, 2)), egcp, MUL).then_inc(dl_S0r, 1)
                        else:
                            step(tt(M_, heads(banks(0, 2)), egcp, MUL))
                            tt(O_, O_, M_, ADD).then_inc(dl_S0r, 1)
                        dve.wait_ge(dl_S0r, 2 * d + 2)
                    if n in (1, 2):
                        dve.wait_ge(st_out, 16 * n)
                    def block_mask(lv):
                        tt(M_, At, over_heads(lvl[:, lv, d, :]), MUL).then_inc(dl_M, 1)

                    block_mask(0)
                    for lv in range(LEVELS):
                        dve.wait_ge(dl_X, LEVELS * n + lv + 1)
                        if lv == 0:
                            tt(T_, over_heads(ident), heads(banks(0, 2)), SUB).then_inc(dl_T, 1)
                            dve.wait_ge(dl_M, LEVELS * n + 1)
                            tt(Tt, over_heads(ident), M_, SUB).then_inc(dl_Tt, 1)
                            dve.wait_ge(dl_Tt, LEVELS * n + 1)
                            block_mask(1)
                            continue
                        if lv < LEVELS - 1:
                            block_mask(lv + 1)
                            dve.wait_ge(dl_Y, (LEVELS - 2) * n + lv)
                            dve.wait_ge(dl_T, (LEVELS - 1) * n + lv)
                            tt(T_, T_, heads(banks(0, 2)), SUB).then_inc(dl_T, 1)
                        dve.wait_ge(dl_Yt, (LEVELS - 1) * n + lv)
                        dve.wait_ge(dl_Tt, LEVELS * n + lv)
                        tt(Tt, Tt, heads(banks(2, 2)), SUB).then_inc(dl_Tt, 1)
                    if p == 0:
                        dve.wait_ge(dl_Vs, n + 1)
                        tt(X_, M_, per_head(egl[:, hd]), MUL).then_inc(dl_Vd, 1)
                    dve.wait_ge(dl_O, n + 1)
                    if n == 0:
                        step(dve.tensor_copy(O_, heads(banks(0, 2))))
                    else:
                        step(tt(O_, O_, heads(banks(0, 2)), ADD))
                sq = E_
                step(tt(sq, O_, O_, MUL))
                step(red(mx[:, 0:8], sq, AX, ADD))
                rsqrt_mean(mx[:, 0:8], den[:, 0:8], P)
                step(tt(O_, O_, per_head(den[:, 0:8]), MUL))
                step(tt(O_, O_, over_heads(onorm[:, :]), MUL))
                tt(O_, O_, heads(gateS[:, p, :]), MUL).then_inc(dl_on, 1)
                if p == 0:
                    dve.wait_ge(dl_oT, 1)

            def add_gate(dst, p, first, bank):
                dve.wait_ge(gt_done, first + p + 1)
                dve.wait_ge(gt_in, 16 * (first + 2))
                tt(dst[:, p, :], dst[:, p, :], banks(bank, 4), ADD).then_inc(gt_saved, 1)

            for p in range(NP):
                add_gate(gt_b, p, 0, 0)
            dve.wait_ge(bg_kept, 2)
            for s in (3, 4):
                step(tt(mod[:, s, :, :], mod[:, s, :, :],
                        vecT[:, 16 * s:16 * s + 16].unsqueeze(2).to_broadcast([P, KT, NP]), ADD))
            scaled_gain(1)
            def low_part(lo, x, hi):
                return tt(lo, x, hi.bitcast(F32), SUB)

            def merge(r, p):
                br, c = r // 2, r % 2
                dve.wait_ge(round_done, R_UPA + r + 1)
                dve.wait_ge(gm_ready, 4 * br + 2 * c + 2)
                up = banks(4 * c + 2 * p, 2).rearrange("p (s n) -> p s n", s=2)
                mix = mixed[:, p, c * HW:(c + 1) * HW].rearrange("p (s n) -> p s n", s=2)
                gates = gm[:, 4 * br + 2 * c:4 * br + 2 * c + 2, p, :]
                if br == 0:
                    tt(mix, up, gates, MUL).then_inc(up_saved, 1)
                else:
                    t = gm_tmp[:, 0:HW].rearrange("p (s n) -> p s n", s=2)
                    dve.wait_ge(up_saved, 4 + 2 * c + p)
                    step(tt(t, up, gates, MUL))
                    tt(mix, mix, t, ADD).then_inc(up_saved, 1)

            def residual(c, p):
                dve.wait_ge(gt_saved, 2)
                dve.wait_ge(x_in, 32)
                dve.wait_ge(round_done, R_O + 2 * c + 2)
                cols = slice(c * HW, (c + 1) * HW)
                step(tt(gt_b[:, p, cols], banks(4 * c + 2 * p, 2), gt_b[:, p, cols], MUL))
                tt(xres[:, p, cols], xres[:, p, cols], gt_b[:, p, cols], ADD).then_inc(x_saved, 1)

            dve.wait_ge(src_hi, 1)
            low_part(oa_lo[:, :, :], oaT, oa_hi[:, :, :]).then_inc(src_lo, 1)
            for i in range(64):
                slot, _, at = split_piece(i)
                dve.wait_ge(hi_w, at)
                low_part(wo_lo[:, i % 2, :], ring[:, slot, 0:HW], wo_hi[:, i % 2, :]).then_inc(lo_w, 1)
                if i == 8:
                    dve.wait_ge(src_hi, 2)
                    low_part(ob_lo[:, :, :], obT, ob_hi[:, :, :]).then_inc(src_lo, 1)
                if i in (10, 12, 18, 20, 26, 28):
                    merge(i // 8 - 1, (i % 8 - 2) // 2)
                if i == 33:
                    merge(3, 0)
                    merge(3, 1)
                    for b in range(8):
                        dve.wait_ge(mixed_hi, b + 1)
                        low_part(mix_lo[:, 2 * b:2 * b + 2, :].rearrange("p k t -> p (k t)"), ps[:, b, :],
                                 mix_hi[:, 2 * b:2 * b + 2, :].rearrange("p k t -> p (k t)")).then_inc(mixed_lo, 1)
                if i in (50, 53):
                    residual(0, (i - 50) // 3)
            for p in range(NP):
                residual(1, p)
            add_gate(gt2_b, 0, 2, 0)
            dve.wait_ge(ssq_ready, 4)
            rsqrt_mean(mx[:, 0:2], den[:, 0:2], D)
            for p in range(NP):
                last = ts(xn2[:, p, :], xres[:, p, :], den[:, p:p + 1], None, MUL)
            last.then_inc(xn_ready, 1)
            add_gate(gt2_b, 1, 2, 4)
            modulate(1)
            for b in range(8):
                dve.memset(yacc_b[:, b, :], 0.0).then_inc(mo_ys, 1)
            dve.memset(ohT, 0.0).then_inc(mo_PTs, 1)
            dve.memset(oe, 0.0).then_inc(mo_dns, 1)

            dve.wait_ge(rt_done, 1)
            tt(r_log, ps[:, 0, 0:72].rearrange("p (a n) -> p a n", a=NP), over_heads(b_rt[:, :], NP),
               ADD).then_inc(rt_log, 1)
            dve.wait_ge(rt_log, 1)
            le = r_log[:, :, NG:].rearrange("p a (g e) -> p a g e", g=NG)
            gl = r_log[:, :, 0:NG]

            def first_max(out, vals, top, t, n):
                step(red(top, vals, AX, MAX))
                step(tt(t, vals, per_head(top, n), EQ))
                step(tt(t, t, over_heads(cst[:, C_TIE:C_TIE + n], NP), MUL))
                step(red(r_tm, t, AX, MAX))
                step(tt(out, t, per_head(r_tm, n), EQ))

            first_max(r_goh, gl, r_gmax, r_t4, NG)
            step(tt(r_ge, gl, per_head(r_gmax, NG), SUB))
            big4 = r_big.rearrange("p a (g e) -> p a g e", g=NG)
            step(tt(big4, le, r_goh.unsqueeze(3).to_broadcast([P, NP, NG, EG]), MUL))
            step(red(r_les, r_big.rearrange("p a (g e) -> p a e g", g=NG), AX, ADD))
            first_max(r_oh1, r_les, r_m1, r_t8, EG)
            step(stt(r_les2, r_oh1, -1e30, r_les, MUL, ADD))
            first_max(r_oh2, r_les2, r_m2, r_t8, EG)
            step(tt(r_s8, r_oh1, r_oh2, ADD))
            mask4 = r_mask.rearrange("p a (g e) -> p a g e", g=NG)
            goh4 = r_goh.unsqueeze(3).to_broadcast([P, NP, NG, EG])
            tt(mask4, goh4, r_s8.unsqueeze(2).to_broadcast([P, NP, NG, EG]), MUL).then_inc(rt_mask, 1)
            tt(r_e2, r_m2, r_m1, SUB).then_inc(rt_dve, 1)
            dve.wait_ge(rt_exp, 1)
            step(red(r_pg, r_ge, AX, ADD))
            step(ts(r_w1, r_e2, 1.0, None, ADD))
            step(tt(r_w1, r_w1, r_pg, MUL))
            step(dve.reciprocal(r_w1, r_w1))
            step(tt(r_w2, r_w1, r_e2, MUL))
            step(tt(r_c8, r_oh1, per_head(r_w1, EG), MUL))
            step(tt(r_t8, r_oh2, per_head(r_w2, EG), MUL))
            step(tt(r_c8, r_c8, r_t8, ADD))
            step(dve.memset(r_comb, 0.0))
            step(dve.memset(r_pos, 1024.0))
            step(tt(r_comb[:, :, 0:NE].rearrange("p a (g e) -> p a g e", g=NG), goh4,
                    r_c8.unsqueeze(2).to_broadcast([P, NP, NG, EG]), MUL))
            step(ts(r_big, r_mask, -1024.0, 1024.0, MUL, ADD))
            dve.wait_ge(rt_pos, 1)
            tt(r_pos[:, :, 0:NE], r_big, ps[:, 4, 0:64].rearrange("p (a n) -> p a n", a=NP), ADD).then_inc(places, 1)
            step(red(r_cnt, ps[:, 4, 64:96], AX, MAX))
            step(tt(r_gt, r_cnt.to_broadcast([P, 3]), cst[:, C_THR:C_THR + 3], ALU.is_gt))
            step(red(r_cnt, r_gt, AX, ADD))
            step(ts(n_slab[:, 0:1], r_cnt, 1.0, None, ADD))
            ts(n_slab[:, 1:2], r_cnt, float(PAIRS), float(PAIRS - 1), MUL, ADD).then_inc(rt_ready, 1)
            dve.wait_ge(rt_ready, 1)
            n_slabs = dve.value_load(n_slab[0:1, 0:1], min_val=1, max_val=MAX_SLABS)
            seen = dve.alloc_register("dve_seen")
            turn = dve.alloc_register("dve_turn")
            dve.reg_mov(seen, 1)
            dve.reg_mov(turn, 1)
            oh4 = onehot.rearrange("p a (e s) -> p a e s", e=2)
            ohc4 = onehot_c.rearrange("p a (e s) -> p a e s", e=2)
            iota4 = cst[:, C_IOTA:C_IOTA + CAP].unsqueeze(1).unsqueeze(1).to_broadcast([P, NP, 2, CAP])

            def one_hots(at, t):
                pos4 = r_pos[:, :, bass.ds(at, 2)].unsqueeze(3).to_broadcast([P, NP, 2, CAP])
                comb4 = r_comb[:, :, bass.ds(at, 2)].unsqueeze(3).to_broadcast([P, NP, 2, CAP])
                tt(oh4, iota4, pos4, EQ).then_inc(mo_oh, 1)
                dve.wait_ge(mo_oh, t)
                tt(ohc4, oh4, comb4, MUL).then_inc(mo_P, 1)

            def gathered_back(v):
                dve.wait_ge(mo_ys, v * 8)
                for j in range(8):
                    dve.wait_ge(mo_y, v * 8 + (j - 7))
                    tt(yacc_b[:, j, :], yacc_b[:, j, :], ps[:, 3 + j % 4, :], ADD).then_inc(mo_ys, 1)

            with dve.Fori(0, n_slabs) as slab:
                t = dve.snap(turn)
                dve.wait_ge(places, slab + 1)
                one_hots(0, t)
                dve.reg_add(turn, turn, 1)
                with dve.Fori(0, PAIRS) as i:
                    v, t = dve.snap(seen), dve.snap(turn)
                    gathered_back(v)
                    dve.wait_ge(mo_PT, v)
                    one_hots(i * 2 + 2, t)
                    dve.wait_ge(mo_silu, v)
                    dve.wait_ge(round_done, v * 3 + (R_MOE - 1))
                    tt(a_act, a_silu, ps[:, 1, :], MUL).then_inc(mo_act, 1)
                    dve.reg_add(seen, seen, 1)
                    dve.reg_add(turn, turn, 1)
                t = dve.snap(turn)
                dve.wait_ge(mo_P, t - 1)
                dve.wait_ge(mo_gath, t * 2 - 2)
                ts(r_pos, r_pos, -float(CAP), None, ADD).then_inc(places, 1)
            v = dve.snap(seen)
            dve.wait_ge(mo_ys, v * 8)
            dve.wait_ge(gt_saved, 4)
            for p in range(NP):
                for j in range(4 * p, 4 * p + 4):
                    dve.wait_ge(mo_y, v * 8 + (j - 7))
                    tt(yacc_b[:, j, :], yacc_b[:, j, :], ps[:, 3 + j % 4, :], ADD).then_inc(mo_ys, 1)
                dve.wait_ge(mo_ys, v * 8 + (4 * p + 4))
                step(tt(yacc[:, p, :], yacc[:, p, :], gt2_b[:, p, :], MUL))
                tt(xres[:, p, :], xres[:, p, :], yacc[:, p, :], ADD).then_inc(x_saved, 1)
            dve.wait_ge(nf_in, 16)
            for p in range(NP):
                dve.wait_ge(ssq_ready, 5 + p)
                rsqrt_mean(mx[:, p:p + 1], den[:, p:p + 1], D)
                stt(yacc[:, p, :], xres[:, p, :], den[:, p:p + 1], nf_b, MUL, MUL).then_inc(y_ready, 1)

        @block.scalar
        def _(act):
            A = act.activation
            roots = [0]

            def root(w):
                roots[0] += 1
                act.wait_ge(ms_ready, roots[0])
                A(rs[:, 0:w], ms[:, 0:w], ACT.Sqrt).then_inc(root_ready, 1)

            def bcast(row):
                return row.partition_broadcast(P)

            act.dma_start(cst[:, :], consts).then_inc(boot_in, 16)
            for p, src in enumerate((c_ctx, c[0])):
                act.dma_start(cT[:, p, :], src.rearrange("(p k) -> p k", k=KT)).then_inc(boot_in, 16)
            act.dma_start(vec_rows[0:96, :], b_ada[0].rearrange("(r q) -> r q", q=P)).then_inc(boot_in, 16)
            act.dma_start(vec_rows[96:112, :], norm_mix[0].rearrange("(r q) -> r q", q=P)).then_inc(boot_in, 16)
            act.dma_start(vec_rows[112:128, :], norm_ffn[0].rearrange("(r q) -> r q", q=P)).then_inc(boot_in, 16)
            act.dma_start(conv_rows[0:72, :], conv_a[0].rearrange("i (m q) -> (i m) q", q=P)).then_inc(boot_in, 16)
            for p in range(NP):
                act.dma_start(xin[:, p, :], x_dram[p]).then_inc(boot_in, 16)
            act.dma_start(w_ba[:, :, :], in_dram[:, :, 4096:4128]).then_inc(small_in, 16)
            act.dma_start(w_rt[:, :, 0:NG], w_rg[0].rearrange("(k p) n -> p k n", p=P)).then_inc(small_in, 16)
            act.dma_start(w_rt[:, :, NG:], w_re[0].rearrange("(k p) n -> p k n", p=P)).then_inc(small_in, 16)
            for dst, src in ((alog[:, :], a_log[0].rearrange("a h -> (a h)")), (dtb[:, :], dt_bias[0].rearrange("a h -> (a h)")),
                             (lamv[:, :, :].rearrange("p a b -> p (a b)"), lam[0].rearrange("a h -> (a h)")),
                             (onorm[:, :], onorm_a[0]), (subln[:, :], subln_b[0]),
                             (b_rt[:, 0:NG], b_rg[0]), (b_rt[:, NG:], b_re[0])):
                act.dma_start(dst, bcast(src)).then_inc(small_in, 16)

            act.wait_ge(boot_in, 16 * 9)
            act.wait_ge(vec_saved, 1)
            for p in range(NP):
                A(silu_cT[:, :, p], cT[:, p, :], ACT.Silu).then_inc(silu_ready, 1)
            for p in range(NP):
                A(ar(8192 + 2048 * p, 2048), xin[:, p, :], ACT.Square, accum_out=mx[:, p:p + 1]).then_inc(ssq_ready, 1)
            root(2)
            for s in range(2):
                act.wait_ge(round_done, 2 * s + 2)
                A(ada_rows[:, s, :], banks(4 * s, 4), ACT.Copy).then_inc(ada_saved, 1)

            def modulate(n):
                act.wait_ge(gain_ready, n + 1)
                for b in range(1, 8, 2):
                    act.wait_ge(xn_turned, 8 * n + b + 1)
                    for i in range(4):
                        k, p = 2 * b + i // 2, i % 2
                        last = A(hT[:, k, p * P:(p + 1) * P], ps[:, b, i * P:(i + 1) * P], ACT.Identity,
                                 scale=modA[:, n, k, p:p + 1], bias=mod[:, 3 * n, k, p:p + 1])
                    last.then_inc(hT_odd, 1)

            modulate(0)
            act.wait_ge(hT_even, 4)
            act.dma_start(heads(cv), cache_v[0, 0].rearrange("h t d -> t h d")).then_inc(at_in, 16)
            act.wait_ge(vec_saved, 3)

            def tail(g, b):
                if b == 0:
                    act.wait_ge(round_done, R_IN + g + 1)
                if g < 3:
                    for m in (2 * b, 2 * b + 1):
                        last = A(convT[:, 8 * g + m, :], ps[:, 4 * (g % 2) + b, 256 * (m % 2):256 * (m % 2) + 256],
                                 ACT.Identity, scale=cw[:, 1, 8 * g + m:8 * g + m + 1])
                    last.then_inc(conv_mid, 1)
                else:
                    cols = slice(512 * (b % 2), 512 * (b % 2) + 512)
                    dst = gateS[:, b // 2, cols] if g == 3 else qkvb[:, g - 4, b // 2, cols]
                    ins = A(dst, ps[:, 4 * (g % 2) + b, :], ACT.Silu if g == 3 else ACT.Copy)
                    if b == 3:
                        ins.then_inc(in_saved, 1)

            def conv_silu(g, half):
                act.wait_ge(in_saved, g + 1)
                y = convT[:, 8 * g + 4 * half:8 * g + 4 * half + 4, :].rearrange("p m t -> p (m t)")
                A(y, y, ACT.Silu).then_inc(conv_done, 1)

            for n in range(7):
                for k in range(KT):
                    j, kk = k // 2, k % 2
                    if n == 0 and kk == 0:
                        act.wait_ge(*modulated(0, j))
                        A(hT_hi[:, k:k + 2, :], hT[:, k:k + 2, :], ACT.Copy).then_inc(hi_x, 1)
                    act.wait_ge(slot_full[j], 16 * (R_IN + n + 1))
                    if kk == 0 and n + k > 0:
                        act.wait_ge(even_used, 8 * n + j)
                    elif kk == 1 and n + j > 0:
                        act.wait_ge(slot_used[(j - 1) % SLOTS], R_IN + n + (1 if j else 0))
                    A(w_hi[:, kk, :], ring[:, j, kk * 1024:(kk + 1) * 1024], ACT.Copy).then_inc(hi_w, 1)
                    if n >= 1 and k % 4 == 1:
                        tail(n - 1, k // 4)
                    if 2 <= n <= 4 and k in (2, 4):
                        conv_silu(n - 2, k // 2 - 1)
                if n == 4:
                    act.wait_ge(bag_dve, 1)
                    A(sc[:, 0, 0:32].rearrange("p (a n) -> p a n", a=NP), ba[:, :, 0:16], ACT.Exp, scale=-1.0)
                    A(sc[:, 1, 0:32], sc[:, 1, 0:32], ACT.Exp, scale=-1.0)
                    A(alog[:, :], alog[:, :], ACT.Exp)
                    A(lam_t[:, 0:2], lam_t[:, 0:2], ACT.Exp).then_inc(bag_exp, 1)
                    act.wait_ge(bag_dve, 2)
                    A(sc[:, 1, 0:32], sc[:, 1, 0:32], ACT.Ln).then_inc(bag_exp, 1)
            for b in range(4):
                tail(6, b)
            act.wait_ge(in_saved, 7)
            act.dma_start(new_k[0, 0].rearrange("h t d -> t h d"), heads(qkvb[:, 1, 0, :])).then_inc(kv_out, 16)
            act.dma_start(new_v[0, 0].rearrange("h t d -> t h d"), heads(qkvb[:, 2, 0, :])).then_inc(kv_out, 16)

            unit = [0]

            def keep(n):
                for item, part in UNIT_LIST[unit[0]:unit[0] + n]:
                    is_ada, i, r = STREAM[item]
                    out = banks(4 + 2 * (item % 2), 2)
                    if is_ada and part == 3:
                        act.wait_ge(round_done, r + 2)
                        A(row_q[:, i % 4, :], out, ACT.Copy).then_inc(bg_saved, 1)
                    elif part == 4 and item in TURN_ITEMS:
                        n_turn = TURN_ITEMS.index(item)
                        act.wait_ge(bg_turned, n_turn + 1)
                        A(mod[:, 3 + n_turn, :, :].rearrange("p k a -> p (k a)"),
                          ps[:, 4 + 2 * ((item - 1) % 2), 0:32], ACT.Copy).then_inc(bg_kept, 1)
                    elif not is_ada and part == 7:
                        act.wait_ge(round_done, r + 1)
                        A(ring[:, i, HW:SW], out, ACT.Copy).then_inc(bg_saved, 1)
                unit[0] += n

            keep(1)
            for p in range(NP):
                nk = 1 + p
                if p == 1:
                    act.wait_ge(at_on, 1)
                    act.dma_start(heads(ck), cache_k[0, 0].rearrange("h t d -> t h d")).then_inc(at_in, 16)
                t0 = 2 * p
                act.wait_ge(at_turned, t0 + 1)
                A(qT.rearrange("p h t -> p (h t)"), banks(0, 2), ACT.Copy).then_inc(at_saved, 1)
                act.wait_ge(at_turned, t0 + 2)
                A(kT.rearrange("p h t -> p (h t)"), banks(2, 2), ACT.Copy).then_inc(at_saved, 1)
                if p == 1:
                    act.wait_ge(at_turned, 5)
                    A(kcT.rearrange("p h t -> p (h t)"), banks(0, 2), ACT.Copy).then_inc(at_saved, 1)
                    keep(1)
                keep(1)
                act.wait_ge(at_cent, 1 + 2 * p)
                n = 16 * nk * P
                A(cent[:, 0:n], cent[:, 0:n], ACT.Exp, scale=64.0 ** -0.5).then_inc(at_exp, 1)
                keep(2 * nk + 1 + 3 * p)
                act.wait_ge(at_pT, p + 1)
                A(pT.rearrange("p k h q -> p (k h q)")[:, 0:1024 * nk], banks(0, 2 * nk), ACT.Copy).then_inc(at_pT_saved, 1)
                keep(1)
                act.wait_ge(at_o, p + 1)
                A(o_b, banks(0, 2), ACT.Copy).then_inc(at_o_saved, 1)
                root(8)
                keep(3)
                act.wait_ge(at_oT, p + 1)
                A(obT[:, :, p * P:(p + 1) * P], heads(banks(2, 2)), ACT.Copy).then_inc(at_oT_saved, 1)
                keep(1)

            act.dma_start(lvl.rearrange("p n d i -> p (n d i)"), level_masks).then_inc(lv_in, 16)
            act.wait_ge(at_o, 2)
            act.wait_ge(kv_out, 32)
            act.wait_ge(conv_done, 6)
            A(l2_buf[:, 0:2048], convT[:, 0:8, :].rearrange("p m t -> p (m t)"), ACT.Square).then_inc(l2_sq, 1)
            act.wait_ge(l2_sum, 1)
            A(sc[:, 0, 0:32], ps[:, 2, 0:32], ACT.Sqrt, bias=eps[:, :]).then_inc(l2_root, 1)
            keep(2)
            act.wait_ge(gc_saved, 1)
            A(egc[:, :], gc[:, 0:32], ACT.Exp)
            A(egl[:, :], gc[:, 32:48], ACT.Exp).then_inc(gc_exp, 1)
            keep(2)
            flat = lambda t: t.rearrange("p h t -> p (h t)")
            for p in range(NP):
                act.wait_ge(tok_turned, p + 1)
                if p == 0:
                    A(flat(K_), banks(2, 2), ACT.Copy)
                A(flat(V_), banks(0, 2), ACT.Copy).then_inc(tok_saved, 1)
                for d in range(2):
                    n = 2 * p + d
                    if p == 1:
                        act.wait_ge(*((dl_S, 2) if d == 0 else (dl_S0, 2)))
                        act.dma_start(K_, state_delta[0, 0, d].rearrange("h k v -> k h v")).then_inc(s0_in, 16)
                    if n:
                        keep(1)
                    act.wait_ge(dl_diff, n + 1)
                    A(flat(E_), flat(E_), ACT.Exp).then_inc(dl_dec, 1)
                    keep(2 + p)
                    for lv in range(LEVELS):
                        if lv:
                            act.wait_ge(dl_X, LEVELS * n + lv + 1)
                            A(flat(X_), banks(0, 2), ACT.Copy).then_inc(dl_Xs, 1)
                        keep(1)
                    act.wait_ge(dl_V, n + 1)
                    A(flat(M_), banks(2, 2), ACT.Copy).then_inc(dl_Vs, 1)
                    keep(1)
                    if p == 0:
                        keep(1)
                        act.wait_ge(dl_S, n + 1)
                        A(flat(T_), banks(2, 2), ACT.Copy).then_inc(dl_Ss, 1)
                        act.wait_ge(dl_Ss, n + 1)
                        act.dma_start(new_state[0, 0, d].rearrange("h k v -> k h v"), T_).then_inc(st_out, 16)
                root(8)
                keep(2)
                act.wait_ge(dl_oT, p + 1)
                A(oaT[:, :, p * P:(p + 1) * P], heads(banks(2, 2)), ACT.Copy).then_inc(dl_oTs, 1)

            def load_gate_bias(section, dst):
                for p in range(NP):
                    act.dma_start(dst[:, p, :], bcast(b_ada[0, section * D:(section + 1) * D])).then_inc(gt_in, 16)

            act.wait_ge(dl_on, 2)
            load_gate_bias(2, gt_b)
            act.wait_ge(dl_oTs, 2)
            A(oa_hi[:, :, :], oaT, ACT.Copy).then_inc(src_hi, 1)
            keep(max(0, UNITS - unit[0]))
            for i in range(64):
                slot, r, _ = split_piece(i)
                act.wait_ge(slot_full[slot], 16 * (r + 1))
                if i >= 2:
                    before, r_before, _ = split_piece(i - 2)
                    act.wait_ge(slot_used[before], r_before + 1)
                A(wo_hi[:, i % 2, :], ring[:, slot, 0:HW], ACT.Copy).then_inc(hi_w, 1)
                if i < 8:
                    act.wait_ge(bg_saved, saved_count(False, i))
                    A(ring[:, i, HW:SW], ring[:, i, HW:SW], ACT.Sigmoid).then_inc(gm_ready, 1)
                if i == 4:
                    act.wait_ge(bg_saved, len(STREAM))
                    A(ob_hi[:, :, :], obT, ACT.Copy).then_inc(src_hi, 1)
                if i == 18:
                    act.wait_ge(round_done, R_UPA + 2)
                    for p in range(NP):
                        act.dma_start(xres[:, p, :], x_dram[p]).then_inc(x_in, 16)
                if i == 33:
                    for b in range(8):
                        act.wait_ge(mix_T, b + 1)
                        A(mix_hi[:, 2 * b:2 * b + 2, :].rearrange("p k t -> p (k t)"), ps[:, b, :],
                          ACT.Copy).then_inc(mixed_hi, 1)
                    load_gate_bias(5, gt2_b)
            for p in range(NP):
                act.wait_ge(x_saved, p + 3)
                A(junk[:, p, :], xres[:, p, :], ACT.Square, accum_out=mx[:, p:p + 1]).then_inc(ssq_ready, 1)
            root(2)
            modulate(1)
            for p in (1, 0):
                act.wait_ge(h2_T, 2 - p)
                A(h2[:, p, :], banks(4 * p, 4), ACT.Copy).then_inc(h2_saved, 1)
                if p == 1:
                    act.wait_ge(rt_dve, 1)
                    A(r_ge, r_ge, ACT.Exp)
                    A(r_e2, r_e2, ACT.Exp).then_inc(rt_exp, 1)
            act.wait_ge(rt_ready, 1)
            n_slabs = act.value_load(n_slab[0:1, 0:1], min_val=1, max_val=MAX_SLABS)
            seen = act.alloc_register("act_seen")
            turn = act.alloc_register("act_turn")
            act.reg_mov(seen, 1)
            act.reg_mov(turn, 1)

            def save_gathered(half, t):
                act.wait_ge(mo_gath, t * 2 + (half - 1))
                A(hg[:, 8 * half:8 * half + 8, :].rearrange("p k s -> p (k s)"), banks(3 + 2 * half, 2),
                  ACT.Copy).then_inc(mo_gaths, 1)

            with act.Fori(0, n_slabs):
                t = act.snap(turn)
                save_gathered(0, t)
                save_gathered(1, t)
                act.reg_add(turn, turn, 1)
                with act.Fori(0, PAIRS):
                    v, t = act.snap(seen), act.snap(turn)
                    act.wait_ge(round_done, v * 3 + (R_MOE - 2))
                    A(a_silu, ps[:, 0, :], ACT.Silu).then_inc(mo_silu, 1)
                    act.wait_ge(mo_PT, v)
                    A(ohT.rearrange("p a t -> p (a t)"), ps[:, 7, 0:256], ACT.Copy).then_inc(mo_PTs, 1)
                    save_gathered(0, t)
                    act.wait_ge(mo_aT, v)
                    A(aT.rearrange("p k s -> p (k s)"), ps[:, 2, :], ACT.Copy).then_inc(mo_aTs, 1)
                    save_gathered(1, t)
                    act.wait_ge(round_done, v * 3 + R_MOE)
                    A(oe, banks(3, 4), ACT.Copy).then_inc(mo_dns, 1)
                    act.reg_add(seen, seen, 1)
                    act.reg_add(turn, turn, 1)
            act.dma_start(nf_b, bcast(norm_final)).then_inc(nf_in, 16)
            for p in range(NP):
                act.wait_ge(x_saved, p + 5)
                A(h2[:, p, :], xres[:, p, :], ACT.Square, accum_out=mx[:, p:p + 1]).then_inc(ssq_ready, 1)
                root(1)


_INS = ['x_prompt', 'x_sample', 'c', 'state_delta', 'cache_k', 'cache_v', 'c_ctx', 'w_ada', 'b_ada', 'norm_mix',
        'norm_ffn', 'w_in', 'conv_a', 'a_log', 'dt_bias', 'onorm_a', 'lam', 'subln_b', 'w_up_a', 'w_up_b', 'w_o',
        'w_rg', 'b_rg', 'w_re', 'b_re', 'w_e_gate', 'w_e_up', 'w_e_down', 'norm_final']
_OUTS = [(1, P, D), (1, P, D), (1, 1, 2, H, P, P), (1, 1, H, P, P), (1, 1, H, P, P)]


def kernel(**inputs):
    import concourse.bacc as _bacc
    from concourse.bass_utils import run_bass_kernel_spmd as _run

    nc = _bacc.Bacc("TRN2", target_bir_lowering=False, num_devices=1)
    arrays, args = {}, []
    given = {name: np.ascontiguousarray(inputs[name]) for name in _INS}
    given["constants"], given["level_masks"] = constants()
    for name, a in given.items():
        arrays[f"in_{name}_dram"] = a
        args.append(nc.dram_tensor(f"in_{name}_dram", a.shape, mybir.dt.from_np(a.dtype), kind="ExternalInput").ap())
    for i, shape in enumerate(_OUTS):
        args.append(nc.dram_tensor(f"out_{i}_dram", shape, F32, kind="ExternalOutput").ap())
    program(nc, *args)
    r = _run(nc, [arrays], core_ids=[0])
    return tuple(r.results[0][f"out_{i}_dram"] for i in range(len(_OUTS)))
```
